# Optimizing a Trainium2 kernel written in Bass

```python
import math
import jax
import jax.numpy as jnp
from jax import lax
import numpy as np
import jax, jax.numpy as jnp

D_MODEL = 1024
BATCH = 1
SEQ = 256
DEPTH = 2

N_BRANCHES = 3
NORM_EPS = 1e-6
D_HYENA = 512
HYENA_EMB_DIM = 33
HYENA_FILTER_ORDER = 64
HYENA_FAST_DECAY_PCT = 0.3
HYENA_SLOW_DECAY_PCT = 1.5
HYENA_DECAY_TARGET = 1e-2
GLA_HEADS = 4
GLA_KEY_DIM = 512
GLA_VALUE_DIM = 512
GLA_HEAD_K = GLA_KEY_DIM // GLA_HEADS
GLA_HEAD_V = GLA_VALUE_DIM // GLA_HEADS
GLA_GATE_RANK = 16
GLA_GATE_NORMALIZER = 16.0
GLA_LOG_GATE_MIN = -1.0
GLA_CHUNK = 64
D_POOL = 512
POOL_WINDOWS = (2, 4, 8, 16)
POOL_GROUP = D_POOL // len(POOL_WINDOWS)
D_FF = 2816
IN_SPLITS = (3 * D_HYENA, GLA_KEY_DIM, GLA_KEY_DIM, GLA_VALUE_DIM, GLA_VALUE_DIM,
             2 * GLA_GATE_RANK, D_POOL, N_BRANCHES * D_MODEL)
D_IN = 3 * D_HYENA + 2 * GLA_KEY_DIM + 2 * GLA_VALUE_DIM + 2 * GLA_GATE_RANK + D_POOL + N_BRANCHES * D_MODEL


def _split(t, sizes):
    out, off = [], 0
    for s in sizes:
        out.append(t[..., off:off + s])
        off += s
    return out

def _rms_norm(x, g):
    xf = x.astype(jnp.float32)
    y = xf * lax.rsqrt(jnp.mean(xf * xf, axis=-1, keepdims=True) + NORM_EPS)
    return (y * g.astype(jnp.float32)).astype(x.dtype)

def _dwconv3_centred(x, w, b):
    L = x.shape[1]
    xp = jnp.pad(x, ((0, 0), (1, 1), (0, 0)))
    return xp[:, :L] * w[0] + xp[:, 1:L + 1] * w[1] + xp[:, 2:] * w[2] + b

def _hyena_positional_features(L):
    t = jnp.linspace(0.0, 1.0, L, dtype=jnp.float32)[:, None]
    bands = (HYENA_EMB_DIM - 1) // 2
    w = 2.0 * math.pi * jnp.arange(L, dtype=jnp.float32)[:, None] / L
    f = jnp.linspace(1e-4, bands - 1, bands, dtype=jnp.float32)[None, :]
    ang = f * w
    z = jnp.concatenate([t, jnp.cos(ang), -jnp.sin(ang)], axis=-1)
    return t, z

def _hyena_filter(t, z, w1, b1, fr1, w2, b2, fr2, w3):
    L = t.shape[0]
    h = jnp.sin(fr1 * (z @ w1 + b1))
    h = jnp.sin(fr2 * (h @ w2 + b2))
    h = (h @ w3).astype(jnp.float32)
    max_decay = math.log(HYENA_DECAY_TARGET) / HYENA_FAST_DECAY_PCT
    min_decay = math.log(HYENA_DECAY_TARGET) / HYENA_SLOW_DECAY_PCT
    deltas = jnp.linspace(min_decay, max_decay, D_HYENA, dtype=jnp.float32)
    decay = jnp.exp(-t * jnp.abs(deltas))
    h_fwd = h[:, :D_HYENA] * decay
    h_bwd = h[:, D_HYENA:] * decay
    zero = jnp.zeros((1, D_HYENA), jnp.float32)
    return jnp.concatenate([h_fwd, zero, h_bwd[:0:-1]], axis=0)

def _hyena_mixer(u, conv_w, conv_b, t, z, w1, b1, fr1, w2, b2, fr2, w3, bias):
    B, L, _ = u.shape
    u = _dwconv3_centred(u, conv_w, conv_b)
    x0, x1, v = _split(u, (D_HYENA, D_HYENA, D_HYENA))
    zv = (x1 * v).astype(jnp.float32)
    k = _hyena_filter(t, z, w1, b1, fr1, w2, b2, fr2, w3)
    Zf = jnp.fft.rfft(zv, n=2 * L, axis=1)
    Kf = jnp.fft.rfft(k, n=2 * L, axis=0)
    y = jnp.fft.irfft(Zf * Kf[None], n=2 * L, axis=1)[:, :L]
    y = y + zv * bias.astype(jnp.float32)
    return (x0.astype(jnp.float32) * y).astype(u.dtype)

def _gla_direction(q, k, v, log_a, include_diag):
    B, L, H, DK = q.shape
    DV = v.shape[-1]
    C = GLA_CHUNK
    N = L // C
    q = q.reshape(B, N, C, H, DK)
    k = k.reshape(B, N, C, H, DK)
    v = v.reshape(B, N, C, H, DV)
    b = jnp.cumsum(log_a.reshape(B, N, C, H, DK), axis=2)
    b_last = b[:, :, -1]
    q_e = q * jnp.exp(b)
    k_e = k * jnp.exp(-b)
    scores = jnp.einsum('bnthd,bnshd->bnhts', q_e, k_e)
    mask = jnp.tril(jnp.ones((C, C), dtype=bool), k=0 if include_diag else -1)
    scores = jnp.where(mask, scores, 0.0)
    o_intra = jnp.einsum('bnhts,bnshe->bnthe', scores, v)
    k_dec = k * jnp.exp(b_last[:, :, None] - b)
    U = jnp.einsum('bnshd,bnshe->bnhde', k_dec, v)
    decay = jnp.exp(b_last)

    def step(S, inp):
        dec, inc = inp
        return dec[..., None] * S + inc, S

    S0 = jnp.zeros((B, H, DK, DV), U.dtype)
    _, S_prev = lax.scan(step, S0, (jnp.moveaxis(decay, 1, 0), jnp.moveaxis(U, 1, 0)))
    S_prev = jnp.moveaxis(S_prev, 0, 1)
    o_inter = jnp.einsum('bnthd,bnhde->bnthe', q_e, S_prev)
    return (o_intra + o_inter).reshape(B, L, H, DV)

def _gla_mixer(q, k, v, g, gate_lr, gate_w2, gate_b, norm_g):
    B, L, _ = q.shape
    q = q.reshape(B, L, GLA_HEADS, GLA_HEAD_K) * (GLA_HEAD_K ** -0.5)
    k = k.reshape(B, L, GLA_HEADS, GLA_HEAD_K)
    v = v.reshape(B, L, GLA_HEADS, GLA_HEAD_V)
    lr = gate_lr.reshape(B, L, 2, GLA_GATE_RANK)
    gk = jnp.einsum('blzr,zrd->blzd', lr, gate_w2) + gate_b
    log_a = jnp.maximum(jax.nn.log_sigmoid(gk.astype(jnp.float32)) / GLA_GATE_NORMALIZER,
                        GLA_LOG_GATE_MIN).reshape(B, L, 2, GLA_HEADS, GLA_HEAD_K)
    o_fwd = _gla_direction(q, k, v, log_a[:, :, 0], True)
    fl = lambda a: jnp.flip(a, axis=1)
    o_bwd = fl(_gla_direction(fl(q), fl(k), fl(v), fl(log_a[:, :, 1]), False))
    o = _rms_norm(o_fwd + o_bwd, norm_g)
    return o.reshape(B, L, GLA_VALUE_DIM).astype(g.dtype) * jax.nn.silu(g)

def _pool_mixer(u, pool_w, pool_scale):
    B, L, _ = u.shape
    pos = jnp.arange(L)
    groups = []
    for gi, w in enumerate(POOL_WINDOWS):
        xg = u[..., gi * POOL_GROUP:(gi + 1) * POOL_GROUP].astype(jnp.float32)
        half = w // 2
        xp = jnp.pad(xg, ((0, 0), (half, half), (0, 0)))
        cs = jnp.pad(jnp.cumsum(xp, axis=1), ((0, 0), (1, 0), (0, 0)))
        wsum = cs[:, w:w + L] - cs[:, :L]
        count = (jnp.minimum(pos + half, L) - jnp.maximum(pos - half, 0)).astype(jnp.float32)
        groups.append(wsum / count[None, :, None] - xg)
    d = jnp.stack(groups, axis=2)
    y = jnp.einsum('blgc,gcd->blgd', d, pool_w.astype(jnp.float32)).reshape(B, L, D_POOL)
    return (y * pool_scale.astype(jnp.float32)).astype(u.dtype)

def first_inputs(seed: int = 0) -> dict:
    key = jax.random.key(seed)
    ks = iter(jax.random.split(key, 40))
    f32 = jnp.float32
    n = DEPTH
    FO = HYENA_FILTER_ORDER

    def nrm(shape, scale):
        return jax.random.normal(next(ks), shape, f32) * scale

    def gain(shape, noise=0.05):
        return 1.0 + nrm(shape, noise)

    return {
        "x": nrm((BATCH, SEQ, D_MODEL), 1.0),
        "norm_mix_pre": gain((n, D_MODEL)),
        "norm_mix_post": gain((n, D_MODEL)),
        "norm_ffn_pre": gain((n, D_MODEL)),
        "norm_ffn_post": gain((n, D_MODEL)),
        "w_in": nrm((n, D_MODEL, D_IN), D_MODEL ** -0.5),
        "hy_conv_w": nrm((n, 3, 3 * D_HYENA), 3 ** -0.5),
        "hy_conv_b": nrm((n, 3 * D_HYENA), 0.02),
        "hy_filt_w1": nrm((n, HYENA_EMB_DIM, FO), HYENA_EMB_DIM ** -0.5),
        "hy_filt_b1": nrm((n, FO), 0.1),
        "hy_filt_freq1": gain((n, FO), 0.01),
        "hy_filt_w2": nrm((n, FO, FO), FO ** -0.5),
        "hy_filt_b2": nrm((n, FO), 0.1),
        "hy_filt_freq2": gain((n, FO), 0.01),
        "hy_filt_w3": nrm((n, FO, 2 * D_HYENA), 0.005),
        "hy_bias": nrm((n, D_HYENA), 1.0),
        "gla_gate_w2": nrm((n, 2, GLA_GATE_RANK, GLA_KEY_DIM), GLA_GATE_RANK ** -0.5),
        "gla_gate_b": nrm((n, 2, GLA_KEY_DIM), 0.1),
        "gla_norm": gain((n, GLA_HEAD_V), 0.01),
        "pool_w": nrm((n, len(POOL_WINDOWS), POOL_GROUP, POOL_GROUP), POOL_GROUP ** -0.5),
        "pool_scale": gain((n, D_POOL), 0.1),
        "w_br_hyena": nrm((n, D_HYENA, D_MODEL), D_HYENA ** -0.5),
        "w_br_gla": nrm((n, GLA_VALUE_DIM, D_MODEL), GLA_VALUE_DIM ** -0.5),
        "w_br_pool": nrm((n, D_POOL, D_MODEL), D_POOL ** -0.5),
        "w_out": nrm((n, D_MODEL, D_MODEL), D_MODEL ** -0.5),
        "ffn_w_up": nrm((n, D_MODEL, 2 * D_FF), D_MODEL ** -0.5),
        "ffn_conv_w": nrm((n, 3, D_FF), 3 ** -0.5),
        "ffn_conv_b": nrm((n, D_FF), 0.02),
        "ffn_w_down": nrm((n, D_FF, D_MODEL), D_FF ** -0.5),
    }

def first_block(x, norm_mix_pre, norm_mix_post, norm_ffn_pre, norm_ffn_post, w_in,
              hy_conv_w, hy_conv_b, hy_filt_w1, hy_filt_b1, hy_filt_freq1, hy_filt_w2,
              hy_filt_b2, hy_filt_freq2, hy_filt_w3, hy_bias, gla_gate_w2, gla_gate_b,
              gla_norm, pool_w, pool_scale, w_br_hyena, w_br_gla, w_br_pool, w_out,
              ffn_w_up, ffn_conv_w, ffn_conv_b, ffn_w_down):
    B, L, _ = x.shape
    t_pos, z_pos = _hyena_positional_features(L)
    for i in range(DEPTH):
        h = _rms_norm(x, norm_mix_pre[i])
        proj = h @ w_in[i]
        u_hy, q, k, v, g_out, gate_lr, u_pool, gate_logits = _split(proj, IN_SPLITS)
        y_hy = _hyena_mixer(u_hy, hy_conv_w[i], hy_conv_b[i], t_pos, z_pos,
                            hy_filt_w1[i], hy_filt_b1[i], hy_filt_freq1[i], hy_filt_w2[i],
                            hy_filt_b2[i], hy_filt_freq2[i], hy_filt_w3[i], hy_bias[i])
        y_gla = _gla_mixer(q, k, v, g_out, gate_lr, gla_gate_w2[i], gla_gate_b[i], gla_norm[i])
        y_pool = _pool_mixer(u_pool, pool_w[i], pool_scale[i])
        gates = jax.nn.sigmoid(gate_logits).reshape(B, L, N_BRANCHES, D_MODEL)
        merged = (gates[:, :, 0] * (y_hy @ w_br_hyena[i])
                  + gates[:, :, 1] * (y_gla @ w_br_gla[i])
                  + gates[:, :, 2] * (y_pool @ w_br_pool[i]))
        x = x + _rms_norm(merged @ w_out[i], norm_mix_post[i])
        h = _rms_norm(x, norm_ffn_pre[i])
        a, b = _split(h @ ffn_w_up[i], (D_FF, D_FF))
        a = _dwconv3_centred(a, ffn_conv_w[i], ffn_conv_b[i])
        y = (jax.nn.gelu(a, approximate=False) * b) @ ffn_w_down[i]
        x = x + _rms_norm(y, norm_ffn_post[i])
    return x


_first_inputs = first_inputs


def first_inputs(seed=0):
    import zlib

    import numpy as np

    out = dict(_first_inputs(seed))
    spreads = {}
    factors = {'hy_filt_b1': 3.546,
     'hy_filt_freq1': 8.0,
     'hy_filt_b2': 3.724,
     'hy_filt_freq2': 8.0,
     'gla_norm': 8.0,
     'ffn_conv_b': 3.271}
    for name, (base, spread) in spreads.items():
        noise = np.random.default_rng([zlib.crc32(name.encode()), seed]).standard_normal(out[name].shape)
        drawn = base * np.exp(spread * noise) if base else spread * noise
        out[name] = jnp.asarray(drawn.astype(out[name].dtype))
    for name, factor in factors.items():
        out[name] = (out[name] * factor).astype(out[name].dtype)
    return out


_narrow_inputs = first_inputs


def first_inputs(seed=0):
    out = dict(_narrow_inputs(seed))
    wider = {'hy_conv_b': 7.08, 'hy_filt_freq1': 3.99, 'hy_filt_freq2': 12.0, 'gla_norm': 5.1}
    for name, times in wider.items():
        mean = out[name].mean()
        out[name] = (mean + times * (out[name] - mean)).astype(out[name].dtype)
    return out


DEPTH_2 = 4

CTX_LEN = 256
GRID_W = 64
N_MIXERS = 3
N_HEADS = 16
HEAD_DIM = D_MODEL // N_HEADS
ATTN_SCALE = HEAD_DIM ** -0.5
WIN_ROWS_MAX = 8
WIN_COLS = 16
RPB_ROWS = 2 * WIN_ROWS_MAX - 1
RPB_COLS = 2 * WIN_COLS - 1
CONF_KERNEL = 31
SHORT_KERNEL = 3
D_FF_2 = 4 * D_MODEL
N_MOD = 6
EPS = 1e-6
N_NA = (DEPTH_2 + 2) // 3
N_CONF = (DEPTH_2 + 1) // 3
N_SC = DEPTH_2 // 3


def rmsnorm(x, g):
    xf = x.astype(jnp.float32)
    y = xf * lax.rsqrt(jnp.mean(xf * xf, axis=-1, keepdims=True) + EPS)
    return (y * g.astype(jnp.float32)).astype(x.dtype)

def layernorm(x, g, b):
    xf = x.astype(jnp.float32)
    mu = jnp.mean(xf, axis=-1, keepdims=True)
    xc = xf - mu
    var = jnp.mean(xc * xc, axis=-1, keepdims=True)
    y = xc * lax.rsqrt(var + EPS) * g.astype(jnp.float32) + b.astype(jnp.float32)
    return y.astype(x.dtype)

def modulate(h, shift, scale):
    return h * (1 + scale) + shift

def dwconv(x, w):
    k = w.shape[0]
    return lax.conv_general_dilated(
        x, w[:, None, :].astype(x.dtype), window_strides=(1,),
        padding=[((k - 1) // 2, k // 2)],
        dimension_numbers=("NWC", "WIO", "NWC"),
        feature_group_count=x.shape[-1])

def split_heads(t, n):
    b, l, _ = t.shape
    return t.reshape(b, l, n, N_HEADS, HEAD_DIM).transpose(2, 0, 3, 1, 4)

def neighbourhood_attention(h_lat, h_ctx, wqkv, wo, rpb, ctx_out):
    b, l, d = h_lat.shape
    rows = l // GRID_W
    kh = min(WIN_ROWS_MAX, rows)
    q, k, v = split_heads(h_lat @ wqkv, 3)
    q = q * ATTN_SCALE
    if ctx_out:
        q_c, k_c, v_c = split_heads(h_ctx @ wqkv, 3)
    else:
        k_c, v_c = split_heads(h_ctx @ wqkv[:, D_MODEL:], 2)
    q_grid = q.reshape(b, N_HEADS, rows, GRID_W, HEAD_DIM)
    k_grid = k.reshape(b, N_HEADS, rows, GRID_W, HEAD_DIM)
    v_grid = v.reshape(b, N_HEADS, rows, GRID_W, HEAD_DIM)

    r_ar = np.arange(rows)
    row_start = np.clip(r_ar - kh // 2, 0, rows - kh)
    row_off = row_start[:, None] + np.arange(kh)[None, :] - r_ar[:, None] + WIN_ROWS_MAX - 1
    c_ar = np.arange(GRID_W)
    col_idx = np.clip(c_ar - WIN_COLS // 2, 0, GRID_W - WIN_COLS)[:, None] + np.arange(WIN_COLS)[None, :]
    col_off = col_idx - c_ar[:, None] + WIN_COLS - 1
    bias_all = rpb[:, row_off[:, :, None, None], col_off[None, None, :, :]]
    bias_all = bias_all.transpose(1, 0, 3, 2, 4)
    n_lat = kh * WIN_COLS

    def row_block(xs):
        q_r, rs, bias_r = xs
        k_rows = lax.dynamic_slice_in_dim(k_grid, rs, kh, axis=2)
        v_rows = lax.dynamic_slice_in_dim(v_grid, rs, kh, axis=2)
        k_nb = k_rows[:, :, :, col_idx, :]
        v_nb = v_rows[:, :, :, col_idx, :]
        s_lat = jnp.einsum("bhqd,bhaqkd->bhqak", q_r, k_nb).astype(jnp.float32)
        s_lat = s_lat + bias_r.astype(jnp.float32)[None]
        s_ctx = jnp.einsum("bhqd,bhcd->bhqc", q_r, k_c).astype(jnp.float32)
        s = jnp.concatenate([s_lat.reshape(b, N_HEADS, GRID_W, n_lat), s_ctx], axis=-1)
        p = jax.nn.softmax(s, axis=-1).astype(v_nb.dtype)
        p_lat = p[..., :n_lat].reshape(b, N_HEADS, GRID_W, kh, WIN_COLS)
        p_ctx = p[..., n_lat:]
        return (jnp.einsum("bhqak,bhaqkd->bhqd", p_lat, v_nb)
                + jnp.einsum("bhqc,bhcd->bhqd", p_ctx, v_c))

    o_grid = lax.map(row_block, (jnp.moveaxis(q_grid, 2, 0),
                                 jnp.asarray(row_start, dtype=jnp.int32),
                                 bias_all))
    o_lat = o_grid.transpose(1, 0, 3, 2, 4).reshape(b, l, d) @ wo

    o_ctx = None
    if ctx_out:
        s_c = jnp.einsum("bhqd,bhkd->bhqk", q_c * ATTN_SCALE, k_c).astype(jnp.float32)
        p_c = jax.nn.softmax(s_c, axis=-1).astype(v_c.dtype)
        o_c = jnp.einsum("bhqk,bhkd->bhqd", p_c, v_c)
        o_ctx = o_c.transpose(0, 2, 1, 3).reshape(b, h_ctx.shape[1], d) @ wo
    return o_lat, o_ctx

def conformer_conv(h, w1, b1, dw, dwb, ln_g, ln_b, w2, b2):
    u = h @ w1 + b1
    a, g = jnp.split(u, 2, axis=-1)
    u = a * jax.nn.sigmoid(g)
    u = dwconv(u, dw) + dwb
    u = jax.nn.silu(layernorm(u, ln_g, ln_b))
    return u @ w2 + b2

def short_gated_conv(h, w_in, conv_w, w_out):
    bg, cg, v = jnp.split(h @ w_in, 3, axis=-1)
    return (bg * dwconv(cg * v, conv_w)) @ w_out

def sq_relu_mlp(h, w1, w2):
    return jnp.square(jax.nn.relu(h @ w1)) @ w2

def second_inputs(seed: int = 0) -> dict:
    key = jax.random.key(seed)
    ks = jax.random.split(key, 32)
    nrm = jax.random.normal
    f32 = jnp.float32
    d = D_MODEL
    return {
        "x": nrm(ks[0], (BATCH, SEQ, d), f32),
        "c": nrm(ks[1], (BATCH, d), f32),
        "ctx": nrm(ks[2], (BATCH, CTX_LEN, d), f32),
        "c_ctx": nrm(ks[3], (d,), f32),
        "mod_w": nrm(ks[4], (DEPTH_2, d, N_MOD * d), f32) * (0.5 * d ** -0.5),
        "mod_b": nrm(ks[5], (DEPTH_2, N_MOD * d), f32) * 0.01,
        "norm1_g": 1.0 + 0.01 * nrm(ks[6], (DEPTH_2, d), f32),
        "norm2_g": 1.0 + 0.01 * nrm(ks[7], (DEPTH_2, d), f32),
        "mlp_w1": nrm(ks[8], (DEPTH_2, d, D_FF_2), f32) * d ** -0.5,
        "mlp_w2": nrm(ks[9], (DEPTH_2, D_FF_2, d), f32) * D_FF_2 ** -0.5,
        "na_wqkv": nrm(ks[10], (N_NA, d, 3 * d), f32) * d ** -0.5,
        "na_wo": nrm(ks[11], (N_NA, d, d), f32) * d ** -0.5,
        "na_rpb": nrm(ks[12], (N_NA, N_HEADS, RPB_ROWS, RPB_COLS), f32) * 0.1,
        "cv_w1": nrm(ks[13], (N_CONF, d, 2 * d), f32) * d ** -0.5,
        "cv_b1": nrm(ks[14], (N_CONF, 2 * d), f32) * 0.01,
        "cv_dw": nrm(ks[15], (N_CONF, CONF_KERNEL, d), f32) * CONF_KERNEL ** -0.5,
        "cv_dwb": nrm(ks[16], (N_CONF, d), f32) * 0.01,
        "cv_ln_g": 1.0 + 0.01 * nrm(ks[17], (N_CONF, d), f32),
        "cv_ln_b": nrm(ks[18], (N_CONF, d), f32) * 0.01,
        "cv_w2": nrm(ks[19], (N_CONF, d, d), f32) * d ** -0.5,
        "cv_b2": nrm(ks[20], (N_CONF, d), f32) * 0.01,
        "sc_win": nrm(ks[21], (N_SC, d, 3 * d), f32) * d ** -0.5,
        "sc_conv": nrm(ks[22], (N_SC, SHORT_KERNEL, d), f32) * SHORT_KERNEL ** -0.5,
        "sc_wout": nrm(ks[23], (N_SC, d, d), f32) * d ** -0.5,
        "final_g": 1.0 + 0.01 * nrm(ks[24], (d,), f32),
    }

def second_block(x, c, ctx, c_ctx, mod_w, mod_b, norm1_g, norm2_g, mlp_w1, mlp_w2,
              na_wqkv, na_wo, na_rpb, cv_w1, cv_b1, cv_dw, cv_dwb, cv_ln_g, cv_ln_b,
              cv_w2, cv_b2, sc_win, sc_conv, sc_wout, final_g):
    b = x.shape[0]
    silu_c = jax.nn.silu(c)
    silu_cc = jax.nn.silu(c_ctx)[None]
    last_attn = max(i for i in range(DEPTH_2) if i % N_MIXERS == 0)
    for i in range(DEPTH_2):
        kind = i % N_MIXERS
        slot = i // N_MIXERS
        ctx_live = i < last_attn
        need_ctx_in = ctx_live or kind == 0
        mod_l = (silu_c @ mod_w[i] + mod_b[i]).reshape(b, N_MOD, 1, D_MODEL)
        a_l = modulate(rmsnorm(x, norm1_g[i]), mod_l[:, 0], mod_l[:, 1])
        a_c = None
        if need_ctx_in:
            mod_c = (silu_cc @ mod_w[i] + mod_b[i]).reshape(1, N_MOD, 1, D_MODEL)
            a_c = modulate(rmsnorm(ctx, norm1_g[i]), mod_c[:, 0], mod_c[:, 1])
        if kind == 0:
            y_l, y_c = neighbourhood_attention(a_l, a_c, na_wqkv[slot], na_wo[slot],
                                               na_rpb[slot], ctx_live)
        elif kind == 1:
            cp = (cv_w1[slot], cv_b1[slot], cv_dw[slot], cv_dwb[slot], cv_ln_g[slot],
                  cv_ln_b[slot], cv_w2[slot], cv_b2[slot])
            y_l = conformer_conv(a_l, *cp)
            y_c = conformer_conv(a_c, *cp) if ctx_live else None
        else:
            sp = (sc_win[slot], sc_conv[slot], sc_wout[slot])
            y_l = short_gated_conv(a_l, *sp)
            y_c = short_gated_conv(a_c, *sp) if ctx_live else None
        x = x + mod_l[:, 2] * y_l
        m_l = modulate(rmsnorm(x, norm2_g[i]), mod_l[:, 3], mod_l[:, 4])
        x = x + mod_l[:, 5] * sq_relu_mlp(m_l, mlp_w1[i], mlp_w2[i])
        if ctx_live:
            ctx = ctx + mod_c[:, 2] * y_c
            m_c = modulate(rmsnorm(ctx, norm2_g[i]), mod_c[:, 3], mod_c[:, 4])
            ctx = ctx + mod_c[:, 5] * sq_relu_mlp(m_c, mlp_w1[i], mlp_w2[i])
    return rmsnorm(x, final_g)


_first_inputs_2 = second_inputs


def second_inputs(seed=0):
    import zlib

    import numpy as np

    out = dict(_first_inputs_2(seed))
    spreads = {}
    factors = {'norm1_g': 8.0,
     'norm2_g': 6.41,
     'na_rpb': 8.0,
     'cv_b1': 64.0,
     'cv_dwb': 64.0,
     'cv_ln_g': 64.0,
     'cv_ln_b': 64.0,
     'cv_b2': 64.0,
     'final_g': 33.872}
    for name, (base, spread) in spreads.items():
        noise = np.random.default_rng([zlib.crc32(name.encode()), seed]).standard_normal(out[name].shape)
        drawn = base * np.exp(spread * noise) if base else spread * noise
        out[name] = __import__('jax').numpy.asarray(drawn.astype(out[name].dtype))
    for name, factor in factors.items():
        out[name] = (out[name] * factor).astype(out[name].dtype)
    return out


_narrow_inputs_2 = second_inputs


def second_inputs(seed=0):

    out = dict(_narrow_inputs_2(seed))
    wider = {'cv_ln_g': 5.96, 'cv_ln_b': 5.72, 'cv_b2': 4.32, 'final_g': 6.67}
    for name, times in wider.items():
        mean = out[name].mean()
        out[name] = (mean + times * (out[name] - mean)).astype(out[name].dtype)
    return out


def setup_inputs(seed=0):
    out = dict(first_inputs(seed))
    for name, value in second_inputs(seed + 1).items():
        if name != "x":
            out[name + "_2"] = value
    return out


def reference(
    x, norm_mix_pre, norm_mix_post, norm_ffn_pre, norm_ffn_post, w_in, hy_conv_w, hy_conv_b,
    hy_filt_w1, hy_filt_b1, hy_filt_freq1, hy_filt_w2, hy_filt_b2, hy_filt_freq2, hy_filt_w3,
    hy_bias, gla_gate_w2, gla_gate_b, gla_norm, pool_w, pool_scale, w_br_hyena, w_br_gla,
    w_br_pool, w_out, ffn_w_up, ffn_conv_w, ffn_conv_b, ffn_w_down, c_2, ctx_2, c_ctx_2,
    mod_w_2, mod_b_2, norm1_g_2, norm2_g_2, mlp_w1_2, mlp_w2_2, na_wqkv_2, na_wo_2, na_rpb_2,
    cv_w1_2, cv_b1_2, cv_dw_2, cv_dwb_2, cv_ln_g_2, cv_ln_b_2, cv_w2_2, cv_b2_2, sc_win_2,
    sc_conv_2, sc_wout_2, final_g_2,
):
    x = first_block(
        x, norm_mix_pre, norm_mix_post, norm_ffn_pre, norm_ffn_post, w_in, hy_conv_w, hy_conv_b,
        hy_filt_w1, hy_filt_b1, hy_filt_freq1, hy_filt_w2, hy_filt_b2, hy_filt_freq2,
        hy_filt_w3, hy_bias, gla_gate_w2, gla_gate_b, gla_norm, pool_w, pool_scale, w_br_hyena,
        w_br_gla, w_br_pool, w_out, ffn_w_up, ffn_conv_w, ffn_conv_b, ffn_w_down,
    )
    return second_block(
        x, c_2, ctx_2, c_ctx_2, mod_w_2, mod_b_2, norm1_g_2, norm2_g_2, mlp_w1_2, mlp_w2_2,
        na_wqkv_2, na_wo_2, na_rpb_2, cv_w1_2, cv_b1_2, cv_dw_2, cv_dwb_2, cv_ln_g_2, cv_ln_b_2,
        cv_w2_2, cv_b2_2, sc_win_2, sc_conv_2, sc_wout_2, final_g_2,
    )


_drawn_inputs = setup_inputs


def setup_inputs(seed=0):
    import zlib

    import numpy as np

    out = dict(_drawn_inputs(seed))
    spreads = {}
    factors = {}
    for name, (base, spread) in spreads.items():
        noise = np.random.default_rng([zlib.crc32(name.encode()), seed]).standard_normal(out[name].shape)
        drawn = base * np.exp(spread * noise) if base else spread * noise
        out[name] = jnp.asarray(drawn.astype(out[name].dtype))
    for name, factor in factors.items():
        out[name] = (out[name] * factor).astype(out[name].dtype)
    return out
```

```python
from contextlib import ExitStack

import numpy as np

import concourse.bass as bass
from concourse import mybir

ALU = mybir.AluOpType
ACT = mybir.ActivationFunctionType
AX = mybir.AxisListType
F32 = mybir.dt.float32

P = 128
D = 1024
KD = D // P
SEQ = 256
T1 = SEQ
T2 = 2 * SEQ
EPS = 1e-6
CREDIT = 4

DEPTH1 = 2
HY = 512
EMB = 33
ORDER = 64
HEADS1 = 4
RANK = 16
GLA_C = 64
WINDOWS = (2, 4, 8, 16)
D_FF = 2816
NFF = D_FF // P
D_IN = 3 * HY + 4 * 512 + 2 * RANK + 512 + 3 * D

DEPTH2 = 4
HEADS2 = 16
HD = D // HEADS2
GRID = 64
ROWS = SEQ // GRID
WCOLS = 16
RPB_R, RPB_C = 15, 31
TAPS = 31
FF2 = 4 * D
NF2 = FF2 // P

C_U, C_Q, C_K, C_V, C_G = 0, 1536, 2048, 2560, 3072
C_LR = 3584
C_POOL = C_LR + 2 * RANK
C_GATE = C_POOL + 512

CON = {}
_at = 0
for _n, _w in (("ident", P), ("flip", P), ("window", GRID),
               ("mask_f", P), ("mask_b", P), ("scan_f", SEQ), ("scan_b", SEQ), ("zT", SEQ),
               ("cos", 2 * SEQ), ("sin", 2 * SEQ), ("icos", 2 * SEQ), ("isin", 2 * SEQ),
               ("decay", 2 * HY), ("band", 8 * SEQ)):
    CON[_n] = (_at, _at + _w)
    _at += _w
NCON = _at
CON2 = CON["window"][1]

ROW1 = {}
_at = 0
for _n, _w in (("norm_mix_pre", 8), ("norm_mix_post", 8), ("norm_ffn_pre", 8), ("norm_ffn_post", 8),
               ("hy_conv_w", 36), ("hy_conv_b", 12), ("hy_bias", 4), ("gla_gate_b", 8), ("gla_norm", 1),
               ("pool_scale", 4), ("hy_filt_b1", 1), ("hy_filt_freq1", 1), ("hy_filt_b2", 1),
               ("hy_filt_freq2", 1), ("ffn_conv_w", 66), ("ffn_conv_b", 22)):
    ROW1[_n] = _at
    _at += _w
ROW2 = {}
_at = 0
for _n, _w in (("mod_b_2", 192), ("norm1_g_2", 32), ("norm2_g_2", 32), ("cv_b1_2", 16), ("cv_dw_2", 248),
               ("cv_dwb_2", 8), ("cv_ln_g_2", 8), ("cv_ln_b_2", 8), ("cv_b2_2", 8), ("sc_conv_2", 24),
               ("final_g_2", 8), ("c_2", 8), ("c_ctx_2", 8)):
    ROW2[_n] = _at
    _at += _w
NT1, NT2 = 2, 5

SL1 = {"u": (0, 3), "q": (3, 1), "k": (4, 1), "v": (5, 1), "g": (6, 1), "pool": (7, 1), "gates": (8, 6),
       "branch": (14, 3), "w_out": (17, 4), "up": (21, 11), "down": (32, 8)}
PER1 = 40
SL2 = {"mod": (0, 12), "mlp_up": (20, 8), "mlp_down": (28, 8),
       "qkv": (12, 6), "wo": (18, 2), "cv1": (12, 4), "cv2": (16, 4), "sc1": (12, 6), "sc2": (18, 2)}
PER2 = 36
ACT_LINKS, DVE_LINKS = 4, 89
MAGIC = 12582912.0
TWO_PI_HI, TWO_PI_MID, TWO_PI_LO = 6.28125, 0.0019350051879882812, 3.019916e-07


class Linear:

    def __init__(self, full, out, slab0, slabs, per, banks, split=None, out2=None):
        self.full, self.out, self.slab0, self.slabs, self.per, self.banks = full, out, slab0, slabs, per, banks
        self.events = slabs * per
        self.out2, self.first = out2, self.events if out2 is None else split

    def all_out(self, uses):
        return uses * self.first + self.first + CREDIT

    def wait_all_out(self, eng, uses):
        eng.wait_ge(self.out, self.all_out(uses))
        if self.out2 is not None:
            eng.wait_ge(self.out2, uses * (self.events - self.first) + self.events - self.first)

    def wait_bank(self, eng, uses, i4, e):
        if e < self.first + 4:
            eng.wait_ge(self.out, uses * self.first + i4 * self.per + e + 1)
        else:
            eng.wait_ge(self.out2, uses * (self.events - self.first) + e - self.first - 4 + 1)

    def read(self, e):
        return self.out if e < self.first else self.out2


class Links:

    def __init__(self, eng, sem):
        self.eng, self.sem, self.base, self.n = eng, sem, 0, 0

    def __call__(self, ins):
        self.mark(ins)
        self.wait()

    def mark(self, ins):
        ins.then_inc(self.sem, 1)
        self.n += 1

    def wait(self):
        self.eng.wait_ge(self.sem, self.base + self.n)


def build(nc, x, ctx_in, con, prm1, prm2, w, out):
    with ExitStack() as stack:
        def sb(name, shape):
            return stack.enter_context(nc.sbuf_tensor(name, shape, F32))

        def sem(name):
            return stack.enter_context(nc.semaphore(name))

        X = sb("X", [P, KD, T2])
        H = sb("H", [P, KD, T2])
        BIG = sb("BIG", [P, 16384])
        RING = sb("RING", [P, 4, 4096])
        CN = sb("CN", [P, NCON])
        SM = sb("SM", [P, 3200])
        PR1 = sb("PR1", [P, DEPTH1 * NT1 * P])
        PR2 = sb("PR2", [P, NT2 * P])
        PRC = sb("PRC", [P, NT1 * P])
        SCR = sb("SCR", [P, 512])
        ONES = sb("ONES", [P, P])
        TG = CN[:, CON2 + 1536:CON2 + 2048].rearrange("p (s t) -> p s t", s=2)
        MOD = sb("MOD", [P, 6 * KD, 2])
        GM = sb("GM", [P, KD, 2])
        epsc = sb("epsc", [P, 1])
        SC = sb("SC", [P, KD, 2])
        PS = stack.enter_context(nc.psum_tensor("PS", [P, 8, 512], F32))

        def c(name):
            return CN[:, CON[name][0]:CON[name][1]]

        def v3(ap, n):
            return ap.rearrange("p (c t) -> p c t", c=n)

        ident, flip, window = c("ident"), c("flip"), c("window")
        zT = CN[0:EMB, CON["zT"][0]:CON["zT"][1]]
        COS, SIN, ICOS, ISIN = (v3(c(n), 2) for n in ("cos", "sin", "icos", "isin"))
        DECAY = v3(c("decay"), 2)
        BAND = c("band").rearrange("p (s g t) -> p s g t", s=2, g=4)

        FW1 = SM[0:EMB, 0:64]
        FW2 = SM[0:ORDER, 64:128]
        FW3 = SM[0:ORDER, 128:1152]
        GW2 = SM[0:2 * RANK, 1152:2176].rearrange("p (z d) -> p z d", z=2)
        PW = v3(SM[:, 2176:2688], 4)
        LRW = v3(SM[:, 2688:2944], KD)
        LR = SM[0:2 * RANK, 2944:3200]

        U = v3(BIG[:, 0:3072], 12)
        Q = v3(BIG[:, 3072:4096], 4)
        K = v3(BIG[:, 4096:5120], 4)
        G = v3(BIG[:, 5120:6144], 4)
        V = v3(BIG[:, 6144:7168], 2)
        UP = v3(BIG[:, 7168:8192], 2)
        YP = v3(BIG[:, 7168:8192], 4)
        W = BIG[:, 8192:16384]
        RAW = v3(W[:, 6144:7168], 4)
        HF, HB, FA, FB = (v3(W[:, i * 1024:(i + 1) * 1024], 2) for i in range(4))
        FARG = W[0:ORDER, 4096:4352]
        FK = W[0:ORDER, 4352:4608]
        H1 = W[0:ORDER, 4608:4864]
        KA = H[:, 0:4, T1:T2]
        KB = H[:, 4:8, T1:T2]
        ZV = v3(W[:, 0:1024], 4)
        ZT = v3(W[:, 1024:2048], 2)
        ZC = v3(W[:, 2048:3072], 4)
        ZS = v3(W[:, 3072:4096], 4)
        PP = v3(W[:, 4096:5120], 4)
        RR = v3(W[:, 5120:6144], 4)
        TMP = v3(W[:, 1024:2048], 4)
        DP = v3(W[:, 7168:8192], 4)
        X1, B1 = W[:, 0:1024], W[:, 1024:2048]
        E1, KE, QE = W[:, 2048:3072], W[:, 3072:4096], W[:, 4096:5120]
        SCO, KT = W[:, 5120:6144], W[:, 6144:7168]
        ST = [W[:, 1024:1536], W[:, 1536:2048], W[:, 7168:7680]]
        OG = BIG[:, 1024:2048]
        GT = v3(W[:, 0:6144], 24)
        MG = v3(W[:, 6144:8192], 8)
        Y1 = v3(BIG[:, 0:2048], KD)
        SQ1 = v3(BIG[:, 14336:16384], KD)
        FT = v3(BIG[:, 0:NFF * T1], NFF)
        FRAW = v3(BIG[:, 11264:12288], 4)
        Y2 = v3(BIG[:, 12288:14336], KD)

        RT2, RS2, MU = CN[:, CON2:CON2 + 512], CN[:, CON2 + 512:CON2 + 1024], CN[:, CON2 + 1024:CON2 + 1536]
        QT = v3(BIG[:, 0:4096], KD)
        KT2 = v3(BIG[:, 4096:8192], KD)
        VT = v3(BIG[:, 8192:12288], 4)
        OT = v3(BIG[:, 12288:16384], KD)
        SQ2 = v3(BIG[:, 12288:16384], KD)
        BI = [SM[:, 512 * j:512 * j + 512].rearrange("p (t r q) -> p t r q", t=2, r=ROWS) for j in range(2)]
        PB = [SM[:, 1024 + 512 * j:1536 + 512 * j] for j in range(2)]
        PT = [v3(SM[:, 2048 + 512 * j:2560 + 512 * j], 4) for j in range(2)]
        MX = SM[:, 3072:3200].rearrange("p (u c) -> p u c", c=2)
        HID = v3(BIG[:, :], NF2)
        UA = v3(BIG[:, 0:4096], KD)
        UPAD = BIG[:, 4096:4096 + KD * 2 * 286].rearrange("p (c h t) -> p c h t", c=KD, h=2)
        CV = v3(BIG[:, 8704:12800], KD)
        XC = v3(BIG[:, 4096:8192], KD)
        BG, CG, SV, SY = (v3(BIG[:, 4096 * i:4096 * i + 4096], KD) for i in range(4))

        s_x, s_ctx, s_con, s_tab = sem("x_loaded"), sem("ctx_loaded"), sem("consts_loaded"), sem("tables_loaded")
        s_small = sem("small_weights_loaded")
        s_slab = [sem(f"slab_loaded_{i}") for i in range(4)]
        slab_done = sem("slab_done")
        dve_step, act_step = sem("dve_step"), sem("act_step")
        ones_set, tab_full, tab_out = sem("ones_set"), sem("table_turned"), sem("table_in_place")
        x_new = sem("x_new")
        sq_ready, stat_full, root_ready, h_ready = sem("squares"), sem("sums"), sem("roots"), sem("h_chunks")
        prm_ready = sem("layer_params")

        def stage(name, slabs, per, banks, split=None):
            return Linear(sem(name + "_full"), sem(name + "_out"), slabs[0], slabs[1], per, banks,
                          split, None if split is None else sem(name + "_out_by_vector"))

        LO, HI = (0, 1, 2, 3), (4, 5, 6, 7)
        L1 = {"u": stage("u", SL1["u"], 4, LO), "q": stage("q", SL1["q"], 4, HI), "k": stage("k", SL1["k"], 4, LO),
              "v": stage("v", SL1["v"], 2, HI), "g": stage("g", SL1["g"], 4, LO),
              "pool": stage("pool", SL1["pool"], 2, HI), "gates": stage("gates", SL1["gates"], 4, HI),
              "branch": stage("branch", SL1["branch"], 8, LO), "w_out": stage("w_out", SL1["w_out"], 2, HI),
              "up": stage("up", SL1["up"], 4, LO, NFF), "down": stage("down", SL1["down"], 1, LO)}
        L2 = {"mlp_up": stage("mlp_up", SL2["mlp_up"], 4, LO),
              "mlp_down": stage("mlp_down", SL2["mlp_down"], 1, HI), "qkv": stage("qkv", SL2["qkv"], 4, LO, 16),
              "wo": stage("wo", SL2["wo"], 4, LO), "cv1": stage("cv1", SL2["cv1"], 4, LO),
              "cv2": stage("cv2", SL2["cv2"], 2, LO), "sc1": stage("sc1", SL2["sc1"], 4, LO, 16),
              "sc2": stage("sc2", SL2["sc2"], 4, HI)}
        stages = list(L1.values()) + list(L2.values())

        filt_full, filt_out = sem("filter_psum"), sem("filter_sbuf")
        sin_arg, sin_out = sem("sine_arguments"), sem("sines")
        kern_full, kern_out = sem("kernel_spectrum_psum"), sem("kernel_spectrum")
        conv_u, conv_f = sem("u_convolved"), sem("ffn_convolved")
        zv_ready, zt_full, zt_out = sem("zv_ready"), sem("zv_turned_psum"), sem("zv_turned")
        zf_full, zf_out, prod_ready = sem("spectrum_psum"), sem("spectrum"), sem("spectra_product")
        hy_full, hy_out = sem("hyena_psum"), sem("hyena_out")
        pd_full, pd_out, pw_full, pw_out = sem("pool_diff_psum"), sem("pool_diff"), sem("pool_psum"), sem("pooled_out")
        lr_full, lr_out = sem("lowrank_psum"), sem("lowrank")
        gk_full, gk_out, ls_ready = sem("gate_psum"), sem("gate_logits"), sem("log_sigmoid_part")
        cum_ready, exp_ready, qk_ready = sem("log_decay_sums"), sem("decay_exps"), sem("decayed_qk")
        sco_full, sco_out = sem("gla_scores_psum"), sem("gla_scores")
        kt_full, kt_out = sem("gla_k_turned_psum"), sem("gla_k_turned")
        st_full, st_out = sem("gla_state_psum"), sem("gla_states")
        og_full, og_out = sem("gla_o_psum"), sem("gla_o")
        gsq, gst_full, groot, gla_done = sem("gla_squares"), sem("gla_sums"), sem("gla_roots"), sem("gla_done")
        gelu_out, ffn_hid = sem("gelu_out"), sem("ffn_hidden")
        mod_ready, mod_psum, silu_c = sem("mod_vectors"), sem("mod_psum"), sem("silu_c")
        g_folded, h_scaled = sem("gain_folded"), sem("h_before_shift")
        hid2, tg_ready = sem("mlp_hidden"), sem("gated_mlp")
        bias_loaded = [sem("bias_loaded_0"), sem("bias_loaded_1")]
        bias_ready = sem("bias_masked")
        sc_full, max_ready, p_exp, p_norm = sem("scores"), sem("row_maxima"), sem("exps"), sem("probs")
        pt_full, pt_out, o_full, o_out = sem("probs_turned_psum"), sem("probs_turned"), sem("attn_psum"), sem("attn")
        cv_u, cv_dw, mu_full, mu_out = sem("conformer_gated"), sem("conformer_conv"), sem("mean_psum"), sem("means")
        xc_ready, cv_sq, cv_stat, cv_root = sem("centred"), sem("cv_squares"), sem("cv_sums"), sem("cv_roots")
        cv_norm, cv_act = sem("cv_normed"), sem("cv_activated")
        pad_set, sg_ready = sem("pads_zeroed"), sem("conformer_gates")
        sc_bg = sem("short_conv_gated")
        stored = sem("stored")
        h_shift = sem("h_modulated")

        def finished(eng, L, uses, before, i4, u, cc):
            if cc == L.per - 1:
                eng.wait_ge(slab_done, before + L.slab0 + i4 + u + 1 + CREDIT)
            else:
                eng.wait_ge(L.full, uses * (L.slabs * (L.per - 1)) + (i4 + u) * (L.per - 1) + cc + 1)

        blk = stack.enter_context(nc.Block())

        def slab(s, k, n):
            return RING[:, s % 4, 0:k * n].rearrange("p (k n) -> p k n", k=k)

        def tiles(a):
            return (0, 1, 2, 3) if a == 0 else (0, 1)

        def first_unit(a, h):
            return h * len(tiles(a))

        def unit0(a):
            return a * HEADS2 * 4

        def bank(L, e):
            return PS[:, L.banks[e % 4]]

        @blk.sync
        def _(sp):
            sp.dma_start(X[:, :, 0:T1], x.rearrange("(c p) t -> p c t", p=P)).then_inc(s_x, 16)
            sp.dma_start(CN[:, :], con).then_inc(s_con, 16)

            def load(s, dst, src, before4):
                sp.wait_ge(slab_done, before4 + s + 1)
                sp.dma_start(dst, src).then_inc(s_slab[s % 4], 16)

            def rows(a):
                return a.rearrange("l (k p) n -> l p k n", p=P)

            w_in, w_outs, up, down = rows(w["w_in"]), rows(w["w_out"]), rows(w["ffn_w_up"]), rows(w["ffn_w_down"])
            with sp.Fori(0, DEPTH1) as lay:
                base = lay * PER1
                cols = [C_U, C_U + 512, C_U + 1024, C_Q, C_K, C_V, C_G, C_POOL] + [C_GATE + 512 * i for i in range(6)]
                for s, col in enumerate(cols):
                    load(s, slab(s, KD, 512), w_in[lay, :, :, col:col + 512], base)
                for j, n in enumerate(("w_br_hyena", "w_br_gla", "w_br_pool")):
                    s = SL1["branch"][0] + j
                    load(s, slab(s, 4, D), rows(w[n])[lay], base)
                for j in range(4):
                    s = SL1["w_out"][0] + j
                    load(s, slab(s, KD, 256), w_outs[lay, :, :, 256 * j:256 * j + 256], base)
                for j in range(11):
                    s = SL1["up"][0] + j
                    load(s, slab(s, KD, 512), up[lay, :, :, 512 * j:512 * j + 512], base)
                with sp.Fori(0, 2) as i:
                    for u in range(4):
                        sp.wait_ge(slab_done, base + SL1["down"][0] + i * 4 + u + 1)
                        sp.dma_start(slab(u, NFF, P), down[lay, :, :, bass.ds(i * 512 + u * P, P)]
                                     ).then_inc(s_slab[u], 16)

            modw, m1, m2 = rows(w["mod_w_2"]), rows(w["mlp_w1_2"]), rows(w["mlp_w2_2"])
            for l in range(DEPTH2):
                base = DEPTH1 * PER1 + l * PER2

                def cols512(s0, src, n, width=512):
                    for j in range(n):
                        load(s0 + j, slab(s0 + j, KD, width), src[:, :, width * j:width * j + width], base)

                with sp.Fori(0, 3) as i:
                    for u in range(4):
                        sp.wait_ge(slab_done, base + i * 4 + u + 1)
                        sp.dma_start(slab(u, KD, 512), modw[l][:, :, bass.ds(i * 2048 + u * 512, 512)]
                                     ).then_inc(s_slab[u], 16)
                if l % 3 == 0:
                    cols512(12, rows(w["na_wqkv_2"])[l // 3], 6)
                    cols512(18, rows(w["na_wo_2"])[l // 3], 2)
                elif l % 3 == 1:
                    cols512(12, rows(w["cv_w1_2"])[0], 4)
                    cols512(16, rows(w["cv_w2_2"])[0], 4, 256)
                else:
                    cols512(12, rows(w["sc_win_2"])[0], 6)
                    cols512(18, rows(w["sc_wout_2"])[0], 2)
                with sp.Fori(0, 2) as i:
                    for u in range(4):
                        sp.wait_ge(slab_done, base + 20 + i * 4 + u + 1)
                        sp.dma_start(slab(u, KD, 512), m1[l][:, :, bass.ds(i * 2048 + u * 512, 512)]
                                     ).then_inc(s_slab[u], 16)
                with sp.Fori(0, 2) as i:
                    for u in range(4):
                        sp.wait_ge(slab_done, base + 28 + i * 4 + u + 1)
                        sp.dma_start(slab(u, NF2, P), m2[l][:, :, bass.ds(i * 512 + u * P, P)]
                                     ).then_inc(s_slab[u], 16)
            sp.wait_ge(h_ready, 8 * (2 * DEPTH1 + 2 * DEPTH2 + 1))
            sp.dma_start(out.rearrange("(c p) t -> p c t", p=P), H[:, :, 0:T1]).then_inc(stored, 16)
            sp.wait_ge(stored, 16)

        @blk.gpsimd
        def _(gp):
            for st in stages:
                gp.sem_inc(st.out, CREDIT)
            for s in (slab_done, conv_u, conv_f):
                gp.sem_inc(s, CREDIT)
            gp.sem_inc(mod_psum, 1)
            nc.gpsimd.memset(GW2, 0.0).then_inc(ones_set, 1)
            nc.gpsimd.memset(ONES[:, :], 1.0).then_inc(ones_set, 1)
            nc.gpsimd.memset(epsc[:, :], EPS).then_inc(ones_set, 1)
            gp.dma_start(v3(BIG[:, 0:512], 4), prm1.rearrange("t r f -> r t f")).then_inc(s_tab, 16)
            gp.dma_start(v3(BIG[:, 512:1152], 5), prm2.rearrange("t r f -> r t f")).then_inc(s_tab, 16)
            gp.wait_ge(ones_set, 3)
            gp.sem_inc(gla_done, 1)
            with gp.Fori(0, DEPTH1) as lay:
                gp.wait_ge(gla_done, lay + 1)
                for dst, src in ((FW1, w["hy_filt_w1"][lay]), (FW2, w["hy_filt_w2"][lay]), (FW3, w["hy_filt_w3"][lay]),
                                 (GW2[0:RANK, 0, :], w["gla_gate_w2"][lay, 0]),
                                 (GW2[RANK:2 * RANK, 1, :], w["gla_gate_w2"][lay, 1]),
                                 (PW, w["pool_w"].rearrange("l g c d -> l c g d")[lay]),
                                 (LRW, w["w_in"].rearrange("l (k p) n -> l p k n", p=P)[lay, :, :, C_LR:C_LR + 2 * RANK])):
                    gp.dma_start(dst, src).then_inc(s_small, 16)
            gp.wait_ge(x_new, 1 + 2 * DEPTH1)
            gp.dma_start(X[:, :, T1:T2], ctx_in.rearrange("(c p) t -> p c t", p=P)).then_inc(s_ctx, 16)
            rpb = w["na_rpb_2"]
            for a in range(2):
                if a == 1:
                    gp.wait_ge(x_new, 1 + 2 * DEPTH1 + 6)
                for h in range(HEADS2):
                    n = a * HEADS2 + h
                    if h >= 2:
                        gp.wait_ge(sc_full, unit0(a) + first_unit(a, h - 1))
                    elif a == 1:
                        gp.wait_ge(sc_full, unit0(1))
                    for t in range(2):
                        for r in range(2):
                            off = (a * HEADS2 + h) * RPB_R * RPB_C + (6 - 2 * t) * RPB_C - 48 + RPB_C * r
                            src = bass.AP(rpb.tensor, off, [[1, GRID], [RPB_C, ROWS], [1, GRID]])
                            gp.dma_start(BI[h % 2][GRID * r:GRID * r + GRID, t], src).then_inc(bias_loaded[h % 2], 16)
                    gp.wait_ge(bias_loaded[h % 2], 64 * (n // 2 + 1))
                    for t in range(2):
                        mk = nc.gpsimd.tensor_tensor(BI[h % 2][:, t], BI[h % 2][:, t],
                                                     window.rearrange("p (o q) -> p o q", o=1)
                                                     .to_broadcast([P, ROWS, GRID]), ALU.add)
                    mk.then_inc(bias_ready, 1)

        @blk.tensor
        def _(pe):
            def chain(dst, pairs):
                n = len(pairs)
                for i, (a, b) in enumerate(pairs):
                    mm = pe.matmul(dst, a, b, start=i == 0, stop=i == n - 1)
                return mm

            def product(L, uses, before, i4, u, cc, dst, pairs):
                s = L.slab0 + u
                if cc == 0:
                    pe.wait_ge(s_slab[s % 4], before * 4 + i4 * 4 + 16 * (s // 4 + 1))
                L.wait_bank(pe, uses, i4, u * L.per + cc)
                mm = chain(dst, pairs)
                if cc == L.per - 1:
                    mm.then_inc(slab_done, 1)
                else:
                    mm.then_inc(L.full, 1)

            def linear(L, uses, before, rhs, k, n, T, i4=0, us=None, first=None):
                for u in (range(L.slabs) if us is None else us):
                    ws = slab(L.slab0 + u, k, n)
                    for cc in range(L.per):
                        product(L, uses, before, i4, u, cc, bank(L, u * L.per + cc)[:, 0:T],
                                [(ws[:, kk, P * cc:P * cc + P], rhs(kk)) for kk in range(k)])

            def norm_sums(n, sq, T):
                for half in range(2):
                    pe.wait_ge(sq_ready, n * 2 + half + 1)
                    for kk in range(4 * half, 4 * half + 4):
                        mm = pe.matmul(PS[:, 7, 0:T], ONES[:, :], sq[:, kk, 0:T], start=kk == 0, stop=kk == 7)
                mm.then_inc(stat_full, 1)

            pe.wait_ge(s_tab, 32)
            pe.wait_ge(s_con, 16)
            pe.wait_ge(ones_set, 3)
            for t in range(2 * NT1 + NT2):
                tr = pe.transpose(PS[:, t // 4, P * (t % 4):P * (t % 4) + P], BIG[:, P * t:P * t + P], ident)
            tr.then_inc(tab_full, 1)
            pe.wait_ge(tab_out, 1)

            with pe.Fori(0, DEPTH1) as lay:
                before = lay * PER1
                pe.wait_ge(s_small, lay * 112 + 112)
                pe.wait_ge(prm_ready, lay + 1)
                pe.matmul(PS[:, 0, 0:SEQ], SM[0:EMB, 0:P], zT, start=True, stop=True).then_inc(filt_full, 1)
                pe.wait_ge(sin_out, lay * 2 + 1)
                pe.matmul(PS[:, 1, 0:SEQ], SM[0:ORDER, 64:64 + P], H1, start=True, stop=True).then_inc(filt_full, 1)
                pe.wait_ge(sin_out, lay * 2 + 2)
                for half in range(2):
                    for tt in range(2):
                        pe.matmul(PS[:, 2 * half + tt], H1[:, P * tt:P * tt + P], FW3[:, 512 * half:512 * half + 512],
                                  start=True, stop=True).then_inc(filt_full, 1)
                pe.wait_ge(filt_out, lay + 1)
                for j, (m, src) in enumerate(((COS, FA), (SIN, FB))):
                    for f in range(2):
                        chain(PS[:, 4 + 2 * j + f], [(m[:, ss, P * f:P * f + P], src[:, ss, :]) for ss in range(2)]
                              ).then_inc(kern_full, 1)
                pe.wait_ge(kern_out, lay * 4 + 4)

                norm_sums(lay * 4, SQ1, T1)
                pe.wait_ge(h_ready, lay * 16 + 8)
                rhs = lambda kk: H[:, kk, 0:T1]
                linear(L1["u"], lay, before, rhs, KD, 512, T1)
                linear(L1["q"], lay, before, rhs, KD, 512, T1)
                L1["u"].wait_all_out(pe, lay)
                linear(L1["k"], lay, before, rhs, KD, 512, T1)
                L1["q"].wait_all_out(pe, lay)
                for tt in range(2):
                    product(L1["v"], lay, before, 0, 0, tt, bank(L1["v"], tt),
                            [(H[:, kk, P * tt:P * tt + P], slab(5, KD, 512)[:, kk, :]) for kk in range(KD)])
                L1["k"].wait_all_out(pe, lay)
                linear(L1["g"], lay, before, rhs, KD, 512, T1)
                chain(PS[0:2 * RANK, 6, 0:T1], [(LRW[:, kk, :], rhs(kk)) for kk in range(KD)]).then_inc(lr_full, 1)
                L1["v"].wait_all_out(pe, lay)
                for tt in range(2):
                    product(L1["pool"], lay, before, 0, 0, tt, bank(L1["pool"], tt),
                            [(H[:, kk, P * tt:P * tt + P], slab(7, KD, 512)[:, kk, :]) for kk in range(KD)])

                L1["pool"].wait_all_out(pe, lay)
                L1["g"].wait_all_out(pe, lay)
                for g in range(4):
                    chain(PS[:, g, 0:T1], [(UP[:, ss, P * g:P * g + P], BAND[:, ss, g, :]) for ss in range(2)]
                          ).then_inc(pd_full, 1)
                for g in range(4):
                    pe.wait_ge(pd_out, lay * 4 + g + 1)
                    pe.matmul(PS[:, 4 + g, 0:T1], PW[:, g, :], DP[:, g, :], start=True, stop=True).then_inc(pw_full, 1)

                pe.wait_ge(zv_ready, lay + 1)
                for ss in range(2):
                    for j in range(4):
                        tr = pe.transpose(PS[:, ss, P * j:P * j + P], ZV[:, j, P * ss:P * ss + P], ident)
                    tr.then_inc(zt_full, 1)
                pe.wait_ge(zt_out, lay * 2 + 2)
                pe.wait_ge(pw_out, lay * 4 + 4)
                for j, m in enumerate((COS, SIN)):
                    for f in range(2):
                        chain(PS[:, 4 + 2 * j + f], [(m[:, ss, P * f:P * f + P], ZT[:, ss, :]) for ss in range(2)]
                              ).then_inc(zf_full, 1)
                pe.wait_ge(prod_ready, lay + 1)
                P2 = W[:, 4096:5120].rearrange("p (f n) -> p f n", f=2)
                R2 = W[:, 5120:6144].rearrange("p (f n) -> p f n", f=2)
                for j in range(4):
                    chain(PS[:, j, 0:T1], [(P2[:, f, P * j:P * j + P], ICOS[:, f, :]) for f in range(2)]
                          + [(R2[:, f, P * j:P * j + P], ISIN[:, f, :]) for f in range(2)]).then_inc(hy_full, 1)

                pe.wait_ge(lr_out, lay + 1)
                for z in range(2):
                    zz = lay * 2 + z
                    pe.wait_ge(zf_out, lay * 4 + 4) if z == 0 else pe.wait_ge(sco_out, lay * 4 + 2)
                    for j in range(4):
                        mm = pe.matmul(PS[:, 4 + j // 2, T1 * (j % 2):T1 * (j % 2) + T1],
                                       GW2[:, z, P * j:P * j + P], LR, start=True, stop=True)
                        if j % 2:
                            mm.then_inc(gk_full, 1)
                    pe.wait_ge(qk_ready, zz + 1)
                    for b in range(2):
                        for j in range(4):
                            h, tt = 2 * b + j // 2, j % 2
                            o = T1 * h + P * tt
                            mm = pe.matmul(PS[:, 4 + b, P * j:P * j + P], KE[:, o:o + P], QE[:, o:o + P],
                                           start=True, stop=True)
                        mm.then_inc(sco_full, 1)
                    if z == 1:
                        pe.wait_ge(og_out, lay * 4 + 2)
                    for b in range(2):
                        for j in range(4):
                            o = 512 * b + P * j
                            tr = pe.transpose(PS[:, 6 + b, P * j:P * j + P], X1[:, o:o + P], ident)
                        tr.then_inc(kt_full, 1)
                    pe.wait_ge(kt_out, zz * 2 + 2)
                    pe.wait_ge(hy_out, lay * 4 + 4)
                    for i, n in enumerate((0, 1, 2) if z == 0 else (3, 2, 1)):
                        r = GLA_C * (n % 2)
                        for h in range(HEADS1):
                            o = T1 * h + P * (n // 2)
                            mm = pe.matmul(PS[:, i, P * h:P * h + P], KT[r:r + GLA_C, o:o + P],
                                           V[r:r + GLA_C, n // 2, P * h:P * h + P], start=True, stop=True)
                        mm.then_inc(st_full, 1)
                    pe.wait_ge(sco_out, zz * 2 + 2)
                    pe.wait_ge(st_out, zz + 1)
                    for b in range(2):
                        for h in (2 * b, 2 * b + 1):
                            for n in range(4):
                                o = T1 * h + GLA_C * n
                                dst = PS[:, 6 + b, T1 * (h % 2) + GLA_C * n:T1 * (h % 2) + GLA_C * n + GLA_C]
                                pairs = [(V[:, n // 2, P * h:P * h + P], SCO[:, o:o + GLA_C])]
                                i = n - 1 if z == 0 else 2 - n
                                if i >= 0:
                                    pairs.append((ST[i][:, P * h:P * h + P], QE[:, o:o + GLA_C]))
                                mm = chain(dst, pairs)
                        mm.then_inc(og_full, 1)
                pe.wait_ge(gsq, lay + 1)
                for b in range(2):
                    for h in (2 * b, 2 * b + 1):
                        mm = pe.matmul(PS[:, 4 + b, T1 * (h % 2):T1 * (h % 2) + T1], ONES[:, :],
                                       W[:, T1 * h:T1 * h + T1], start=True, stop=True)
                    mm.then_inc(gst_full, 1)

                pe.wait_ge(gla_done, lay + 2)
                linear(L1["gates"], lay, before, rhs, KD, 512, T1)
                L1["gates"].wait_all_out(pe, lay)
                for j, ys in enumerate((U, Q, YP)):
                    linear(L1["branch"], lay, before, lambda kk, ys=ys: ys[:, kk, :], 4, D, T1, us=(j,))
                L1["branch"].wait_all_out(pe, lay)
                linear(L1["w_out"], lay, before, lambda kk: MG[:, kk, :], KD, 256, T1)
                L1["w_out"].wait_all_out(pe, lay)
                norm_sums(lay * 4 + 1, SQ1, T1)

                norm_sums(lay * 4 + 2, SQ1, T1)
                pe.wait_ge(h_ready, lay * 16 + 16)
                linear(L1["up"], lay, before, rhs, KD, 512, T1)
                with pe.Fori(0, 2) as i:
                    L1["up"].wait_all_out(pe, lay)
                    linear(L1["down"], lay, before, lambda kk: FT[:, kk, :], NFF, P, T1, i4=i * 4, us=range(4))
                L1["down"].wait_all_out(pe, lay)
                norm_sums(lay * 4 + 3, SQ1, T1)

            nn = 4 * DEPTH1
            hh = 16 * DEPTH1
            pe.wait_ge(silu_c, 1)
            for l in range(DEPTH2):
                before = DEPTH1 * PER1 + l * PER2
                T = T2 if l < DEPTH2 - 1 else T1
                rhs = lambda kk, T=T: H[:, kk, 0:T]
                rhs2 = lambda kk: H[:, kk, 0:T2]
                if l:
                    L2["mlp_down"].wait_all_out(pe, l - 1)
                with pe.Fori(0, 3) as i:
                    pe.wait_ge(mod_psum, l * 3 + i + 1)
                    for u in range(4):
                        pe.wait_ge(s_slab[u], before * 4 + i * 16 + 16)
                        for cc in range(4):
                            mm = chain(PS[:, 5, 8 * u + 2 * cc:8 * u + 2 * cc + 2],
                                       [(slab(u, KD, 512)[:, kk, P * cc:P * cc + P], SC[:, kk, :]) for kk in range(KD)])
                        mm.then_inc(slab_done, 1)
                norm_sums(nn, SQ2, T2)
                nn += 1
                hh += 8
                pe.wait_ge(h_shift, (2 * l + 1) * 8)
                if l % 3 == 0:
                    a = l // 3
                    for u in range(4):
                        Tq = T if u < 2 else T2
                        linear(L2["qkv"], a, before, (rhs if u < 2 else rhs2), KD, 512, Tq, us=(u,))
                    for u in (4, 5):
                        for tt in range(4):
                            product(L2["qkv"], a, before, 0, u, tt, bank(L2["qkv"], tt),
                                    [(H[:, kk, P * tt:P * tt + P], slab(12 + u, KD, 512)[:, kk, :]) for kk in range(KD)])
                    L2["qkv"].wait_all_out(pe, a)

                    units = [(h, t) for h in range(HEADS2) for t in tiles(a)]
                    LAG = 2

                    def scores(n):
                        h, t = units[n]
                        g = unit0(a) + n
                        r = HD * (h % 2)
                        dst = PS[:, n % 3]
                        if n >= 3:
                            pe.wait_ge(p_exp, g - 2)
                        q = QT[r:r + HD, h // 2, P * t:P * t + P]
                        if t < 2:
                            if t == 0:
                                pe.wait_ge(bias_ready, a * HEADS2 + h + 1)
                            pe.matmul(dst[:, 0:SEQ], flip, BI[h % 2][:, t].rearrange("p r q -> p (r q)"),
                                      start=True, stop=False)
                            pe.matmul(dst[:, 0:SEQ], q, KT2[r:r + HD, h // 2, 0:SEQ], start=False, stop=True)
                            pe.matmul(dst[:, SEQ:T2], q, KT2[r:r + HD, h // 2, SEQ:T2],
                                      start=True, stop=True).then_inc(sc_full, 1)
                        else:
                            pe.matmul(dst[:, SEQ:T2], q, KT2[r:r + HD, h // 2, SEQ:T2],
                                      start=True, stop=True).then_inc(sc_full, 1)

                    def turn(n):
                        h, t = units[n]
                        g = unit0(a) + n
                        pe.wait_ge(p_norm, g + 1)
                        if n >= 2:
                            pe.wait_ge(pt_out, g - 1)
                        for j in (range(4) if t < 2 else (2, 3)):
                            tr = pe.transpose(PS[:, 3 + n % 2, P * j:P * j + P], PB[n % 2][:, P * j:P * j + P], ident)
                        tr.then_inc(pt_full, 1)

                    def values(n):
                        h, t = units[n]
                        g = unit0(a) + n
                        r = HD * (h % 2)
                        pe.wait_ge(pt_out, g + 1)
                        if t == 0 and h % 2 == 0 and h >= 4:
                            pe.wait_ge(o_out, a * 8 + h // 2 - 1)
                        mm = chain(PS[r:r + HD, 5 + (h // 2) % 2, P * t:P * t + P],
                                   [(VT[:, j, HD * h:HD * h + HD], PT[n % 2][:, j, :])
                                    for j in (range(4) if t < 2 else (2, 3))])
                        if h % 2 and t == tiles(a)[-1]:
                            mm.then_inc(o_full, 1)

                    N = len(units)
                    for n in range(N + 2):
                        if n < N:
                            scores(n)
                        if 1 <= n <= N:
                            turn(n - 1)
                        if n >= 2:
                            values(n - 2)
                    pe.wait_ge(o_out, a * 8 + 8)
                    linear(L2["wo"], a, before, lambda kk, T=T: OT[:, kk, 0:T], KD, 512, T)
                elif l % 3 == 1:
                    linear(L2["cv1"], 0, before, rhs, KD, 512, T2)
                    pe.wait_ge(cv_dw, 1)
                    chain(PS[:, 7, :], [(ONES[:, :], CV[:, kk, :]) for kk in range(KD)]).then_inc(mu_full, 1)
                    pe.wait_ge(cv_sq, 1)
                    chain(PS[:, 7, :], [(ONES[:, :], UA[:, kk, :]) for kk in range(KD)]).then_inc(cv_stat, 1)
                    pe.wait_ge(cv_act, 8)
                    linear(L2["cv2"], 0, before, lambda kk: CV[:, kk, :], KD, 256, T2)
                else:
                    linear(L2["sc1"], 0, before, rhs, KD, 512, T2)
                    pe.wait_ge(sc_bg, 8)
                    linear(L2["sc2"], 0, before, lambda kk: BG[:, kk, :], KD, 512, T2)

                norm_sums(nn, SQ2, T)
                nn += 1
                pe.wait_ge(h_shift, (2 * l + 2) * 8)
                L = L2["mlp_up"]
                with pe.Fori(0, 2) as i:
                    linear(L, l, before, rhs, KD, 512, T, i4=i * 4, us=range(4))
                L = L2["mlp_down"]
                pe.wait_ge(hid2, 32 * (l + 1))
                with pe.Fori(0, 2) as i:
                    linear(L, l, before, lambda kk, T=T: HID[:, kk, 0:T], NF2, P, T, i4=i * 4, us=range(4))
            norm_sums(nn, SQ2, T1)


        def col1(name, j=0):
            return PRC[:, ROW1[name] + j:ROW1[name] + j + 1]

        def col2(name, j=0):
            return PR2[:, ROW2[name] + j:ROW2[name] + j + 1]

        @blk.scalar
        def _(act):
            A = nc.scalar.activation
            step = Links(act, act_step)

            def squares(dst, src, T):
                for half in range(2):
                    ks = slice(4 * half, 4 * half + 4)
                    A(dst[:, ks, 0:T], src[:, ks, 0:T], ACT.Square).then_inc(sq_ready, 1)

            def root(n, T, dst):
                act.wait_ge(stat_full, n + 1)
                A(dst[:, 0:T], PS[:, 7, 0:T], ACT.Sqrt, scale=1.0 / D, bias=epsc[:, :]).then_inc(root_ready, 1)

            def take(L, uses, before, events, put, i4=0):
                for e in events:
                    finished(act, L, uses, before, i4, e // L.per, e % L.per)
                    put(e, bank(L, e)).then_inc(L.read(e), 1)

            act.wait_ge(ones_set, 3)
            act.wait_ge(tab_out, 1)
            with act.Fori(0, DEPTH1) as lay:
                before = lay * PER1
                step.base, step.n = lay * ACT_LINKS, 0
                for j in range(2):
                    act.wait_ge(sin_arg, lay * 2 + j + 1)
                    A(H1, FARG, ACT.Sin).then_inc(sin_out, 1)
                for j, dst in enumerate((KA, KB)):
                    for f in range(2):
                        act.wait_ge(kern_full, lay * 4 + 2 * j + f + 1)
                        A(dst[:, 2 * f:2 * f + 2, :], v3(PS[:, 4 + 2 * j + f], 2), ACT.Copy).then_inc(kern_out, 1)
                act.wait_ge(x_new, lay * 2 + 1)
                squares(SQ1, X, T1)
                root(lay * 4, T1, SCR)

                def conv_in(raw, dst, wname, bname, n, freed, count):
                    def put(e, ps):
                        act.wait_ge(freed, lay * count + e + 1)
                        A(raw[:, e % 4, :], ps[:, 0:T1], ACT.Identity)
                        return A(dst[:, e, :], ps[:, 0:T1], ACT.Identity, scale=col1(wname, n + e), bias=col1(bname, e))
                    return put

                take(L1["u"], lay, before, range(12), conv_in(RAW, U, "hy_conv_w", "hy_conv_b", 12, conv_u, 12))
                take(L1["q"], lay, before, range(4),
                     lambda e, ps: A(Q[:, e, :], ps[:, 0:T1], ACT.Copy, scale=float(P) ** -0.5))
                take(L1["k"], lay, before, range(4), lambda e, ps: A(K[:, e, :], ps[:, 0:T1], ACT.Copy))
                take(L1["g"], lay, before, range(4), lambda e, ps: A(G[:, e, :], ps[:, 0:T1], ACT.Silu))
                act.wait_ge(lr_full, lay + 1)
                A(LR, PS[0:2 * RANK, 6, 0:T1], ACT.Copy).then_inc(lr_out, 1)
                for g in range(4):
                    act.wait_ge(pd_full, lay * 4 + g + 1)
                    A(DP[:, g, :], PS[:, g, 0:T1], ACT.Copy).then_inc(pd_out, 1)
                for j in range(4):
                    act.wait_ge(zf_full, lay * 4 + j + 1)
                    A(W[:, 2048 + 512 * j:2560 + 512 * j], PS[:, 4 + j], ACT.Copy).then_inc(zf_out, 1)
                for z in range(2):
                    zz = lay * 2 + z
                    act.wait_ge(gk_out, zz + 1)
                    step(A(B1, X1, ACT.Abs))
                    step(A(B1, B1, ACT.Exp, scale=-1.0))
                    A(B1, B1, ACT.Ln, bias=1.0).then_inc(ls_ready, 1)
                    act.wait_ge(cum_ready, zz + 1)
                    A(E1, B1, ACT.Exp)
                    A(KE, B1, ACT.Exp, scale=-1.0).then_inc(exp_ready, 1)
                    for b in range(2):
                        act.wait_ge(kt_full, zz * 2 + b + 1)
                        A(KT[:, 512 * b:512 * b + 512], PS[:, 6 + b], ACT.Copy).then_inc(kt_out, 1)
                act.wait_ge(og_out, lay * 4 + 4)
                A(W[:, 0:1024], OG, ACT.Square).then_inc(gsq, 1)
                for b in range(2):
                    act.wait_ge(gst_full, lay * 2 + b + 1)
                    A(W[:, 1024 + 512 * b:1536 + 512 * b], PS[:, 4 + b], ACT.Sqrt, scale=1.0 / P,
                      bias=epsc[:, :]).then_inc(groot, 1)
                take(L1["gates"], lay, before, range(24), lambda e, ps: A(GT[:, e, :], ps[:, 0:T1], ACT.Sigmoid))
                take(L1["w_out"], lay, before, range(8), lambda e, ps: A(Y1[:, e, :], ps[:, 0:T1], ACT.Copy))
                L1["w_out"].wait_all_out(act, lay)
                squares(SQ1, Y1, T1)
                root(lay * 4 + 1, T1, SCR)
                act.wait_ge(x_new, lay * 2 + 2)
                squares(SQ1, X, T1)
                root(lay * 4 + 2, T1, SCR)
                take(L1["up"], lay, before, range(NFF), conv_in(FRAW, FT, "ffn_conv_w", "ffn_conv_b", NFF, conv_f, NFF))
                for m in range(NFF):
                    act.wait_ge(conv_f, lay * NFF + CREDIT + m + 1)
                    A(FT[:, m, :], FT[:, m, :], ACT.Gelu).then_inc(gelu_out, 1)
                with act.Fori(0, 2) as i:
                    take(L1["down"], lay, before, range(4),
                         lambda e, ps: A(Y2[:, bass.ds(i * 4 + e, 1), :], ps[:, 0:T1].rearrange("p (o t) -> p o t", o=1),
                                         ACT.Copy), i4=i * 4)
                L1["down"].wait_all_out(act, lay)
                squares(SQ1, Y2, T1)
                root(lay * 4 + 3, T1, SCR)
                assert step.n == ACT_LINKS, step.n
            step.base, step.n = 0, ACT_LINKS * DEPTH1

            for j, name in enumerate(("c_2", "c_ctx_2")):
                r = ROW2[name]
                last = A(SC[:, :, j], PR2[:, r:r + KD], ACT.Silu)
            last.then_inc(silu_c, 1)
            nn = 4 * DEPTH1
            norms = 0

            def shift(l, j, T):
                act.wait_ge(mod_psum, 3 * (l + 1) + 1)
                for k in range(KD):
                    act.wait_ge(h_ready, 8 * (2 * DEPTH1 + norms) + k + 1)
                    for s in range(T // T1):
                        hs = H[:, k, T1 * s:T1 * s + T1]
                        last = A(hs, hs, ACT.Identity, bias=MOD[:, KD * j + k, s:s + 1])
                    last.then_inc(h_shift, 1)

            act.wait_ge(s_ctx, 16)
            for l in range(DEPTH2):
                before = DEPTH1 * PER1 + l * PER2
                T = T2 if l < DEPTH2 - 1 else T1
                act.wait_ge(x_new, 1 + 2 * DEPTH1 + 2 * l)
                squares(SQ2, X, T2)
                root(nn, T2, RT2)
                nn += 1
                shift(l, 0, T2)
                norms += 1
                if l % 3 == 0:
                    a = l // 3
                    L = L2["qkv"]
                    take(L, a, before, range(8),
                         lambda e, ps: A(QT[:, e, 0:T], ps[:, 0:T], ACT.Copy, scale=float(HD) ** -0.5))
                    take(L, a, before, range(8, 16), lambda e, ps: A(KT2[:, e - 8, :], ps, ACT.Copy))
                    units = [(h, t) for h in range(HEADS2) for t in tiles(a)]
                    for n in range(len(units) + 1):
                        if n < len(units):
                            g = unit0(a) + n
                            lo = 0 if units[n][1] < 2 else SEQ
                            act.wait_ge(max_ready, g + 1)
                            if n >= 2:
                                act.wait_ge(pt_full, g - 1)
                            A(PB[n % 2][:, lo:T2], PS[:, n % 3, lo:T2], ACT.Exp, bias=MX[:, n, 0:1],
                              accum_out=MX[:, n, 1:2]).then_inc(p_exp, 1)
                        if n >= 1:
                            g = unit0(a) + n - 1
                            lo = 0 if units[n - 1][1] < 2 else 2
                            act.wait_ge(pt_full, g + 1)
                            A(PT[(n - 1) % 2][:, lo:4, :], v3(PS[:, 3 + (n - 1) % 2], 4)[:, lo:4, :],
                              ACT.Copy).then_inc(pt_out, 1)
                elif l % 3 == 1:
                    L = L2["cv1"]
                    take(L, 0, before, range(8),
                         lambda e, ps: A(UA[:, e, :], ps, ACT.Identity, bias=col2("cv_b1_2", e)))
                    take(L, 0, before, range(8, 16),
                         lambda e, ps: A(CV[:, e - 8, :], ps, ACT.Sigmoid, bias=col2("cv_b1_2", e)))
                    act.wait_ge(mu_full, 1)
                    A(MU, PS[:, 7, :], ACT.Copy, scale=1.0 / D).then_inc(mu_out, 1)
                    act.wait_ge(xc_ready, 1)
                    A(UA[:, :, :], XC[:, :, :], ACT.Square).then_inc(cv_sq, 1)
                    act.wait_ge(cv_stat, 1)
                    A(RT2, PS[:, 7, :], ACT.Sqrt, scale=1.0 / D, bias=epsc[:, :]).then_inc(cv_root, 1)
                    for k in range(KD):
                        act.wait_ge(cv_norm, k + 1)
                        A(CV[:, k, :], XC[:, k, :], ACT.Silu, bias=col2("cv_ln_b_2", k)).then_inc(cv_act, 1)
                else:
                    L = L2["sc1"]
                    take(L, 0, before, range(8), lambda e, ps: A(BG[:, e, :], ps, ACT.Copy))
                    take(L, 0, before, range(8, 16), lambda e, ps: A(CG[:, e - 8, :], ps, ACT.Copy))
                act.wait_ge(x_new, 2 + 2 * DEPTH1 + 2 * l)
                squares(SQ2, X, T)
                root(nn, T, RT2)
                nn += 1
                shift(l, 3, T)
                norms += 1
                with act.Fori(0, 2) as i:
                    take(L2["mlp_up"], l, before, range(16),
                         lambda e, ps: A(HID[:, bass.ds(i * 16 + e, 1), 0:T], ps[:, 0:T].rearrange("p (o t) -> p o t", o=1),
                                         ACT.Relu), i4=i * 4)
            act.wait_ge(x_new, 1 + 2 * DEPTH1 + 2 * DEPTH2)
            squares(SQ2, X, T1)
            root(nn, T1, RT2)

        @blk.vector
        def _(dve):
            v = nc.vector
            step = Links(dve, dve_step)

            def take(L, uses, before, events, put, i4=0):
                for e in events:
                    finished(dve, L, uses, before, i4, e // L.per, e % L.per)
                    put(e, bank(L, e)).then_inc(L.read(e), 1)

            def conv3(dst, raw, w0, w2, done):
                n = dst.shape[-1]
                step(v.scalar_tensor_tensor(dst[..., 1:n], raw[..., 0:n - 1], w0, dst[..., 1:n], ALU.mult, ALU.add))
                last = v.scalar_tensor_tensor(dst[..., 0:n - 1], raw[..., 1:n], w2, dst[..., 0:n - 1],
                                              ALU.mult, ALU.add)
                if done is None:
                    step(last)
                else:
                    last.then_inc(done, 1)

            def rms_into_h(n, gain):
                dve.wait_ge(root_ready, n + 1)
                step(v.reciprocal(SCR[:, T1:T2], SCR[:, 0:T1]))
                for k in range(KD):
                    v.scalar_tensor_tensor(H[:, k, 0:T1], X[:, k, 0:T1], col1(gain, k), SCR[:, T1:T2],
                                           ALU.mult, ALU.mult).then_inc(h_ready, 1)

            def add_normed(n, gain, Y):
                dve.wait_ge(root_ready, n + 1)
                step(v.reciprocal(SCR[:, T1:T2], SCR[:, 0:T1]))
                for k in range(KD):
                    last = v.scalar_tensor_tensor(Y[:, k, :], Y[:, k, :], col1(gain, k), SCR[:, T1:T2],
                                                  ALU.mult, ALU.mult)
                step(last)
                v.tensor_tensor(X[:, :, 0:T1], X[:, :, 0:T1], Y, ALU.add).then_inc(x_new, 1)

            dve.wait_ge(tab_full, 1)
            v.tensor_copy(PR1[:, :], PS[:, 0])
            v.tensor_copy(PR2[:, 0:512], PS[:, 1])
            v.tensor_copy(PR2[:, 512:640], PS[:, 2, 0:P]).then_inc(tab_out, 1)
            dve.wait_ge(tab_out, 1)
            dve.wait_ge(s_x, 16)
            dve.wait_ge(s_con, 16)
            v.memset(GM[:, :, :], 0.0).then_inc(x_new, 1)
            with dve.Fori(0, DEPTH1) as lay:
                before = lay * PER1
                step.base, step.n = 3 * 0 + lay * DVE_LINKS, 0
                v.tensor_copy(PRC[:, :], PR1[:, bass.ds(lay * (NT1 * P), NT1 * P)]).then_inc(prm_ready, 1)
                dve.wait_ge(prm_ready, lay + 1)
                for j, (b, f) in enumerate((("hy_filt_b1", "hy_filt_freq1"), ("hy_filt_b2", "hy_filt_freq2"))):
                    dve.wait_ge(filt_full, lay * 6 + j + 1)
                    step(v.tensor_scalar(FARG, PS[0:ORDER, j, 0:SEQ], col1(b)[0:ORDER], col1(f)[0:ORDER], ALU.add, ALU.mult))
                    step(v.tensor_scalar(FK, FARG, 1.0 / (2.0 * np.pi), MAGIC, ALU.mult, ALU.add))
                    step(v.tensor_scalar(FK, FK, -MAGIC, None, ALU.add))
                    for part in (TWO_PI_HI, TWO_PI_MID, TWO_PI_LO):
                        step(v.scalar_tensor_tensor(FARG, FK, -part, FARG, ALU.mult, ALU.add))
                    v.tensor_scalar(FARG, FARG, 3.1415925, -3.1415925, ALU.min, ALU.max).then_inc(sin_arg, 1)
                dve.wait_ge(filt_full, lay * 6 + 6)
                for tt in range(2):
                    v.tensor_tensor(HF[:, tt, :], PS[:, tt], DECAY[:, tt, :], ALU.mult)
                    last = v.tensor_tensor(HB[:, tt, :], PS[:, 2 + tt], DECAY[:, tt, :], ALU.mult)
                step(last)
                step(v.memset(HB[0:1, 0, :], 0.0))
                v.tensor_tensor(FA, HF, HB, ALU.add)
                v.tensor_tensor(FB, HF, HB, ALU.subtract).then_inc(filt_out, 1)

                rms_into_h(lay * 4, "norm_mix_pre")
                for e in range(12):
                    dve.wait_ge(L1["u"].out, lay * 12 + CREDIT + e + 1)
                    conv3(U[:, e, :], RAW[:, e % 4, :], col1("hy_conv_w", e), col1("hy_conv_w", 24 + e), conv_u)
                dve.wait_ge(conv_u, lay * 12 + CREDIT + 12)
                v.tensor_tensor(ZV, U[:, 4:8, :], U[:, 8:12, :], ALU.mult).then_inc(zv_ready, 1)
                take(L1["v"], lay, before, range(2), lambda e, ps: v.tensor_copy(V[:, e, :], ps))
                take(L1["pool"], lay, before, range(2), lambda e, ps: v.tensor_copy(UP[:, e, :], ps))
                for g in range(4):
                    dve.wait_ge(pw_full, lay * 4 + g + 1)
                    v.tensor_scalar(YP[:, g, :], PS[:, 4 + g, 0:T1], col1("pool_scale", g), None,
                                    ALU.mult).then_inc(pw_out, 1)
                for ss in range(2):
                    dve.wait_ge(zt_full, lay * 2 + ss + 1)
                    v.tensor_copy(ZT[:, ss, :], PS[:, ss]).then_inc(zt_out, 1)
                dve.wait_ge(kern_out, lay * 4 + 4)
                dve.wait_ge(zf_out, lay * 4 + 4)
                v.tensor_tensor(PP, ZC, KA, ALU.mult)
                step(v.tensor_tensor(TMP, ZS, KB, ALU.mult))
                v.tensor_tensor(RR, ZC, KB, ALU.mult)
                step(v.tensor_tensor(PP, PP, TMP, ALU.subtract))
                step(v.tensor_tensor(TMP, ZS, KA, ALU.mult))
                v.tensor_tensor(RR, RR, TMP, ALU.add).then_inc(prod_ready, 1)
                dve.wait_ge(prod_ready, lay + 1)
                for j in range(4):
                    dve.wait_ge(hy_full, lay * 4 + j + 1)
                    step(v.scalar_tensor_tensor(TMP[:, j, :], ZV[:, j, :], col1("hy_bias", j), PS[:, j, 0:T1],
                                                ALU.mult, ALU.add))
                    v.tensor_tensor(U[:, j, :], U[:, j, :], TMP[:, j, :], ALU.mult).then_inc(hy_out, 1)
                for z in range(2):
                    zz = lay * 2 + z
                    for j in range(4):
                        if j % 2 == 0:
                            dve.wait_ge(gk_full, zz * 2 + j // 2 + 1)
                        o = T1 * (j % 2)
                        last = v.tensor_scalar(X1[:, T1 * j:T1 * j + T1], PS[:, 4 + j // 2, o:o + T1],
                                               col1("gla_gate_b", 4 * z + j), None, ALU.add)
                    last.then_inc(gk_out, 1)
                    dve.wait_ge(ls_ready, zz + 1)
                    step(v.scalar_tensor_tensor(X1, X1, 0.0, B1, ALU.min, ALU.subtract))
                    step(v.tensor_scalar(X1, X1, 1.0 / 16.0, -1.0, ALU.mult, ALU.max))
                    for j in range(4):
                        la, cum = X1[:, T1 * j:T1 * j + T1], B1[:, T1 * j:T1 * j + T1]
                        if z == 0:
                            last = v.tensor_tensor_scan(out=cum, data0=c("scan_f"), data1=la, initial=0.0,
                                                        op0=ALU.mult, op1=ALU.add)
                        else:
                            last = v.tensor_tensor_scan(out=cum[:, ::-1], data0=c("scan_b")[:, ::-1], data1=la[:, ::-1],
                                                        initial=0.0, op0=ALU.mult, op1=ALU.add)
                    last.then_inc(cum_ready, 1)
                    dve.wait_ge(exp_ready, zz + 1)
                    v.tensor_tensor(QE, BIG[:, 3072:4096], E1, ALU.mult)
                    step(v.tensor_tensor(KE, BIG[:, 4096:5120], KE, ALU.mult))
                    edge = GLA_C - 1 if z == 0 else 0
                    chunks = lambda ap: ap.rearrange("p (n t) -> p n t", t=GLA_C)
                    v.tensor_tensor(chunks(X1), chunks(KE), chunks(E1)[:, :, edge:edge + 1].to_broadcast([P, 16, GLA_C]),
                                    ALU.mult).then_inc(qk_ready, 1)
                    mask = c("mask_f" if z == 0 else "mask_b").rearrange("p (o t) -> p o t", o=1)
                    for b in range(2):
                        dve.wait_ge(sco_full, zz * 2 + b + 1)
                        v.tensor_tensor(v3(SCO[:, 512 * b:512 * b + 512], 4), v3(PS[:, 4 + b], 4),
                                        mask.to_broadcast([P, 4, P]), ALU.mult).then_inc(sco_out, 1)
                    for i in range(3):
                        dve.wait_ge(st_full, zz * 3 + i + 1)
                        if i == 0:
                            step(v.tensor_copy(ST[0], PS[:, 0]))
                            continue
                        n = i if z == 0 else 3 - i
                        for h in range(HEADS1):
                            hs = slice(P * h, P * h + P)
                            o = T1 * h + GLA_C * n + edge
                            last = v.scalar_tensor_tensor(ST[i][:, hs], ST[i - 1][:, hs], E1[:, o:o + 1],
                                                          PS[:, i, hs], ALU.mult, ALU.add)
                        if i == 1:
                            step(last)
                        else:
                            last.then_inc(st_out, 1)
                    for b in range(2):
                        dve.wait_ge(og_full, zz * 2 + b + 1)
                        og = OG[:, 512 * b:512 * b + 512]
                        if z == 0:
                            v.tensor_copy(og, PS[:, 6 + b]).then_inc(og_out, 1)
                        else:
                            v.tensor_tensor(og, og, PS[:, 6 + b], ALU.add).then_inc(og_out, 1)
                dve.wait_ge(groot, lay * 2 + 2)
                step(v.reciprocal(B1, B1))
                yg = BIG[:, 3072:4096]
                step(v.scalar_tensor_tensor(yg, OG, col1("gla_norm"), B1, ALU.mult, ALU.mult))
                v.tensor_tensor(yg, yg, BIG[:, 5120:6144], ALU.mult).then_inc(gla_done, 1)

                L1["gates"].wait_all_out(dve, lay)

                def merge(e, ps):
                    if e < 8:
                        return v.tensor_tensor(MG[:, e, :], GT[:, e, :], ps[:, 0:T1], ALU.mult)
                    step(v.tensor_tensor(GT[:, e, :], GT[:, e, :], ps[:, 0:T1], ALU.mult))
                    return v.tensor_tensor(MG[:, e % 8, :], MG[:, e % 8, :], GT[:, e, :], ALU.add)

                take(L1["branch"], lay, before, range(24), merge)
                add_normed(lay * 4 + 1, "norm_mix_post", Y1)
                dve.wait_ge(x_new, lay * 2 + 2)
                rms_into_h(lay * 4 + 2, "norm_ffn_pre")
                for m in range(NFF):
                    dve.wait_ge(L1["up"].out, lay * NFF + CREDIT + m + 1)
                    conv3(FT[:, m, :], FRAW[:, m % 4, :], col1("ffn_conv_w", m), col1("ffn_conv_w", 2 * NFF + m), conv_f)

                def times_gelu(e, ps):
                    dve.wait_ge(gelu_out, lay * NFF + e - NFF + 1)
                    return v.tensor_tensor(FT[:, e - NFF, :], FT[:, e - NFF, :], ps[:, 0:T1], ALU.mult)

                take(L1["up"], lay, before, range(NFF, 2 * NFF), times_gelu)
                add_normed(lay * 4 + 3, "norm_ffn_post", Y2)
                dve.wait_ge(x_new, lay * 2 + 3)
                assert step.n == DVE_LINKS, step.n
            step.base, step.n = 0, DVE_LINKS * DEPTH1

            nn = 4 * DEPTH1

            def scaled_into_h(n, l, gain, j, T):
                grow = PR2[:, ROW2[gain] + KD * l:ROW2[gain] + KD * l + KD].rearrange("p (k o) -> p k o", o=1)
                step(v.scalar_tensor_tensor(GM[:, :, :], MOD[:, KD * (j + 1):KD * (j + 2), :], 1.0,
                                            grow.to_broadcast([P, KD, 2]), ALU.add, ALU.mult))
                dve.wait_ge(root_ready, n + 1)
                step(v.reciprocal(RS2[:, 0:T], RT2[:, 0:T]))
                for k in range(KD):
                    for s in range(T // T1):
                        ts = slice(T1 * s, T1 * s + T1)
                        last = v.scalar_tensor_tensor(H[:, k, ts], X[:, k, ts], GM[:, k, s:s + 1], RS2[:, ts],
                                                      ALU.mult, ALU.mult)
                    last.then_inc(h_ready, 1)

            def add_gated(j, k, T, src):
                for s in range(T // T1):
                    ts = slice(T1 * s, T1 * s + T1)
                    last = v.scalar_tensor_tensor(X[:, k, ts], src[:, ts], MOD[:, KD * j + k, s:s + 1], X[:, k, ts],
                                                  ALU.mult, ALU.add)
                return last

            for l in range(DEPTH2):
                before = DEPTH1 * PER1 + l * PER2
                T = T2 if l < DEPTH2 - 1 else T1
                with dve.Fori(0, 3) as i:
                    dve.wait_ge(slab_done, before + i * 4 + 4 + CREDIT)
                    v.tensor_tensor(MOD[:, bass.ds(i * 16, 16), :], PS[:, 5, 0:32].rearrange("p (k o) -> p k o", o=2),
                                    PR2[:, bass.ds(i * 16 + ROW2["mod_b_2"] + 48 * l, 16)]
                                    .rearrange("p (k o) -> p k o", o=1).to_broadcast([P, 16, 2]), ALU.add
                                    ).then_inc(mod_psum, 1)
                dve.wait_ge(mod_psum, 3 * (l + 1) + 1)
                if l == 0:
                    dve.wait_ge(s_ctx, 16)
                scaled_into_h(nn, l, "norm1_g_2", 0, T2)
                nn += 1
                if l % 3 == 0:
                    a = l // 3
                    take(L2["qkv"], a, before, range(16, 24),
                         lambda e, ps: v.tensor_copy(VT[:, e % 4, 512 * (e // 4 - 4):512 * (e // 4 - 3)], ps))
                    units = [(h, t) for h in range(HEADS2) for t in tiles(a)]
                    N = len(units)
                    per_pair = 2 * len(tiles(a))
                    for n in range(N + 3):
                        if n < N:
                            g = unit0(a) + n
                            lo = 0 if units[n][1] < 2 else SEQ
                            dve.wait_ge(sc_full, g + 1)
                            v.tensor_reduce(MX[:, n, 0:1], PS[:, n % 3, lo:T2], AX.X, ALU.max,
                                            negate=True).then_inc(max_ready, 1)
                        if 1 <= n <= N:
                            g = unit0(a) + n - 1
                            lo = 0 if units[n - 1][1] < 2 else SEQ
                            pb = PB[(n - 1) % 2][:, lo:T2]
                            dve.wait_ge(p_exp, g + 1)
                            step(v.reciprocal(MX[:, n - 1, 1:2], MX[:, n - 1, 1:2]))
                            v.tensor_scalar(pb, pb, MX[:, n - 1, 1:2], None, ALU.mult).then_inc(p_norm, 1)
                        if n >= 3 and (n - 2) % per_pair == 0:
                            k = (n - 2) // per_pair - 1
                            dve.wait_ge(o_full, a * 8 + k + 1)
                            v.tensor_copy(OT[:, k, 0:T], PS[:, 5 + k % 2, 0:T]).then_inc(o_out, 1)
                    assert (N + 2 - 2) % per_pair == 0
                    take(L2["wo"], a, before, range(8), lambda e, ps: add_gated(2, e, T, ps))
                elif l % 3 == 1:
                    v.memset(UPAD[:, :, :, 0:15], 0.0)
                    v.memset(UPAD[:, :, :, 15 + SEQ:286], 0.0)
                    for k in range(KD):
                        dve.wait_ge(L2["cv1"].out, CREDIT + 8 + k + 1)
                        last = v.tensor_tensor(UPAD[:, k, :, 15:15 + SEQ], v3(UA[:, k, :], 2), v3(CV[:, k, :], 2), ALU.mult)
                    step(last)
                    for k in range(KD):
                        cvk = v3(CV[:, k, :], 2)
                        for tap in range(TAPS):
                            win = UPAD[:, k, :, tap:tap + SEQ]
                            wcol = col2("cv_dw_2", KD * tap + k)
                            if tap == 0:
                                step(v.tensor_scalar(cvk, win, wcol, col2("cv_dwb_2", k), ALU.mult, ALU.add))
                            elif tap < TAPS - 1 or k < KD - 1:
                                step(v.scalar_tensor_tensor(cvk, win, wcol, cvk, ALU.mult, ALU.add))
                            else:
                                v.scalar_tensor_tensor(cvk, win, wcol, cvk, ALU.mult, ALU.add).then_inc(cv_dw, 1)
                    dve.wait_ge(mu_out, 1)
                    v.tensor_tensor(XC, CV, MU.rearrange("p (o t) -> p o t", o=1).to_broadcast([P, KD, T2]),
                                    ALU.subtract).then_inc(xc_ready, 1)
                    dve.wait_ge(cv_root, 1)
                    step(v.reciprocal(RS2, RT2))
                    for k in range(KD):
                        v.scalar_tensor_tensor(XC[:, k, :], XC[:, k, :], col2("cv_ln_g_2", k), RS2, ALU.mult,
                                               ALU.mult).then_inc(cv_norm, 1)

                    def add_conf(e, ps):
                        t = SM[:, 512 * (e % 4):512 * (e % 4) + 512]
                        step(v.tensor_scalar(t, ps, col2("cv_b2_2", e), None, ALU.add))
                        return add_gated(2, e, T2, t)

                    take(L2["cv2"], 0, before, range(8), add_conf)
                else:
                    def conv_in(e, ps):
                        m = e - 16
                        return v.tensor_tensor(SV[:, m, :], CG[:, m, :], ps, ALU.mult)

                    dve.wait_ge(L2["sc1"].out, CREDIT + 16)
                    for m in range(KD):
                        take(L2["sc1"], 0, before, (16 + m,), conv_in)
                        dve.wait_ge(L2["sc1"].out2, m + 1)
                        s, y = v3(SV[:, m, :], 2), v3(SY[:, m, :], 2)
                        step(v.tensor_scalar(y, s, col2("sc_conv_2", KD + m), None, ALU.mult))
                        conv3(y, s, col2("sc_conv_2", m), col2("sc_conv_2", 2 * KD + m), None)
                        v.tensor_tensor(BG[:, m, :], BG[:, m, :], SY[:, m, :], ALU.mult).then_inc(sc_bg, 1)
                    take(L2["sc2"], 0, before, range(8), lambda e, ps: add_gated(2, e, T2, ps))
                v.memset(GM[:, :, :], 0.0).then_inc(x_new, 1)
                dve.wait_ge(x_new, 2 + 2 * DEPTH1 + 2 * l)
                scaled_into_h(nn, l, "norm2_g_2", 3, T)
                nn += 1
                with dve.Fori(0, 2) as i:
                    for e in range(16):
                        dve.wait_ge(L2["mlp_up"].out, i * 16 + (l * 32 + CREDIT + e + 1))
                        hd = HID[:, bass.ds(i * 16 + e, 1), 0:T]
                        v.tensor_tensor(hd, hd, hd, ALU.mult).then_inc(hid2, 1)
                with dve.Fori(0, 2) as i:
                    for e in range(4):
                        L = L2["mlp_down"]
                        finished(dve, L, l, before, i * 4, e, 0)
                        dve.wait_ge(L.out, i * 4 + (l * 8 + e + CREDIT))
                        for s in range(T // T1):
                            xs = X[:, bass.ds(i * 4 + e, 1), T1 * s:T1 * s + T1]
                            last = v.tensor_tensor(TG[:, s, :].rearrange("p (o t) -> p o t", o=1),
                                                   PS[:, L.banks[e], T1 * s:T1 * s + T1].rearrange("p (o t) -> p o t", o=1),
                                                   MOD[:, bass.ds(i * 4 + e + 5 * KD, 1), s:s + 1].to_broadcast([P, 1, T1]),
                                                   ALU.mult)
                        last.then_inc(tg_ready, 1)
                        dve.wait_ge(tg_ready, i * 4 + (l * 8 + e + 1))
                        xs = X[:, bass.ds(i * 4 + e, 1), 0:T]
                        v.tensor_tensor(xs, xs, TG.rearrange("p s t -> p (s t)")[:, 0:T].rearrange("p (o t) -> p o t", o=1),
                                        ALU.add).then_inc(L.out, 1)
                v.memset(GM[:, :, :], 0.0).then_inc(x_new, 1)
                dve.wait_ge(x_new, 3 + 2 * DEPTH1 + 2 * l)
            dve.wait_ge(root_ready, nn + 1)
            step(v.reciprocal(RS2[:, 0:T1], RT2[:, 0:T1]))
            for k in range(KD):
                v.scalar_tensor_tensor(H[:, k, 0:T1], X[:, k, 0:T1], col2("final_g_2", k), RS2[:, 0:T1],
                                       ALU.mult, ALU.mult).then_inc(h_ready, 1)


def constants():
    C = np.zeros((P, NCON), np.float32)

    def put(name, a):
        lo, hi = CON[name]
        C[:a.shape[0], lo:hi] = a.reshape(a.shape[0], -1)

    i = np.arange(P)
    put("ident", np.eye(P))
    put("flip", np.eye(P)[::-1])
    q = GRID - 1 - i % GRID
    start = np.clip(q - WCOLS // 2, 0, GRID - WCOLS)[:, None]
    k = np.arange(GRID)[None]
    put("window", np.where((k >= start) & (k < start + WCOLS), 0.0, -1e30))
    same = i[:, None] // GLA_C == i[None] // GLA_C
    put("mask_f", (same & (i[:, None] <= i[None])).astype(float))
    put("mask_b", (same & (i[:, None] > i[None])).astype(float))
    t = np.arange(SEQ)
    put("scan_f", np.tile((t % GLA_C != 0).astype(float), (P, 1)))
    put("scan_b", np.tile((t % GLA_C != GLA_C - 1).astype(float), (P, 1)))
    bands = (EMB - 1) // 2
    tl = np.linspace(0.0, 1.0, SEQ, dtype=np.float32)[:, None]
    ang = (np.linspace(1e-4, bands - 1, bands, dtype=np.float32)[None]
           * (2.0 * np.pi * np.arange(SEQ, dtype=np.float32)[:, None] / SEQ).astype(np.float32))
    put("zT", np.concatenate([tl, np.cos(ang), -np.sin(ang)], axis=1).T)
    th = (2 * t[None] + 1) * t[:, None] * np.pi / (2 * SEQ)

    def tiled(m):
        return m.reshape(2, P, -1).transpose(1, 0, 2)

    put("cos", tiled(np.cos(th)))
    put("sin", tiled(np.sin(th)))
    put("icos", tiled(np.cos(th).T / SEQ))
    put("isin", tiled(np.sin(th).T / SEQ))
    lo, hi = np.log(1e-2) / 1.5, np.log(1e-2) / 0.3
    deltas = np.linspace(lo, hi, HY, dtype=np.float32)
    put("decay", tiled(np.exp(-tl * np.abs(deltas)[None])))
    band = np.zeros((SEQ, 4, SEQ))
    for g, wn in enumerate(WINDOWS):
        half = wn // 2
        for tt in range(SEQ):
            a, b = max(tt - half, 0), min(tt + half, SEQ)
            band[a:b, g, tt] = 1.0 / (b - a)
            band[tt, g, tt] -= 1.0
    put("band", band.reshape(2, P, 4, SEQ).transpose(1, 0, 2, 3))
    return C


def kernel(**inputs):
    import concourse.bacc as bacc
    from concourse.bass_utils import run_bass_kernel_spmd as run

    def table(names, rows_of, tables, layer=None):
        out = np.zeros((tables, P, P), np.float32)
        flat = out.reshape(tables * P, P)
        for name in names:
            a = np.asarray(inputs[name])
            a = a[layer] if layer is not None else a
            if a.shape[-1] < P:
                flat[rows_of[name], :a.shape[-1]] = a
            else:
                a = a.reshape(-1, P)
                flat[rows_of[name]:rows_of[name] + len(a)] = a
        return out

    arrays = {
        "xT": np.ascontiguousarray(np.asarray(inputs["x"])[0].T),
        "ctxT": np.ascontiguousarray(np.asarray(inputs["ctx_2"])[0].T),
        "consts": constants(),
        "params1": np.concatenate([table(ROW1, ROW1, NT1, l) for l in range(DEPTH1)]),
        "params2": table(ROW2, ROW2, NT2),
    }
    nc = bacc.Bacc("TRN2", target_bir_lowering=False, num_devices=1)
    big = ("w_in", "w_br_hyena", "w_br_gla", "w_br_pool", "w_out", "ffn_w_up", "ffn_w_down", "hy_filt_w1",
           "hy_filt_w2", "hy_filt_w3", "gla_gate_w2", "pool_w", "mod_w_2", "mlp_w1_2", "mlp_w2_2", "na_wqkv_2",
           "na_wo_2", "na_rpb_2", "cv_w1_2", "cv_w2_2", "sc_win_2", "sc_wout_2")
    for name in big:
        arrays[name] = np.ascontiguousarray(inputs[name])
    aps = {n: nc.dram_tensor(n, a.shape, mybir.dt.from_np(a.dtype), kind="ExternalInput").ap()
           for n, a in arrays.items()}
    out = nc.dram_tensor("out_0", (D, SEQ), F32, kind="ExternalOutput").ap()
    build(nc, aps["xT"], aps["ctxT"], aps["consts"], aps["params1"], aps["params2"], aps, out)
    r = run(nc, [arrays], core_ids=[0])
    return np.ascontiguousarray(r.results[0]["out_0"].T)[None]
```

```python
from contextlib import ExitStack

import numpy as np

import concourse.bass as bass
from concourse import mybir

ALU = mybir.AluOpType
ACT = mybir.ActivationFunctionType
AX = mybir.AxisListType
F32 = mybir.dt.float32
F32R = mybir.dt.float32r

P = 128
D = 1024
KD = D // P
SEQ = 256
T1 = SEQ
T2 = 2 * SEQ
EPS = 1e-6
CREDIT = 4

DEPTH1 = 2
HY = 512
EMB = 33
ORDER = 64
HEADS1 = 4
RANK = 16
GLA_C = 64
WINDOWS = (2, 4, 8, 16)
D_FF = 2816
NFF = D_FF // P
D_IN = 3 * HY + 4 * 512 + 2 * RANK + 512 + 3 * D

DEPTH2 = 4
HEADS2 = 16
HD = D // HEADS2
GRID = 64
ROWS = SEQ // GRID
WCOLS = 16
RPB_R, RPB_C = 15, 31
TAPS = 31
FF2 = 4 * D
NF2 = FF2 // P

C_U, C_Q, C_K, C_V, C_G = 0, 1536, 2048, 2560, 3072
C_LR = 3584
C_POOL = C_LR + 2 * RANK
C_GATE = C_POOL + 512

CON = {}
_at = 0
for _n, _w in (("ident", P), ("flip", P), ("window", GRID),
               ("mask_f", P), ("mask_b", P), ("scan_f", SEQ), ("scan_b", SEQ), ("zT", SEQ),
               ("cos", 2 * SEQ), ("sin", 2 * SEQ), ("icos", 2 * SEQ), ("isin", 2 * SEQ),
               ("decay", 2 * HY), ("band", 8 * SEQ)):
    CON[_n] = (_at, _at + _w)
    _at += _w
NCON = _at
CON2 = CON["window"][1]

ROW1 = {}
_at = 0
for _n, _w in (("norm_mix_pre", 8), ("norm_mix_post", 8), ("norm_ffn_pre", 8), ("norm_ffn_post", 8),
               ("hy_conv_w", 36), ("hy_conv_b", 12), ("hy_bias", 4), ("gla_gate_b", 8), ("gla_norm", 1),
               ("pool_scale", 4), ("hy_filt_b1", 1), ("hy_filt_freq1", 1), ("hy_filt_b2", 1),
               ("hy_filt_freq2", 1), ("ffn_conv_w", 66), ("ffn_conv_b", 22)):
    ROW1[_n] = _at
    _at += _w
ROW2 = {}
_at = 0
for _n, _w in (("mod_b_2", 192), ("norm1_g_2", 32), ("norm2_g_2", 32), ("cv_b1_2", 16), ("cv_dw_2", 248),
               ("cv_dwb_2", 8), ("cv_ln_g_2", 8), ("cv_ln_b_2", 8), ("cv_b2_2", 8), ("sc_conv_2", 24),
               ("final_g_2", 8), ("c_2", 8), ("c_ctx_2", 8)):
    ROW2[_n] = _at
    _at += _w
NT1, NT2 = 2, 5

SL1 = {"u": (2, 3), "q": (5, 1), "k": (6, 1), "v": (7, 1), "g": (8, 1), "pool": (9, 1), "gates": (16, 6),
       "branch": (22, 3), "w_out": (25, 4), "up": (31, 11), "down": (42, 8)}
MOD1 = (0, 1, 10, 11, 12, 13, 14, 15, 29, 30, 50, 51)
PER1 = 52
SL2 = {"qkv": (0, 6), "wo": (6, 2), "cv1": (0, 4), "cv2": (28, 4),
       "sc1": (0, 6), "sc2": (6, 2)}
MOD2 = tuple(range(4, 28))
SLABS2 = (8, 8 + len(MOD2), 8, 8)
BEFORE2 = [DEPTH1 * PER1 + sum(SLABS2[:l]) for l in range(DEPTH2)]

QUARTERS = FF2 // D
PROD_Q = 2 * KD
PROD_L = QUARTERS * PROD_Q
AHEAD = 3
SPLIT_CREDIT, HID_CREDIT, DOWN_CREDIT = 8, 2, 8
MODP = 12
ACT_LINKS, DVE_LINKS = 4, 89
MAGIC = 12582912.0
TWO_PI_HI, TWO_PI_MID, TWO_PI_LO = 6.28125, 0.0019350051879882812, 3.019916e-07


class Linear:

    def __init__(self, full, out, slab0, slabs, per, banks, split=None, out2=None):
        self.full, self.out, self.slab0, self.slabs, self.per, self.banks = full, out, slab0, slabs, per, banks
        self.events = slabs * per
        self.out2, self.first = out2, self.events if out2 is None else split

    def all_out(self, uses):
        return uses * self.first + self.first + CREDIT

    def wait_all_out(self, eng, uses):
        eng.wait_ge(self.out, self.all_out(uses))
        if self.out2 is not None:
            eng.wait_ge(self.out2, uses * (self.events - self.first) + self.events - self.first)

    def wait_bank(self, eng, uses, i4, e):
        if e < self.first + 4:
            eng.wait_ge(self.out, uses * self.first + i4 * self.per + e + 1)
        else:
            eng.wait_ge(self.out2, uses * (self.events - self.first) + e - self.first - 4 + 1)

    def read(self, e):
        return self.out if e < self.first else self.out2


class Links:

    def __init__(self, eng, sem):
        self.eng, self.sem, self.base, self.n = eng, sem, 0, 0

    def __call__(self, ins):
        self.mark(ins)
        self.wait()

    def mark(self, ins):
        ins.then_inc(self.sem, 1)
        self.n += 1

    def wait(self):
        self.eng.wait_ge(self.sem, self.base + self.n)


def build(nc, x, ctx_in, con, prm1, prm2, w, out):
    with ExitStack() as stack:
        place = {}

        def sb(name, shape):
            place[name] = (nc.sbuf_base + 31) // 32 * 32
            return stack.enter_context(nc.sbuf_tensor(name, shape, F32))

        def sem(name):
            return stack.enter_context(nc.semaphore(name))

        X = sb("X", [P, KD, T2])
        H = sb("H", [P, KD, T2])
        BIG = sb("BIG", [P, 16384])
        RING = sb("RING", [P, 4, 4096])
        CN = sb("CN", [P, NCON])
        SM = sb("SM", [P, 3200])
        PR1 = sb("PR1", [P, DEPTH1 * NT1 * P])
        PR2 = sb("PR2", [P, NT2 * P])
        PRC = sb("PRC", [P, NT1 * P])
        SCR = sb("SCR", [P, 512])
        ONES = sb("ONES", [P, P])
        MODS = sb("MODS", [P, DEPTH2 * 6 * KD, 2])
        GM = sb("GM", [P, KD, 2])
        epsc = sb("epsc", [P, 1])
        SC = sb("SC", [P, KD, 2])
        MROW1 = X[:, 0:2, T1:T2]
        MROW2 = SCR[:, :].rearrange("p (c t) -> p c t", c=2)
        PS = stack.enter_context(nc.psum_tensor("PS", [P, 8, 512], F32))

        def alias(name, host, at, shape):
            return nc.alloc_sbuf_tensor_at(name, shape, F32R, offset=place[host] + 4 * at)

        WRAW = RING[:, 0:2, :].rearrange("p a (b k n) -> p (a b) k n", b=2, k=KD)
        WH = alias("W_hi", "RING", 2 * 4096, [P, 4, KD, P])
        WL = alias("W_lo", "RING", 3 * 4096, [P, 4, KD, P])
        H_HI = alias("H_hi", "H", 0, [P, KD, T2])
        H_LO = alias("H_lo", "BIG", 12288, [P, KD, T2])
        HID_HI = alias("hidden_hi", "BIG", 0, [P, KD, T2])
        HID_LO = alias("hidden_lo", "BIG", 4096, [P, KD, T2])
        HNORM = BIG[:, 4096:8192].rearrange("p (c t) -> p c t", c=KD)
        RELU = BIG[:, 8192:9216].rearrange("p (c t) -> p c t", c=2)
        RELU2 = BIG[:, 9216:10240].rearrange("p (c t) -> p c t", c=2)

        def c(name):
            return CN[:, CON[name][0]:CON[name][1]]

        def v3(ap, n):
            return ap.rearrange("p (c t) -> p c t", c=n)

        ident, flip, window = c("ident"), c("flip"), c("window")
        zT = CN[0:EMB, CON["zT"][0]:CON["zT"][1]]
        COS, SIN, ICOS, ISIN = (v3(c(n), 2) for n in ("cos", "sin", "icos", "isin"))
        DECAY = v3(c("decay"), 2)
        BAND = c("band").rearrange("p (s g t) -> p s g t", s=2, g=4)

        FW1 = SM[0:EMB, 0:64]
        FW2 = SM[0:ORDER, 64:128]
        FW3 = SM[0:ORDER, 128:1152]
        GW2 = SM[0:2 * RANK, 1152:2176].rearrange("p (z d) -> p z d", z=2)
        PW = v3(SM[:, 2176:2688], 4)
        LRW = v3(SM[:, 2688:2944], KD)
        LR = SM[0:2 * RANK, 2944:3200]

        U = v3(BIG[:, 0:3072], 12)
        Q = v3(BIG[:, 3072:4096], 4)
        K = v3(BIG[:, 4096:5120], 4)
        G = v3(BIG[:, 5120:6144], 4)
        V = v3(BIG[:, 6144:7168], 2)
        UP = v3(BIG[:, 7168:8192], 2)
        YP = v3(BIG[:, 7168:8192], 4)
        W = BIG[:, 8192:16384]
        RAW = v3(W[:, 6144:7168], 4)
        HF, HB, FA, FB = (v3(W[:, i * 1024:(i + 1) * 1024], 2) for i in range(4))
        FARG = W[0:ORDER, 4096:4352]
        FK = W[0:ORDER, 4352:4608]
        H1 = W[0:ORDER, 4608:4864]
        KA = H[:, 0:4, T1:T2]
        KB = H[:, 4:8, T1:T2]
        ZV = v3(W[:, 0:1024], 4)
        ZT = v3(W[:, 1024:2048], 2)
        ZC = v3(W[:, 2048:3072], 4)
        ZS = v3(W[:, 3072:4096], 4)
        PP = v3(W[:, 4096:5120], 4)
        RR = v3(W[:, 5120:6144], 4)
        TMP = v3(W[:, 1024:2048], 4)
        DP = v3(W[:, 7168:8192], 4)
        X1, B1 = W[:, 0:1024], W[:, 1024:2048]
        E1, KE, QE = W[:, 2048:3072], W[:, 3072:4096], W[:, 4096:5120]
        SCO, KT = W[:, 5120:6144], W[:, 6144:7168]
        ST = [W[:, 1024:1536], W[:, 1536:2048], W[:, 7168:7680]]
        OG = BIG[:, 1024:2048]
        GT = v3(W[:, 0:6144], 24)
        MG = v3(W[:, 6144:8192], 8)
        Y1 = v3(BIG[:, 0:2048], KD)
        SQ1 = v3(BIG[:, 14336:16384], KD)
        FT = v3(BIG[:, 0:NFF * T1], NFF)
        FRAW = v3(BIG[:, 11264:12288], 4)
        Y2 = v3(BIG[:, 12288:14336], KD)

        RT2, RS2, MU = CN[:, CON2:CON2 + 512], CN[:, CON2 + 512:CON2 + 1024], CN[:, CON2 + 1024:CON2 + 1536]
        QT = v3(BIG[:, 0:4096], KD)
        KT2 = v3(BIG[:, 4096:8192], KD)
        VT = v3(BIG[:, 8192:12288], 4)
        OT = v3(BIG[:, 12288:16384], KD)
        SQ2 = v3(BIG[:, 12288:16384], KD)
        BI = [SM[:, 512 * j:512 * j + 512].rearrange("p (t r q) -> p t r q", t=2, r=ROWS) for j in range(2)]
        PB = [SM[:, 1024 + 512 * j:1536 + 512 * j] for j in range(2)]
        PT = [v3(SM[:, 2048 + 512 * j:2560 + 512 * j], 4) for j in range(2)]
        MX = SM[:, 3072:3200].rearrange("p (u c) -> p u c", c=2)
        UA = v3(BIG[:, 0:4096], KD)
        UPAD = BIG[:, 4096:4096 + KD * 2 * 286].rearrange("p (c h t) -> p c h t", c=KD, h=2)
        CV = v3(BIG[:, 8704:12800], KD)
        XC = v3(BIG[:, 4096:8192], KD)
        BG, CG, SV, SY = (v3(BIG[:, 4096 * i:4096 * i + 4096], KD) for i in range(4))

        s_x, s_ctx, s_con, s_tab = sem("x_loaded"), sem("ctx_loaded"), sem("consts_loaded"), sem("tables_loaded")
        s_small = sem("small_weights_loaded")
        s_slab = [sem(f"slab_loaded_{i}") for i in range(4)]
        slab_done = sem("slab_done")
        dve_step, act_step = sem("dve_step"), sem("act_step")
        ones_set, tab_full, tab_out = sem("ones_set"), sem("table_turned"), sem("table_in_place")
        x_new = sem("x_new")
        sq_ready, stat_full, root_ready, h_ready = sem("squares"), sem("sums"), sem("roots"), sem("h_chunks")
        prm_ready = sem("layer_params")

        def stage(name, slabs, per, banks, split=None):
            return Linear(sem(name + "_full"), sem(name + "_out"), slabs[0], slabs[1], per, banks,
                          split, None if split is None else sem(name + "_out_by_vector"))

        LO, HI = (0, 1, 2, 3), (4, 5, 6, 7)
        L1 = {"u": stage("u", SL1["u"], 4, LO), "q": stage("q", SL1["q"], 4, HI), "k": stage("k", SL1["k"], 4, LO),
              "v": stage("v", SL1["v"], 2, HI), "g": stage("g", SL1["g"], 4, LO),
              "pool": stage("pool", SL1["pool"], 2, HI), "gates": stage("gates", SL1["gates"], 4, HI),
              "branch": stage("branch", SL1["branch"], 8, LO), "w_out": stage("w_out", SL1["w_out"], 2, HI),
              "up": stage("up", SL1["up"], 4, LO, NFF), "down": stage("down", SL1["down"], 1, LO)}
        L2 = {"qkv": stage("qkv", SL2["qkv"], 4, LO, 16),
              "wo": stage("wo", SL2["wo"], 4, LO), "cv1": stage("cv1", SL2["cv1"], 4, LO),
              "cv2": stage("cv2", SL2["cv2"], 2, LO), "sc1": stage("sc1", SL2["sc1"], 4, LO, 16),
              "sc2": stage("sc2", SL2["sc2"], 4, HI)}
        stages = list(L1.values()) + list(L2.values())

        filt_full, filt_out = sem("filter_psum"), sem("filter_sbuf")
        sin_arg, sin_out = sem("sine_arguments"), sem("sines")
        kern_full, kern_out = sem("kernel_spectrum_psum"), sem("kernel_spectrum")
        conv_u, conv_f = sem("u_convolved"), sem("ffn_convolved")
        zv_ready, zt_full, zt_out = sem("zv_ready"), sem("zv_turned_psum"), sem("zv_turned")
        zf_full, zf_out, prod_ready = sem("spectrum_psum"), sem("spectrum"), sem("spectra_product")
        hy_full, hy_out = sem("hyena_psum"), sem("hyena_out")
        pd_full, pd_out, pw_full, pw_out = sem("pool_diff_psum"), sem("pool_diff"), sem("pool_psum"), sem("pooled_out")
        lr_full, lr_out = sem("lowrank_psum"), sem("lowrank")
        gk_full, gk_out, ls_ready = sem("gate_psum"), sem("gate_logits"), sem("log_sigmoid_part")
        cum_ready, exp_ready, qk_ready = sem("log_decay_sums"), sem("decay_exps"), sem("decayed_qk")
        sco_full, sco_out = sem("gla_scores_psum"), sem("gla_scores")
        kt_full, kt_out = sem("gla_k_turned_psum"), sem("gla_k_turned")
        st_full, st_out = sem("gla_state_psum"), sem("gla_states")
        og_full, og_out = sem("gla_o_psum"), sem("gla_o")
        gsq, gst_full, groot, gla_done = sem("gla_squares"), sem("gla_sums"), sem("gla_roots"), sem("gla_done")
        gelu_out, ffn_hid = sem("gelu_out"), sem("ffn_hidden")
        mod_row, mod_turned, mod_out, silu_c = sem("mod_row"), sem("mod_turned"), sem("mod_vectors"), sem("silu_c")
        g_folded, h_scaled = sem("gain_folded"), sem("h_before_shift")
        w_raw = [sem(f"raw_weights_{i}") for i in range(4)]
        w_hi, w_lo, w_used = sem("weights_hi"), sem("weights_lo"), sem("product_done")
        h_lo, hid_relu, hid_sq, hid_hi, hid_lo, down_out = (sem("h_lo"), sem("relu"), sem("relu_squared"), sem("hidden_hi_done"),
                                                  sem("hidden_lo_done"), sem("down_added"))
        bias_loaded = [sem("bias_loaded_0"), sem("bias_loaded_1")]
        bias_ready = sem("bias_masked")
        sc_full, max_ready, p_exp, p_norm = sem("scores"), sem("row_maxima"), sem("exps"), sem("probs")
        pt_full, pt_out, o_full, o_out = sem("probs_turned_psum"), sem("probs_turned"), sem("attn_psum"), sem("attn")
        cv_u, cv_dw, mu_full, mu_out = sem("conformer_gated"), sem("conformer_conv"), sem("mean_psum"), sem("means")
        xc_ready, cv_sq, cv_stat, cv_root = sem("centred"), sem("cv_squares"), sem("cv_sums"), sem("cv_roots")
        cv_norm, cv_act = sem("cv_normed"), sem("cv_activated")
        pad_set, sg_ready = sem("pads_zeroed"), sem("conformer_gates")
        sc_bg = sem("short_conv_gated")
        stored = sem("stored")
        h_shift = sem("h_modulated")

        def finished(eng, L, uses, before, i4, u, cc):
            if cc == L.per - 1:
                eng.wait_ge(slab_done, before + L.slab0 + i4 + u + 1 + CREDIT)
            else:
                eng.wait_ge(L.full, uses * (L.slabs * (L.per - 1)) + (i4 + u) * (L.per - 1) + cc + 1)

        blk = stack.enter_context(nc.Block())

        def slab(s, k, n):
            return RING[:, s % 4, 0:k * n].rearrange("p (k n) -> p k n", k=k)

        def tiles(a):
            return (0, 1, 2, 3) if a == 0 else (0, 1)

        def first_unit(a, h):
            return h * len(tiles(a))

        def unit0(a):
            return a * HEADS2 * 4

        def bank(L, e):
            return PS[:, L.banks[e % 4]]

        @blk.sync
        def _(sp):
            sp.dma_start(X[:, :, 0:T1], x.rearrange("(c p) t -> p c t", p=P)).then_inc(s_x, 16)
            sp.dma_start(CN[:, :], con).then_inc(s_con, 16)

            def load(s, dst, src, before4):
                sp.wait_ge(slab_done, before4 + s + 1)
                sp.dma_start(dst, src).then_inc(s_slab[s % 4], 16)

            def rows(a):
                return a.rearrange("l (k p) n -> l p k n", p=P)

            w_in, w_outs, up, down = rows(w["w_in"]), rows(w["w_out"]), rows(w["ffn_w_up"]), rows(w["ffn_w_down"])
            modw = rows(w["mod_w_2"])
            with sp.Fori(0, DEPTH1) as lay:
                base = lay * PER1

                def mod(j):
                    load(MOD1[j], slab(MOD1[j], KD, 512), modw[lay, :, :, 512 * j:512 * j + 512], base)

                mod(0)
                mod(1)
                for s, col in enumerate((C_U, C_U + 512, C_U + 1024, C_Q, C_K, C_V, C_G, C_POOL)):
                    load(s + 2, slab(s + 2, KD, 512), w_in[lay, :, :, col:col + 512], base)
                for j in range(2, 8):
                    mod(j)
                for j in range(6):
                    s = SL1["gates"][0] + j
                    load(s, slab(s, KD, 512), w_in[lay, :, :, C_GATE + 512 * j:C_GATE + 512 * j + 512], base)
                for j, n in enumerate(("w_br_hyena", "w_br_gla", "w_br_pool")):
                    s = SL1["branch"][0] + j
                    load(s, slab(s, 4, D), rows(w[n])[lay], base)
                for j in range(4):
                    s = SL1["w_out"][0] + j
                    load(s, slab(s, KD, 256), w_outs[lay, :, :, 256 * j:256 * j + 256], base)
                mod(8)
                mod(9)
                for j in range(11):
                    s = SL1["up"][0] + j
                    load(s, slab(s, KD, 512), up[lay, :, :, 512 * j:512 * j + 512], base)
                with sp.Fori(0, 2) as i:
                    for u in range(4):
                        sp.wait_ge(slab_done, base + SL1["down"][0] + i * 4 + u + 1)
                        s = SL1["down"][0] + u
                        sp.dma_start(slab(s, NFF, P), down[lay, :, :, bass.ds(i * 512 + u * P, P)]
                                     ).then_inc(s_slab[s % 4], 16)
                mod(10)
                mod(11)

            m1, m2 = rows(w["mlp_w1_2"]), rows(w["mlp_w2_2"])
            for l in range(DEPTH2):
                base = BEFORE2[l]
                end = base + SLABS2[l]

                def cols512(s0, src, n, width=512):
                    for j in range(n):
                        if l and s0 + j == 0:
                            sp.wait_ge(w_lo, SPLIT_CREDIT + PROD_L * l)
                        if l and s0 + j == 2:
                            sp.wait_ge(w_used, CREDIT + PROD_L * l)
                        load(s0 + j, slab(s0 + j, KD, width), src[:, :, width * j:width * j + width], base)

                if l % 3 == 0:
                    cols512(0, rows(w["na_wqkv_2"])[l // 3], 6)
                    cols512(6, rows(w["na_wo_2"])[l // 3], 2)
                elif l % 3 == 1:
                    cols512(0, rows(w["cv_w1_2"])[0], 4)
                    for n in range(2):
                        with sp.Fori(0, 3) as i:
                            for u in range(4):
                                sp.wait_ge(slab_done, base + 4 + n * MODP + i * 4 + u + 1)
                                sp.dma_start(slab(u, KD, 512), modw[2 + n][:, :, bass.ds(i * 2048 + u * 512, 512)]
                                             ).then_inc(s_slab[u], 16)
                    cols512(28, rows(w["cv_w2_2"])[0], 4, 256)
                else:
                    cols512(0, rows(w["sc_win_2"])[0], 6)
                    cols512(6, rows(w["sc_wout_2"])[0], 2)
                sp.wait_ge(slab_done, end + 2)
                with sp.Fori(0, QUARTERS) as q:
                    for r in range(PROD_Q // 2):
                        sp.wait_ge(w_lo, q * PROD_Q + (l * PROD_L + 2 * r + 2))
                        if r < KD // 2:
                            src = m1[l][:, :, bass.ds(q * D + 2 * P * r, 2 * P)]
                        else:
                            src = m2[l][:, bass.ds(q * KD, KD), 2 * P * (r - KD // 2):2 * P * (r - KD // 2 + 1)]
                        sp.dma_start(WRAW[:, r % 4], src).then_inc(w_raw[r % 4], 16)
            sp.wait_ge(h_ready, 8 * (2 * DEPTH1 + 2 * DEPTH2 + 1))
            sp.dma_start(out.rearrange("(c p) t -> p c t", p=P), H[:, :, 0:T1]).then_inc(stored, 16)
            sp.wait_ge(stored, 16)

        @blk.gpsimd
        def _(gp):
            for st in stages:
                gp.sem_inc(st.out, CREDIT)
            for s in (slab_done, conv_u, conv_f):
                gp.sem_inc(s, CREDIT)
            gp.sem_inc(mod_out, 1)
            for s, n in ((w_lo, SPLIT_CREDIT), (w_used, CREDIT), (hid_relu, CREDIT), (hid_lo, HID_CREDIT),
                         (down_out, DOWN_CREDIT)):
                gp.sem_inc(s, n)
            nc.gpsimd.memset(GW2, 0.0).then_inc(ones_set, 1)
            nc.gpsimd.memset(ONES[:, :], 1.0).then_inc(ones_set, 1)
            nc.gpsimd.memset(epsc[:, :], EPS).then_inc(ones_set, 1)
            nc.gpsimd.memset(MROW1, 0.0).then_inc(ones_set, 1)
            gp.dma_start(v3(BIG[:, 0:512], 4), prm1.rearrange("t r f -> r t f")).then_inc(s_tab, 16)
            gp.dma_start(v3(BIG[:, 512:1152], 5), prm2.rearrange("t r f -> r t f")).then_inc(s_tab, 16)
            gp.wait_ge(ones_set, 4)
            gp.sem_inc(gla_done, 1)
            with gp.Fori(0, DEPTH1) as lay:
                gp.wait_ge(gla_done, lay + 1)
                for dst, src in ((FW1, w["hy_filt_w1"][lay]), (FW2, w["hy_filt_w2"][lay]), (FW3, w["hy_filt_w3"][lay]),
                                 (GW2[0:RANK, 0, :], w["gla_gate_w2"][lay, 0]),
                                 (GW2[RANK:2 * RANK, 1, :], w["gla_gate_w2"][lay, 1]),
                                 (PW, w["pool_w"].rearrange("l g c d -> l c g d")[lay]),
                                 (LRW, w["w_in"].rearrange("l (k p) n -> l p k n", p=P)[lay, :, :, C_LR:C_LR + 2 * RANK])):
                    gp.dma_start(dst, src).then_inc(s_small, 16)
            gp.wait_ge(x_new, 1 + 2 * DEPTH1)
            gp.wait_ge(mod_out, 2 * MODP + 1)
            gp.dma_start(X[:, :, T1:T2], ctx_in.rearrange("(c p) t -> p c t", p=P)).then_inc(s_ctx, 16)
            rpb = w["na_rpb_2"]
            for a in range(2):
                if a == 1:
                    gp.wait_ge(x_new, 1 + 2 * DEPTH1 + 6)
                for h in range(HEADS2):
                    n = a * HEADS2 + h
                    if h >= 2:
                        gp.wait_ge(sc_full, unit0(a) + first_unit(a, h - 1))
                    elif a == 1:
                        gp.wait_ge(sc_full, unit0(1))
                    for t in range(2):
                        for r in range(2):
                            off = (a * HEADS2 + h) * RPB_R * RPB_C + (6 - 2 * t) * RPB_C - 48 + RPB_C * r
                            src = bass.AP(rpb.tensor, off, [[1, GRID], [RPB_C, ROWS], [1, GRID]])
                            gp.dma_start(BI[h % 2][GRID * r:GRID * r + GRID, t], src).then_inc(bias_loaded[h % 2], 16)
                    gp.wait_ge(bias_loaded[h % 2], 64 * (n // 2 + 1))
                    for t in range(2):
                        mk = nc.gpsimd.tensor_tensor(BI[h % 2][:, t], BI[h % 2][:, t],
                                                     window.rearrange("p (o q) -> p o q", o=1)
                                                     .to_broadcast([P, ROWS, GRID]), ALU.add)
                    mk.then_inc(bias_ready, 1)

        @blk.tensor
        def _(pe):
            def chain(dst, pairs):
                n = len(pairs)
                for i, (a, b) in enumerate(pairs):
                    mm = pe.matmul(dst, a, b, start=i == 0, stop=i == n - 1)
                return mm

            def product(L, uses, before, i4, u, cc, dst, pairs):
                s = L.slab0 + u
                if cc == 0:
                    pe.wait_ge(s_slab[s % 4], before * 4 + i4 * 4 + 16 * (s // 4 + 1))
                L.wait_bank(pe, uses, i4, u * L.per + cc)
                mm = chain(dst, pairs)
                if cc == L.per - 1:
                    mm.then_inc(slab_done, 1)
                else:
                    mm.then_inc(L.full, 1)

            def linear(L, uses, before, rhs, k, n, T, i4=0, us=None, first=None):
                for u in (range(L.slabs) if us is None else us):
                    ws = slab(L.slab0 + u, k, n)
                    for cc in range(L.per):
                        product(L, uses, before, i4, u, cc, bank(L, u * L.per + cc)[:, 0:T],
                                [(ws[:, kk, P * cc:P * cc + P], rhs(kk)) for kk in range(k)])

            def norm_sums(n, sq, T):
                for half in range(2):
                    pe.wait_ge(sq_ready, n * 2 + half + 1)
                    for kk in range(4 * half, 4 * half + 4):
                        mm = pe.matmul(PS[:, 7, 0:T], ONES[:, :], sq[:, kk, 0:T], start=kk == 0, stop=kk == 7)
                mm.then_inc(stat_full, 1)

            def mod_piece(pos, before, p, row, i4=0):
                pe.wait_ge(s_slab[pos % 4], before * 4 + i4 * 4 + 16 * (pos // 4 + 1))
                pe.wait_ge(mod_out, p + 1)
                ws = slab(pos, KD, 512)
                chain(PS[0:2, 3, :], [(SC[:, kk, :], ws[:, kk, :]) for kk in range(KD)]).then_inc(slab_done, 1)
                pe.wait_ge(mod_row, p + 1)
                for j in range(4):
                    tr = pe.transpose(PS[:, 3, P * j:P * j + P], row[:, j // 2, P * (j % 2):P * (j % 2) + P], ident)
                tr.then_inc(mod_turned, 1)

            pe.wait_ge(s_tab, 32)
            pe.wait_ge(s_con, 16)
            pe.wait_ge(ones_set, 4)
            for t in range(2 * NT1 + NT2):
                tr = pe.transpose(PS[:, t // 4, P * (t % 4):P * (t % 4) + P], BIG[:, P * t:P * t + P], ident)
            tr.then_inc(tab_full, 1)
            pe.wait_ge(tab_out, 1)

            with pe.Fori(0, DEPTH1) as lay:
                before = lay * PER1
                pe.wait_ge(s_small, lay * 112 + 112)
                pe.wait_ge(prm_ready, lay + 1)
                pe.matmul(PS[:, 0, 0:SEQ], SM[0:EMB, 0:P], zT, start=True, stop=True).then_inc(filt_full, 1)
                pe.wait_ge(sin_out, lay * 2 + 1)
                pe.matmul(PS[:, 1, 0:SEQ], SM[0:ORDER, 64:64 + P], H1, start=True, stop=True).then_inc(filt_full, 1)
                pe.wait_ge(sin_out, lay * 2 + 2)
                for half in range(2):
                    for tt in range(2):
                        pe.matmul(PS[:, 2 * half + tt], H1[:, P * tt:P * tt + P], FW3[:, 512 * half:512 * half + 512],
                                  start=True, stop=True).then_inc(filt_full, 1)
                pe.wait_ge(filt_out, lay + 1)
                for j, (m, src) in enumerate(((COS, FA), (SIN, FB))):
                    for f in range(2):
                        chain(PS[:, 4 + 2 * j + f], [(m[:, ss, P * f:P * f + P], src[:, ss, :]) for ss in range(2)]
                              ).then_inc(kern_full, 1)
                mod1 = lambda *js: [mod_piece(MOD1[j], before, lay * MODP + j, MROW1) for j in js]
                pe.wait_ge(silu_c, 1)
                mod1(0, 1)
                pe.wait_ge(kern_out, lay * 4 + 4)

                norm_sums(lay * 4, SQ1, T1)
                pe.wait_ge(h_ready, lay * 16 + 8)
                rhs = lambda kk: H[:, kk, 0:T1]
                pe.wait_ge(mod_out, lay * MODP + 3)
                linear(L1["u"], lay, before, rhs, KD, 512, T1)
                linear(L1["q"], lay, before, rhs, KD, 512, T1)
                L1["u"].wait_all_out(pe, lay)
                linear(L1["k"], lay, before, rhs, KD, 512, T1)
                L1["q"].wait_all_out(pe, lay)
                for tt in range(2):
                    product(L1["v"], lay, before, 0, 0, tt, bank(L1["v"], tt),
                            [(H[:, kk, P * tt:P * tt + P], slab(L1["v"].slab0, KD, 512)[:, kk, :]) for kk in range(KD)])
                L1["k"].wait_all_out(pe, lay)
                linear(L1["g"], lay, before, rhs, KD, 512, T1)
                chain(PS[0:2 * RANK, 6, 0:T1], [(LRW[:, kk, :], rhs(kk)) for kk in range(KD)]).then_inc(lr_full, 1)
                L1["v"].wait_all_out(pe, lay)
                for tt in range(2):
                    product(L1["pool"], lay, before, 0, 0, tt, bank(L1["pool"], tt),
                            [(H[:, kk, P * tt:P * tt + P], slab(L1["pool"].slab0, KD, 512)[:, kk, :]) for kk in range(KD)])

                L1["pool"].wait_all_out(pe, lay)
                L1["g"].wait_all_out(pe, lay)
                for g in range(4):
                    chain(PS[:, g, 0:T1], [(UP[:, ss, P * g:P * g + P], BAND[:, ss, g, :]) for ss in range(2)]
                          ).then_inc(pd_full, 1)
                for g in range(4):
                    pe.wait_ge(pd_out, lay * 4 + g + 1)
                    pe.matmul(PS[:, 4 + g, 0:T1], PW[:, g, :], DP[:, g, :], start=True, stop=True).then_inc(pw_full, 1)

                pe.wait_ge(zv_ready, lay + 1)
                for ss in range(2):
                    for j in range(4):
                        tr = pe.transpose(PS[:, ss, P * j:P * j + P], ZV[:, j, P * ss:P * ss + P], ident)
                    tr.then_inc(zt_full, 1)
                pe.wait_ge(zt_out, lay * 2 + 2)
                pe.wait_ge(pw_out, lay * 4 + 4)
                for j, m in enumerate((COS, SIN)):
                    for f in range(2):
                        chain(PS[:, 4 + 2 * j + f], [(m[:, ss, P * f:P * f + P], ZT[:, ss, :]) for ss in range(2)]
                              ).then_inc(zf_full, 1)
                pe.wait_ge(prod_ready, lay + 1)
                P2 = W[:, 4096:5120].rearrange("p (f n) -> p f n", f=2)
                R2 = W[:, 5120:6144].rearrange("p (f n) -> p f n", f=2)
                for j in range(4):
                    chain(PS[:, j, 0:T1], [(P2[:, f, P * j:P * j + P], ICOS[:, f, :]) for f in range(2)]
                          + [(R2[:, f, P * j:P * j + P], ISIN[:, f, :]) for f in range(2)]).then_inc(hy_full, 1)

                pe.wait_ge(lr_out, lay + 1)
                for z in range(2):
                    zz = lay * 2 + z
                    pe.wait_ge(zf_out, lay * 4 + 4) if z == 0 else pe.wait_ge(sco_out, lay * 4 + 2)
                    for j in range(4):
                        mm = pe.matmul(PS[:, 4 + j // 2, T1 * (j % 2):T1 * (j % 2) + T1],
                                       GW2[:, z, P * j:P * j + P], LR, start=True, stop=True)
                        if j % 2:
                            mm.then_inc(gk_full, 1)
                    if z == 0:
                        pe.wait_ge(hy_out, lay * 4 + 4)
                    mod1(*((2, 3) if z == 0 else (5, 6)))
                    pe.wait_ge(qk_ready, zz + 1)
                    for b in range(2):
                        for j in range(4):
                            h, tt = 2 * b + j // 2, j % 2
                            o = T1 * h + P * tt
                            mm = pe.matmul(PS[:, 4 + b, P * j:P * j + P], KE[:, o:o + P], QE[:, o:o + P],
                                           start=True, stop=True)
                        mm.then_inc(sco_full, 1)
                    if z == 1:
                        pe.wait_ge(og_out, lay * 4 + 2)
                    for b in range(2):
                        for j in range(4):
                            o = 512 * b + P * j
                            tr = pe.transpose(PS[:, 6 + b, P * j:P * j + P], X1[:, o:o + P], ident)
                        tr.then_inc(kt_full, 1)
                    if z == 0:
                        mod1(4)
                    pe.wait_ge(kt_out, zz * 2 + 2)
                    for i, n in enumerate((0, 1, 2) if z == 0 else (3, 2, 1)):
                        r = GLA_C * (n % 2)
                        for h in range(HEADS1):
                            o = T1 * h + P * (n // 2)
                            mm = pe.matmul(PS[:, i, P * h:P * h + P], KT[r:r + GLA_C, o:o + P],
                                           V[r:r + GLA_C, n // 2, P * h:P * h + P], start=True, stop=True)
                        mm.then_inc(st_full, 1)
                    pe.wait_ge(sco_out, zz * 2 + 2)
                    pe.wait_ge(st_out, zz + 1)
                    for b in range(2):
                        for h in (2 * b, 2 * b + 1):
                            for n in range(4):
                                o = T1 * h + GLA_C * n
                                dst = PS[:, 6 + b, T1 * (h % 2) + GLA_C * n:T1 * (h % 2) + GLA_C * n + GLA_C]
                                pairs = [(V[:, n // 2, P * h:P * h + P], SCO[:, o:o + GLA_C])]
                                i = n - 1 if z == 0 else 2 - n
                                if i >= 0:
                                    pairs.append((ST[i][:, P * h:P * h + P], QE[:, o:o + GLA_C]))
                                mm = chain(dst, pairs)
                        mm.then_inc(og_full, 1)
                mod1(7)
                pe.wait_ge(gsq, lay + 1)
                for b in range(2):
                    for h in (2 * b, 2 * b + 1):
                        mm = pe.matmul(PS[:, 4 + b, T1 * (h % 2):T1 * (h % 2) + T1], ONES[:, :],
                                       W[:, T1 * h:T1 * h + T1], start=True, stop=True)
                    mm.then_inc(gst_full, 1)

                pe.wait_ge(gla_done, lay + 2)
                pe.wait_ge(mod_out, lay * MODP + 9)
                linear(L1["gates"], lay, before, rhs, KD, 512, T1)
                L1["gates"].wait_all_out(pe, lay)
                for j, ys in enumerate((U, Q, YP)):
                    linear(L1["branch"], lay, before, lambda kk, ys=ys: ys[:, kk, :], 4, D, T1, us=(j,))
                L1["branch"].wait_all_out(pe, lay)
                linear(L1["w_out"], lay, before, lambda kk: MG[:, kk, :], KD, 256, T1)
                L1["w_out"].wait_all_out(pe, lay)
                mod1(8)
                norm_sums(lay * 4 + 1, SQ1, T1)
                mod1(9)

                norm_sums(lay * 4 + 2, SQ1, T1)
                pe.wait_ge(h_ready, lay * 16 + 16)
                pe.wait_ge(mod_out, lay * MODP + 11)
                linear(L1["up"], lay, before, rhs, KD, 512, T1)
                with pe.Fori(0, 2) as i:
                    L1["up"].wait_all_out(pe, lay)
                    linear(L1["down"], lay, before, lambda kk: FT[:, kk, :], NFF, P, T1, i4=i * 4, us=range(4))
                L1["down"].wait_all_out(pe, lay)
                mod1(10)
                norm_sums(lay * 4 + 3, SQ1, T1)
                mod1(11)
                pe.wait_ge(mod_out, lay * MODP + 13)

            nn = 4 * DEPTH1
            hh = 16 * DEPTH1
            for l in range(DEPTH2):
                before = BEFORE2[l]
                T = T2 if l < DEPTH2 - 1 else T1
                rhs = lambda kk, T=T: H[:, kk, 0:T]
                rhs2 = lambda kk: H[:, kk, 0:T2]
                if l:
                    pe.wait_ge(down_out, DOWN_CREDIT + QUARTERS * KD * l)
                norm_sums(nn, SQ2, T2)
                nn += 1
                hh += 8
                pe.wait_ge(h_shift, (2 * l + 1) * 8)
                if l % 3 == 0:
                    a = l // 3
                    for u in range(4):
                        Tq = T if u < 2 else T2
                        linear(L2["qkv"], a, before, (rhs if u < 2 else rhs2), KD, 512, Tq, us=(u,))
                    for u in (4, 5):
                        for tt in range(4):
                            product(L2["qkv"], a, before, 0, u, tt, bank(L2["qkv"], tt),
                                    [(H[:, kk, P * tt:P * tt + P], slab(u, KD, 512)[:, kk, :]) for kk in range(KD)])
                    L2["qkv"].wait_all_out(pe, a)

                    units = [(h, t) for h in range(HEADS2) for t in tiles(a)]
                    LAG = 2

                    def scores(n):
                        h, t = units[n]
                        g = unit0(a) + n
                        r = HD * (h % 2)
                        dst = PS[:, n % 3]
                        if n >= 3:
                            pe.wait_ge(p_exp, g - 2)
                        q = QT[r:r + HD, h // 2, P * t:P * t + P]
                        if t < 2:
                            if t == 0:
                                pe.wait_ge(bias_ready, a * HEADS2 + h + 1)
                            pe.matmul(dst[:, 0:SEQ], flip, BI[h % 2][:, t].rearrange("p r q -> p (r q)"),
                                      start=True, stop=False)
                            pe.matmul(dst[:, 0:SEQ], q, KT2[r:r + HD, h // 2, 0:SEQ], start=False, stop=True)
                            pe.matmul(dst[:, SEQ:T2], q, KT2[r:r + HD, h // 2, SEQ:T2],
                                      start=True, stop=True).then_inc(sc_full, 1)
                        else:
                            pe.matmul(dst[:, SEQ:T2], q, KT2[r:r + HD, h // 2, SEQ:T2],
                                      start=True, stop=True).then_inc(sc_full, 1)

                    def turn(n):
                        h, t = units[n]
                        g = unit0(a) + n
                        pe.wait_ge(p_norm, g + 1)
                        if n >= 2:
                            pe.wait_ge(pt_out, g - 1)
                        for j in (range(4) if t < 2 else (2, 3)):
                            tr = pe.transpose(PS[:, 3 + n % 2, P * j:P * j + P], PB[n % 2][:, P * j:P * j + P], ident)
                        tr.then_inc(pt_full, 1)

                    def values(n):
                        h, t = units[n]
                        g = unit0(a) + n
                        r = HD * (h % 2)
                        pe.wait_ge(pt_out, g + 1)
                        if t == 0 and h % 2 == 0 and h >= 4:
                            pe.wait_ge(o_out, a * 8 + h // 2 - 1)
                        mm = chain(PS[r:r + HD, 5 + (h // 2) % 2, P * t:P * t + P],
                                   [(VT[:, j, HD * h:HD * h + HD], PT[n % 2][:, j, :])
                                    for j in (range(4) if t < 2 else (2, 3))])
                        if h % 2 and t == tiles(a)[-1]:
                            mm.then_inc(o_full, 1)

                    N = len(units)
                    for n in range(N + 2):
                        if n < N:
                            scores(n)
                        if 1 <= n <= N:
                            turn(n - 1)
                        if n >= 2:
                            values(n - 2)
                    pe.wait_ge(o_out, a * 8 + 8)
                    linear(L2["wo"], a, before, lambda kk, T=T: OT[:, kk, 0:T], KD, 512, T)
                elif l % 3 == 1:
                    linear(L2["cv1"], 0, before, rhs, KD, 512, T2)
                    pe.wait_ge(L2["cv1"].out, L2["cv1"].all_out(0))
                    for n in range(2):
                        with pe.Fori(0, 3) as i:
                            for u in range(4):
                                mod_piece(MOD2[0] + n * MODP + u, before, i * 4 + ((2 + n) * MODP + u), MROW2, i4=i * 4)
                    pe.wait_ge(mod_out, 4 * MODP + 1)
                    pe.wait_ge(cv_dw, 1)
                    chain(PS[:, 7, :], [(ONES[:, :], CV[:, kk, :]) for kk in range(KD)]).then_inc(mu_full, 1)
                    pe.wait_ge(cv_sq, 1)
                    chain(PS[:, 7, :], [(ONES[:, :], UA[:, kk, :]) for kk in range(KD)]).then_inc(cv_stat, 1)
                    pe.wait_ge(cv_act, 8)
                    linear(L2["cv2"], 0, before, lambda kk: CV[:, kk, :], KD, 256, T2)
                else:
                    linear(L2["sc1"], 0, before, rhs, KD, 512, T2)
                    pe.wait_ge(sc_bg, 8)
                    linear(L2["sc2"], 0, before, lambda kk: BG[:, kk, :], KD, 512, T2)

                norm_sums(nn, SQ2, T)
                nn += 1
                with pe.Fori(0, QUARTERS) as q:
                    for j in range(PROD_Q):
                        m = j % KD
                        b, x_hi, x_lo = (LO[m % 4], H_HI, H_LO) if j < KD else (HI[m % 4], HID_HI, HID_LO)
                        pe.wait_ge(w_lo, q * PROD_Q + (l * PROD_L + j + 1 + SPLIT_CREDIT))
                        if j < KD:
                            pe.wait_ge(hid_relu, q * KD + (l * QUARTERS * KD + m + 1))
                        else:
                            pe.wait_ge(down_out, q * KD + (l * QUARTERS * KD + m + 1 + DOWN_CREDIT - 4))
                        for k in range(KD):
                            if m == 0:
                                if j == 0:
                                    pe.wait_ge(h_lo, KD * l + k + 1)
                                else:
                                    pe.wait_ge(hid_lo, q * KD + (l * QUARTERS * KD + k + 1 + HID_CREDIT))
                            for wt, xt in ((WH, x_hi), (WH, x_lo), (WL, x_hi)):
                                mm = pe.matmul(PS[:, b, 0:T], wt[:, j % 4, k, :], xt[:, k, 0:T],
                                               start=k == 0 and wt is WH and xt is x_hi, stop=k == KD - 1 and wt is WL)
                        mm.then_inc(w_used, 1)
            norm_sums(nn, SQ2, T1)


        def col1(name, j=0):
            return PRC[:, ROW1[name] + j:ROW1[name] + j + 1]

        def col2(name, j=0):
            return PR2[:, ROW2[name] + j:ROW2[name] + j + 1]

        @blk.scalar
        def _(act):
            A = nc.scalar.activation
            step = Links(act, act_step)

            def squares(dst, src, T):
                for half in range(2):
                    ks = slice(4 * half, 4 * half + 4)
                    A(dst[:, ks, 0:T], src[:, ks, 0:T], ACT.Square).then_inc(sq_ready, 1)

            def root(n, T, dst):
                act.wait_ge(stat_full, n + 1)
                A(dst[:, 0:T], PS[:, 7, 0:T], ACT.Sqrt, scale=1.0 / D, bias=epsc[:, :]).then_inc(root_ready, 1)

            def take(L, uses, before, events, put, i4=0):
                for e in events:
                    finished(act, L, uses, before, i4, e // L.per, e % L.per)
                    put(e, bank(L, e)).then_inc(L.read(e), 1)

            act.wait_ge(ones_set, 4)
            act.wait_ge(tab_out, 1)
            for j, name in enumerate(("c_2", "c_ctx_2")):
                r = ROW2[name]
                last = A(SC[:, :, j], PR2[:, r:r + KD], ACT.Silu)
            last.then_inc(silu_c, 1)

            def mod_piece(pos, before, p, row, i4=0):
                act.wait_ge(slab_done, before + i4 + pos + 1 + CREDIT)
                A(row[0:2], PS[0:2, 3, :].rearrange("p (c t) -> p c t", c=2), ACT.Copy).then_inc(mod_row, 1)

            with act.Fori(0, DEPTH1) as lay:
                before = lay * PER1
                mod1 = lambda *js: [mod_piece(MOD1[j], before, lay * MODP + j, MROW1) for j in js]
                step.base, step.n = lay * ACT_LINKS, 0
                for j in range(2):
                    act.wait_ge(sin_arg, lay * 2 + j + 1)
                    A(H1, FARG, ACT.Sin).then_inc(sin_out, 1)
                for j, dst in enumerate((KA, KB)):
                    for f in range(2):
                        act.wait_ge(kern_full, lay * 4 + 2 * j + f + 1)
                        A(dst[:, 2 * f:2 * f + 2, :], v3(PS[:, 4 + 2 * j + f], 2), ACT.Copy).then_inc(kern_out, 1)
                act.wait_ge(x_new, lay * 2 + 1)
                squares(SQ1, X, T1)
                mod1(0, 1)
                root(lay * 4, T1, SCR)

                def conv_in(raw, dst, wname, bname, n, freed, count):
                    def put(e, ps):
                        act.wait_ge(freed, lay * count + e + 1)
                        A(raw[:, e % 4, :], ps[:, 0:T1], ACT.Identity)
                        return A(dst[:, e, :], ps[:, 0:T1], ACT.Identity, scale=col1(wname, n + e), bias=col1(bname, e))
                    return put

                take(L1["u"], lay, before, range(12), conv_in(RAW, U, "hy_conv_w", "hy_conv_b", 12, conv_u, 12))
                take(L1["q"], lay, before, range(4),
                     lambda e, ps: A(Q[:, e, :], ps[:, 0:T1], ACT.Copy, scale=float(P) ** -0.5))
                take(L1["k"], lay, before, range(4), lambda e, ps: A(K[:, e, :], ps[:, 0:T1], ACT.Copy))
                take(L1["g"], lay, before, range(4), lambda e, ps: A(G[:, e, :], ps[:, 0:T1], ACT.Silu))
                act.wait_ge(lr_full, lay + 1)
                A(LR, PS[0:2 * RANK, 6, 0:T1], ACT.Copy).then_inc(lr_out, 1)
                for g in range(4):
                    act.wait_ge(pd_full, lay * 4 + g + 1)
                    A(DP[:, g, :], PS[:, g, 0:T1], ACT.Copy).then_inc(pd_out, 1)
                for j in range(4):
                    act.wait_ge(zf_full, lay * 4 + j + 1)
                    A(W[:, 2048 + 512 * j:2560 + 512 * j], PS[:, 4 + j], ACT.Copy).then_inc(zf_out, 1)
                for z in range(2):
                    zz = lay * 2 + z
                    act.wait_ge(gk_out, zz + 1)
                    step(A(B1, X1, ACT.Abs))
                    step(A(B1, B1, ACT.Exp, scale=-1.0))
                    A(B1, B1, ACT.Ln, bias=1.0).then_inc(ls_ready, 1)
                    mod1(2 if z == 0 else 5)
                    act.wait_ge(cum_ready, zz + 1)
                    A(E1, B1, ACT.Exp)
                    A(KE, B1, ACT.Exp, scale=-1.0).then_inc(exp_ready, 1)
                    mod1(3 if z == 0 else 6)
                    for b in range(2):
                        act.wait_ge(kt_full, zz * 2 + b + 1)
                        A(KT[:, 512 * b:512 * b + 512], PS[:, 6 + b], ACT.Copy).then_inc(kt_out, 1)
                    if z == 0:
                        mod1(4)
                act.wait_ge(og_out, lay * 4 + 4)
                A(W[:, 0:1024], OG, ACT.Square).then_inc(gsq, 1)
                mod1(7)
                for b in range(2):
                    act.wait_ge(gst_full, lay * 2 + b + 1)
                    A(W[:, 1024 + 512 * b:1536 + 512 * b], PS[:, 4 + b], ACT.Sqrt, scale=1.0 / P,
                      bias=epsc[:, :]).then_inc(groot, 1)
                take(L1["gates"], lay, before, range(24), lambda e, ps: A(GT[:, e, :], ps[:, 0:T1], ACT.Sigmoid))
                take(L1["w_out"], lay, before, range(8), lambda e, ps: A(Y1[:, e, :], ps[:, 0:T1], ACT.Copy))
                L1["w_out"].wait_all_out(act, lay)
                squares(SQ1, Y1, T1)
                mod1(8)
                root(lay * 4 + 1, T1, SCR)
                mod1(9)
                act.wait_ge(x_new, lay * 2 + 2)
                squares(SQ1, X, T1)
                root(lay * 4 + 2, T1, SCR)
                take(L1["up"], lay, before, range(NFF), conv_in(FRAW, FT, "ffn_conv_w", "ffn_conv_b", NFF, conv_f, NFF))
                for m in range(NFF):
                    act.wait_ge(conv_f, lay * NFF + CREDIT + m + 1)
                    A(FT[:, m, :], FT[:, m, :], ACT.Gelu).then_inc(gelu_out, 1)
                with act.Fori(0, 2) as i:
                    take(L1["down"], lay, before, range(4),
                         lambda e, ps: A(Y2[:, bass.ds(i * 4 + e, 1), :], ps[:, 0:T1].rearrange("p (o t) -> p o t", o=1),
                                         ACT.Copy), i4=i * 4)
                L1["down"].wait_all_out(act, lay)
                squares(SQ1, Y2, T1)
                mod1(10)
                root(lay * 4 + 3, T1, SCR)
                mod1(11)
                assert step.n == ACT_LINKS, step.n
            step.base, step.n = 0, ACT_LINKS * DEPTH1

            nn = 4 * DEPTH1
            norms = 0

            def split_hi(l, q, j):
                r = j // 2
                act.wait_ge(w_raw[r % 4], q * 32 + (l * 128 + 16 * (r // 4 + 1)))
                act.wait_ge(w_used, q * PROD_Q + (l * PROD_L + j + 1))
                A(WH[:, j % 4], WRAW[:, r % 4, :, P * (j % 2):P * (j % 2) + P], ACT.Copy).then_inc(w_hi, 1)

            def shift_hi(l, T):
                for k in range(KD):
                    act.wait_ge(h_ready, 8 * (2 * DEPTH1 + norms) + k + 1)
                    for s in range(T // T1):
                        ts = slice(T1 * s, T1 * s + T1)
                        last = A(H_HI[:, k, ts], HNORM[:, k, ts], ACT.Identity,
                                 bias=MODS[:, 48 * l + KD * 3 + k, s:s + 1])
                    last.then_inc(h_shift, 1)

            def shift(l, j, T):
                act.wait_ge(mod_out, MODP * (l + 1 if l < 2 else 4) + 1)
                for k in range(KD):
                    act.wait_ge(h_ready, 8 * (2 * DEPTH1 + norms) + k + 1)
                    for s in range(T // T1):
                        hs = H[:, k, T1 * s:T1 * s + T1]
                        last = A(hs, hs, ACT.Identity, bias=MODS[:, 48 * l + KD * j + k, s:s + 1])
                    last.then_inc(h_shift, 1)

            act.wait_ge(s_ctx, 16)
            for l in range(DEPTH2):
                before = BEFORE2[l]
                T = T2 if l < DEPTH2 - 1 else T1
                act.wait_ge(x_new, 1 + 2 * DEPTH1 + 2 * l)
                squares(SQ2, X, T2)
                root(nn, T2, RT2)
                nn += 1
                shift(l, 0, T2)
                norms += 1
                if l % 3 == 0:
                    a = l // 3
                    L = L2["qkv"]
                    take(L, a, before, range(8),
                         lambda e, ps: A(QT[:, e, 0:T], ps[:, 0:T], ACT.Copy, scale=float(HD) ** -0.5))
                    take(L, a, before, range(8, 16), lambda e, ps: A(KT2[:, e - 8, :], ps, ACT.Copy))
                    units = [(h, t) for h in range(HEADS2) for t in tiles(a)]
                    for n in range(len(units) + 1):
                        if n < len(units):
                            g = unit0(a) + n
                            lo = 0 if units[n][1] < 2 else SEQ
                            act.wait_ge(max_ready, g + 1)
                            if n >= 2:
                                act.wait_ge(pt_full, g - 1)
                            A(PB[n % 2][:, lo:T2], PS[:, n % 3, lo:T2], ACT.Exp, bias=MX[:, n, 0:1],
                              accum_out=MX[:, n, 1:2]).then_inc(p_exp, 1)
                        if n >= 1:
                            g = unit0(a) + n - 1
                            lo = 0 if units[n - 1][1] < 2 else 2
                            act.wait_ge(pt_full, g + 1)
                            A(PT[(n - 1) % 2][:, lo:4, :], v3(PS[:, 3 + (n - 1) % 2], 4)[:, lo:4, :],
                              ACT.Copy).then_inc(pt_out, 1)
                elif l % 3 == 1:
                    L = L2["cv1"]
                    take(L, 0, before, range(8),
                         lambda e, ps: A(UA[:, e, :], ps, ACT.Identity, bias=col2("cv_b1_2", e)))
                    take(L, 0, before, range(8, 16),
                         lambda e, ps: A(CV[:, e - 8, :], ps, ACT.Sigmoid, bias=col2("cv_b1_2", e)))
                    for n in range(2):
                        with act.Fori(0, 3) as i:
                            for u in range(4):
                                mod_piece(MOD2[0] + n * MODP + u, before, None, MROW2, i4=i * 4)
                    act.wait_ge(mu_full, 1)
                    A(MU, PS[:, 7, :], ACT.Copy, scale=1.0 / D).then_inc(mu_out, 1)
                    act.wait_ge(xc_ready, 1)
                    A(UA[:, :, :], XC[:, :, :], ACT.Square).then_inc(cv_sq, 1)
                    act.wait_ge(cv_stat, 1)
                    A(RT2, PS[:, 7, :], ACT.Sqrt, scale=1.0 / D, bias=epsc[:, :]).then_inc(cv_root, 1)
                    for k in range(KD):
                        act.wait_ge(cv_norm, k + 1)
                        A(CV[:, k, :], XC[:, k, :], ACT.Silu, bias=col2("cv_ln_b_2", k)).then_inc(cv_act, 1)
                else:
                    L = L2["sc1"]
                    take(L, 0, before, range(8), lambda e, ps: A(BG[:, e, :], ps, ACT.Copy))
                    take(L, 0, before, range(8, 16), lambda e, ps: A(CG[:, e - 8, :], ps, ACT.Copy))
                act.wait_ge(x_new, 2 + 2 * DEPTH1 + 2 * l)
                squares(SQ2, X, T)
                act.wait_ge(slab_done, before + SLABS2[l] + 3)
                for j in range(AHEAD):
                    split_hi(l, 0, j)
                root(nn, T, RT2)
                nn += 1
                shift_hi(l, T)
                norms += 1

                def quarter(q, more):
                    hid = l * QUARTERS * KD
                    for j in range(PROD_Q):
                        if j < KD:
                            act.wait_ge(w_used, q * PROD_Q + (l * PROD_L + j + 1 + CREDIT))
                            act.wait_ge(hid_lo, q * KD + (hid + j + 1))
                            A(RELU[:, j % 2, 0:T], PS[:, LO[j % 4], 0:T], ACT.Relu).then_inc(hid_relu, 1)
                        if more or j + AHEAD < PROD_Q:
                            split_hi(l, q, j + AHEAD)
                        if j < KD:
                            act.wait_ge(hid_relu, q * KD + (hid + j + 1 + CREDIT))
                            A(HID_HI[:, j, 0:T], RELU[:, j % 2, 0:T], ACT.Square).then_inc(hid_hi, 1)

                with act.Fori(0, QUARTERS - 1) as q:
                    quarter(q, True)
                quarter(QUARTERS - 1, False)
            act.wait_ge(x_new, 1 + 2 * DEPTH1 + 2 * DEPTH2)
            squares(SQ2, X, T1)
            root(nn, T1, RT2)

        @blk.vector
        def _(dve):
            v = nc.vector
            step = Links(dve, dve_step)

            def take(L, uses, before, events, put, i4=0):
                for e in events:
                    finished(dve, L, uses, before, i4, e // L.per, e % L.per)
                    put(e, bank(L, e)).then_inc(L.read(e), 1)

            def conv3(dst, raw, w0, w2, done):
                n = dst.shape[-1]
                step(v.scalar_tensor_tensor(dst[..., 1:n], raw[..., 0:n - 1], w0, dst[..., 1:n], ALU.mult, ALU.add))
                last = v.scalar_tensor_tensor(dst[..., 0:n - 1], raw[..., 1:n], w2, dst[..., 0:n - 1],
                                              ALU.mult, ALU.add)
                if done is None:
                    step(last)
                else:
                    last.then_inc(done, 1)

            def rms_into_h(n, gain):
                dve.wait_ge(root_ready, n + 1)
                step(v.reciprocal(SCR[:, T1:T2], SCR[:, 0:T1]))
                for k in range(KD):
                    v.scalar_tensor_tensor(H[:, k, 0:T1], X[:, k, 0:T1], col1(gain, k), SCR[:, T1:T2],
                                           ALU.mult, ALU.mult).then_inc(h_ready, 1)

            def add_normed(n, gain, Y):
                dve.wait_ge(root_ready, n + 1)
                step(v.reciprocal(SCR[:, T1:T2], SCR[:, 0:T1]))
                for k in range(KD):
                    last = v.scalar_tensor_tensor(Y[:, k, :], Y[:, k, :], col1(gain, k), SCR[:, T1:T2],
                                                  ALU.mult, ALU.mult)
                step(last)
                v.tensor_tensor(X[:, :, 0:T1], X[:, :, 0:T1], Y, ALU.add).then_inc(x_new, 1)

            def mod_piece(p, c0):
                dve.wait_ge(mod_turned, p + 1)
                v.tensor_tensor(MODS[:, bass.ds(c0, 4), :], v3(PS[:, 3], 4)[:, :, 0:2],
                                PR2[:, bass.ds(c0 + ROW2["mod_b_2"], 4)]
                                .rearrange("p (k o) -> p k o", o=1).to_broadcast([P, 4, 2]), ALU.add).then_inc(mod_out, 1)

            dve.wait_ge(tab_full, 1)
            v.tensor_copy(PR1[:, :], PS[:, 0])
            v.tensor_copy(PR2[:, 0:512], PS[:, 1])
            v.tensor_copy(PR2[:, 512:640], PS[:, 2, 0:P]).then_inc(tab_out, 1)
            dve.wait_ge(tab_out, 1)
            dve.wait_ge(s_x, 16)
            dve.wait_ge(s_con, 16)
            v.memset(GM[:, :, :], 0.0).then_inc(x_new, 1)
            with dve.Fori(0, DEPTH1) as lay:
                before = lay * PER1
                step.base, step.n = 3 * 0 + lay * DVE_LINKS, 0
                v.tensor_copy(PRC[:, :], PR1[:, bass.ds(lay * (NT1 * P), NT1 * P)]).then_inc(prm_ready, 1)
                dve.wait_ge(prm_ready, lay + 1)
                for j, (b, f) in enumerate((("hy_filt_b1", "hy_filt_freq1"), ("hy_filt_b2", "hy_filt_freq2"))):
                    dve.wait_ge(filt_full, lay * 6 + j + 1)
                    step(v.tensor_scalar(FARG, PS[0:ORDER, j, 0:SEQ], col1(b)[0:ORDER], col1(f)[0:ORDER], ALU.add, ALU.mult))
                    step(v.tensor_scalar(FK, FARG, 1.0 / (2.0 * np.pi), MAGIC, ALU.mult, ALU.add))
                    step(v.tensor_scalar(FK, FK, -MAGIC, None, ALU.add))
                    for part in (TWO_PI_HI, TWO_PI_MID, TWO_PI_LO):
                        step(v.scalar_tensor_tensor(FARG, FK, -part, FARG, ALU.mult, ALU.add))
                    v.tensor_scalar(FARG, FARG, 3.1415925, -3.1415925, ALU.min, ALU.max).then_inc(sin_arg, 1)
                dve.wait_ge(filt_full, lay * 6 + 6)
                for tt in range(2):
                    v.tensor_tensor(HF[:, tt, :], PS[:, tt], DECAY[:, tt, :], ALU.mult)
                    last = v.tensor_tensor(HB[:, tt, :], PS[:, 2 + tt], DECAY[:, tt, :], ALU.mult)
                step(last)
                step(v.memset(HB[0:1, 0, :], 0.0))
                v.tensor_tensor(FA, HF, HB, ALU.add)
                v.tensor_tensor(FB, HF, HB, ALU.subtract).then_inc(filt_out, 1)

                mod1 = lambda *js: [mod_piece(lay * MODP + j, lay * 48 + 4 * j) for j in js]
                mod1(0, 1)
                rms_into_h(lay * 4, "norm_mix_pre")
                for e in range(12):
                    dve.wait_ge(L1["u"].out, lay * 12 + CREDIT + e + 1)
                    conv3(U[:, e, :], RAW[:, e % 4, :], col1("hy_conv_w", e), col1("hy_conv_w", 24 + e), conv_u)
                dve.wait_ge(conv_u, lay * 12 + CREDIT + 12)
                v.tensor_tensor(ZV, U[:, 4:8, :], U[:, 8:12, :], ALU.mult).then_inc(zv_ready, 1)
                take(L1["v"], lay, before, range(2), lambda e, ps: v.tensor_copy(V[:, e, :], ps))
                take(L1["pool"], lay, before, range(2), lambda e, ps: v.tensor_copy(UP[:, e, :], ps))
                for g in range(4):
                    dve.wait_ge(pw_full, lay * 4 + g + 1)
                    v.tensor_scalar(YP[:, g, :], PS[:, 4 + g, 0:T1], col1("pool_scale", g), None,
                                    ALU.mult).then_inc(pw_out, 1)
                for ss in range(2):
                    dve.wait_ge(zt_full, lay * 2 + ss + 1)
                    v.tensor_copy(ZT[:, ss, :], PS[:, ss]).then_inc(zt_out, 1)
                dve.wait_ge(kern_out, lay * 4 + 4)
                dve.wait_ge(zf_out, lay * 4 + 4)
                v.tensor_tensor(PP, ZC, KA, ALU.mult)
                step(v.tensor_tensor(TMP, ZS, KB, ALU.mult))
                v.tensor_tensor(RR, ZC, KB, ALU.mult)
                step(v.tensor_tensor(PP, PP, TMP, ALU.subtract))
                step(v.tensor_tensor(TMP, ZS, KA, ALU.mult))
                v.tensor_tensor(RR, RR, TMP, ALU.add).then_inc(prod_ready, 1)
                dve.wait_ge(prod_ready, lay + 1)
                for j in range(4):
                    dve.wait_ge(hy_full, lay * 4 + j + 1)
                    step(v.scalar_tensor_tensor(TMP[:, j, :], ZV[:, j, :], col1("hy_bias", j), PS[:, j, 0:T1],
                                                ALU.mult, ALU.add))
                    v.tensor_tensor(U[:, j, :], U[:, j, :], TMP[:, j, :], ALU.mult).then_inc(hy_out, 1)
                for z in range(2):
                    zz = lay * 2 + z
                    for j in range(4):
                        if j % 2 == 0:
                            dve.wait_ge(gk_full, zz * 2 + j // 2 + 1)
                        o = T1 * (j % 2)
                        last = v.tensor_scalar(X1[:, T1 * j:T1 * j + T1], PS[:, 4 + j // 2, o:o + T1],
                                               col1("gla_gate_b", 4 * z + j), None, ALU.add)
                    last.then_inc(gk_out, 1)
                    dve.wait_ge(ls_ready, zz + 1)
                    step(v.scalar_tensor_tensor(X1, X1, 0.0, B1, ALU.min, ALU.subtract))
                    step(v.tensor_scalar(X1, X1, 1.0 / 16.0, -1.0, ALU.mult, ALU.max))
                    for j in range(4):
                        la, cum = X1[:, T1 * j:T1 * j + T1], B1[:, T1 * j:T1 * j + T1]
                        if z == 0:
                            last = v.tensor_tensor_scan(out=cum, data0=c("scan_f"), data1=la, initial=0.0,
                                                        op0=ALU.mult, op1=ALU.add)
                        else:
                            last = v.tensor_tensor_scan(out=cum[:, ::-1], data0=c("scan_b")[:, ::-1], data1=la[:, ::-1],
                                                        initial=0.0, op0=ALU.mult, op1=ALU.add)
                    last.then_inc(cum_ready, 1)
                    mod1(2 if z == 0 else 5)
                    dve.wait_ge(exp_ready, zz + 1)
                    v.tensor_tensor(QE, BIG[:, 3072:4096], E1, ALU.mult)
                    step(v.tensor_tensor(KE, BIG[:, 4096:5120], KE, ALU.mult))
                    edge = GLA_C - 1 if z == 0 else 0
                    chunks = lambda ap: ap.rearrange("p (n t) -> p n t", t=GLA_C)
                    v.tensor_tensor(chunks(X1), chunks(KE), chunks(E1)[:, :, edge:edge + 1].to_broadcast([P, 16, GLA_C]),
                                    ALU.mult).then_inc(qk_ready, 1)
                    mod1(3 if z == 0 else 6)
                    mask = c("mask_f" if z == 0 else "mask_b").rearrange("p (o t) -> p o t", o=1)
                    for b in range(2):
                        dve.wait_ge(sco_full, zz * 2 + b + 1)
                        v.tensor_tensor(v3(SCO[:, 512 * b:512 * b + 512], 4), v3(PS[:, 4 + b], 4),
                                        mask.to_broadcast([P, 4, P]), ALU.mult).then_inc(sco_out, 1)
                    if z == 0:
                        mod1(4)
                    for i in range(3):
                        dve.wait_ge(st_full, zz * 3 + i + 1)
                        if i == 0:
                            step(v.tensor_copy(ST[0], PS[:, 0]))
                            continue
                        n = i if z == 0 else 3 - i
                        for h in range(HEADS1):
                            hs = slice(P * h, P * h + P)
                            o = T1 * h + GLA_C * n + edge
                            last = v.scalar_tensor_tensor(ST[i][:, hs], ST[i - 1][:, hs], E1[:, o:o + 1],
                                                          PS[:, i, hs], ALU.mult, ALU.add)
                        if i == 1:
                            step(last)
                        else:
                            last.then_inc(st_out, 1)
                    for b in range(2):
                        dve.wait_ge(og_full, zz * 2 + b + 1)
                        og = OG[:, 512 * b:512 * b + 512]
                        if z == 0:
                            v.tensor_copy(og, PS[:, 6 + b]).then_inc(og_out, 1)
                        else:
                            v.tensor_tensor(og, og, PS[:, 6 + b], ALU.add).then_inc(og_out, 1)
                mod1(7)
                dve.wait_ge(groot, lay * 2 + 2)
                step(v.reciprocal(B1, B1))
                yg = BIG[:, 3072:4096]
                step(v.scalar_tensor_tensor(yg, OG, col1("gla_norm"), B1, ALU.mult, ALU.mult))
                v.tensor_tensor(yg, yg, BIG[:, 5120:6144], ALU.mult).then_inc(gla_done, 1)

                L1["gates"].wait_all_out(dve, lay)

                def merge(e, ps):
                    if e < 8:
                        return v.tensor_tensor(MG[:, e, :], GT[:, e, :], ps[:, 0:T1], ALU.mult)
                    step(v.tensor_tensor(GT[:, e, :], GT[:, e, :], ps[:, 0:T1], ALU.mult))
                    return v.tensor_tensor(MG[:, e % 8, :], MG[:, e % 8, :], GT[:, e, :], ALU.add)

                take(L1["branch"], lay, before, range(24), merge)
                mod1(8)
                add_normed(lay * 4 + 1, "norm_mix_post", Y1)
                mod1(9)
                dve.wait_ge(x_new, lay * 2 + 2)
                rms_into_h(lay * 4 + 2, "norm_ffn_pre")
                for m in range(NFF):
                    dve.wait_ge(L1["up"].out, lay * NFF + CREDIT + m + 1)
                    conv3(FT[:, m, :], FRAW[:, m % 4, :], col1("ffn_conv_w", m), col1("ffn_conv_w", 2 * NFF + m), conv_f)

                def times_gelu(e, ps):
                    dve.wait_ge(gelu_out, lay * NFF + e - NFF + 1)
                    return v.tensor_tensor(FT[:, e - NFF, :], FT[:, e - NFF, :], ps[:, 0:T1], ALU.mult)

                take(L1["up"], lay, before, range(NFF, 2 * NFF), times_gelu)
                mod1(10)
                add_normed(lay * 4 + 3, "norm_ffn_post", Y2)
                mod1(11)
                dve.wait_ge(x_new, lay * 2 + 3)
                assert step.n == DVE_LINKS, step.n
            step.base, step.n = 0, DVE_LINKS * DEPTH1

            nn = 4 * DEPTH1

            def gain_rstd(n, l, gain, j, T):
                grow = PR2[:, ROW2[gain] + KD * l:ROW2[gain] + KD * l + KD].rearrange("p (k o) -> p k o", o=1)
                step(v.scalar_tensor_tensor(GM[:, :, :], MODS[:, 48 * l + KD * (j + 1):48 * l + KD * (j + 2), :], 1.0,
                                            grow.to_broadcast([P, KD, 2]), ALU.add, ALU.mult))
                dve.wait_ge(root_ready, n + 1)
                step(v.reciprocal(RS2[:, 0:T], RT2[:, 0:T]))

            def scaled_into_h(n, l, gain, j, T):
                gain_rstd(n, l, gain, j, T)
                for k in range(KD):
                    for s in range(T // T1):
                        ts = slice(T1 * s, T1 * s + T1)
                        last = v.scalar_tensor_tensor(H[:, k, ts], X[:, k, ts], GM[:, k, s:s + 1], RS2[:, ts],
                                                      ALU.mult, ALU.mult)
                    last.then_inc(h_ready, 1)

            def split_lo(l, q, j):
                r = j // 2
                dve.wait_ge(w_hi, q * PROD_Q + (l * PROD_L + j + 1))
                v.tensor_tensor(WL[:, j % 4], WRAW[:, r % 4, :, P * (j % 2):P * (j % 2) + P],
                                WH[:, j % 4].bitcast(F32), ALU.subtract).then_inc(w_lo, 1)

            def scaled_and_lo(n, l, T):
                gain_rstd(n, l, "norm2_g_2", 3, T)
                for k in range(KD):
                    for s in range(T // T1):
                        ts = slice(T1 * s, T1 * s + T1)
                        last = v.scalar_tensor_tensor(HNORM[:, k, ts], X[:, k, ts], GM[:, k, s:s + 1], RS2[:, ts],
                                                      ALU.mult, ALU.mult)
                    last.then_inc(h_ready, 1)
                    for kk in ((k - 1,) if 0 < k < KD - 1 else (k - 1, k) if k else ()):
                        dve.wait_ge(h_shift, (2 * l + 1) * KD + kk + 1)
                        for s in range(T // T1):
                            ts = slice(T1 * s, T1 * s + T1)
                            last = v.scalar_tensor_tensor(H_LO[:, kk, ts], HNORM[:, kk, ts],
                                                          MODS[:, 48 * l + KD * 3 + kk, s:s + 1],
                                                          H_HI[:, kk, ts].bitcast(F32), ALU.add, ALU.subtract)
                        last.then_inc(h_lo, 1)

            def add_gated(j, k, T, src):
                for s in range(T // T1):
                    ts = slice(T1 * s, T1 * s + T1)
                    last = v.scalar_tensor_tensor(X[:, k, ts], src[:, ts], MODS[:, 48 * l + KD * j + k, s:s + 1], X[:, k, ts],
                                                  ALU.mult, ALU.add)
                return last

            for l in range(DEPTH2):
                before = BEFORE2[l]
                T = T2 if l < DEPTH2 - 1 else T1
                dve.wait_ge(mod_out, MODP * (l + 1 if l < 2 else 4) + 1)
                if l == 0:
                    dve.wait_ge(s_ctx, 16)
                scaled_into_h(nn, l, "norm1_g_2", 0, T2)
                nn += 1
                if l % 3 == 0:
                    a = l // 3
                    take(L2["qkv"], a, before, range(16, 24),
                         lambda e, ps: v.tensor_copy(VT[:, e % 4, 512 * (e // 4 - 4):512 * (e // 4 - 3)], ps))
                    units = [(h, t) for h in range(HEADS2) for t in tiles(a)]
                    N = len(units)
                    per_pair = 2 * len(tiles(a))
                    for n in range(N + 3):
                        if n < N:
                            g = unit0(a) + n
                            lo = 0 if units[n][1] < 2 else SEQ
                            dve.wait_ge(sc_full, g + 1)
                            v.tensor_reduce(MX[:, n, 0:1], PS[:, n % 3, lo:T2], AX.X, ALU.max,
                                            negate=True).then_inc(max_ready, 1)
                        if 1 <= n <= N:
                            g = unit0(a) + n - 1
                            lo = 0 if units[n - 1][1] < 2 else SEQ
                            pb = PB[(n - 1) % 2][:, lo:T2]
                            dve.wait_ge(p_exp, g + 1)
                            step(v.reciprocal(MX[:, n - 1, 1:2], MX[:, n - 1, 1:2]))
                            v.tensor_scalar(pb, pb, MX[:, n - 1, 1:2], None, ALU.mult).then_inc(p_norm, 1)
                        if n >= 3 and (n - 2) % per_pair == 0:
                            k = (n - 2) // per_pair - 1
                            dve.wait_ge(o_full, a * 8 + k + 1)
                            v.tensor_copy(OT[:, k, 0:T], PS[:, 5 + k % 2, 0:T]).then_inc(o_out, 1)
                    assert (N + 2 - 2) % per_pair == 0
                    take(L2["wo"], a, before, range(8), lambda e, ps: add_gated(2, e, T, ps))
                elif l % 3 == 1:
                    v.memset(UPAD[:, :, :, 0:15], 0.0)
                    v.memset(UPAD[:, :, :, 15 + SEQ:286], 0.0)
                    for k in range(KD):
                        dve.wait_ge(L2["cv1"].out, CREDIT + 8 + k + 1)
                        last = v.tensor_tensor(UPAD[:, k, :, 15:15 + SEQ], v3(UA[:, k, :], 2), v3(CV[:, k, :], 2), ALU.mult)
                    step(last)
                    for k in range(KD):
                        cvk = v3(CV[:, k, :], 2)
                        for tap in range(TAPS):
                            win = UPAD[:, k, :, tap:tap + SEQ]
                            wcol = col2("cv_dw_2", KD * tap + k)
                            if tap == 0:
                                step(v.tensor_scalar(cvk, win, wcol, col2("cv_dwb_2", k), ALU.mult, ALU.add))
                            elif tap < TAPS - 1 or k < KD - 1:
                                step(v.scalar_tensor_tensor(cvk, win, wcol, cvk, ALU.mult, ALU.add))
                            else:
                                v.scalar_tensor_tensor(cvk, win, wcol, cvk, ALU.mult, ALU.add).then_inc(cv_dw, 1)
                            if tap % 10 == 5:
                                m = 3 * k + tap // 10
                                mod_piece(2 * MODP + m, 96 + 4 * m)
                    dve.wait_ge(mu_out, 1)
                    v.tensor_tensor(XC, CV, MU.rearrange("p (o t) -> p o t", o=1).to_broadcast([P, KD, T2]),
                                    ALU.subtract).then_inc(xc_ready, 1)
                    dve.wait_ge(cv_root, 1)
                    step(v.reciprocal(RS2, RT2))
                    for k in range(KD):
                        v.scalar_tensor_tensor(XC[:, k, :], XC[:, k, :], col2("cv_ln_g_2", k), RS2, ALU.mult,
                                               ALU.mult).then_inc(cv_norm, 1)

                    def add_conf(e, ps):
                        t = SM[:, 512 * (e % 4):512 * (e % 4) + 512]
                        step(v.tensor_scalar(t, ps, col2("cv_b2_2", e), None, ALU.add))
                        return add_gated(2, e, T2, t)

                    take(L2["cv2"], 0, before, range(8), add_conf)
                else:
                    def conv_in(e, ps):
                        m = e - 16
                        return v.tensor_tensor(SV[:, m, :], CG[:, m, :], ps, ALU.mult)

                    dve.wait_ge(L2["sc1"].out, CREDIT + 16)
                    for m in range(KD):
                        take(L2["sc1"], 0, before, (16 + m,), conv_in)
                        dve.wait_ge(L2["sc1"].out2, m + 1)
                        s, y = v3(SV[:, m, :], 2), v3(SY[:, m, :], 2)
                        step(v.tensor_scalar(y, s, col2("sc_conv_2", KD + m), None, ALU.mult))
                        conv3(y, s, col2("sc_conv_2", m), col2("sc_conv_2", 2 * KD + m), None)
                        v.tensor_tensor(BG[:, m, :], BG[:, m, :], SY[:, m, :], ALU.mult).then_inc(sc_bg, 1)
                    take(L2["sc2"], 0, before, range(8), lambda e, ps: add_gated(2, e, T2, ps))
                v.memset(GM[:, :, :], 0.0).then_inc(x_new, 1)
                dve.wait_ge(x_new, 2 + 2 * DEPTH1 + 2 * l)
                dve.wait_ge(slab_done, before + SLABS2[l] + 4)
                for j in range(AHEAD):
                    split_lo(l, 0, j)
                scaled_and_lo(nn, l, T)
                nn += 1

                def quarter(q, more):
                    hid = l * QUARTERS * KD
                    for j in range(PROD_Q):
                        if j < KD:
                            r1, r2 = RELU[:, j % 2, 0:T], RELU2[:, j % 2, 0:T]
                            dve.wait_ge(hid_relu, q * KD + (hid + j + 1 + CREDIT))
                            dve.wait_ge(hid_lo, q * KD + (hid + j + 1))
                            v.tensor_tensor(r2, r1, r1, ALU.mult).then_inc(hid_sq, 1)
                        else:
                            dve.wait_ge(w_used, q * PROD_Q + (l * PROD_L + j + 1 + CREDIT))
                            dve.wait_ge(down_out, q * KD + (hid + j - KD + 1))
                            add_gated(5, j - KD, T, PS[:, HI[j % 4]]).then_inc(down_out, 1)
                        if more or j + AHEAD < PROD_Q:
                            split_lo(l, q, j + AHEAD)
                        if j < KD:
                            dve.wait_ge(hid_sq, q * KD + (hid + j + 1))
                            dve.wait_ge(hid_hi, q * KD + (hid + j + 1))
                            v.tensor_tensor(HID_LO[:, j, 0:T], r2, HID_HI[:, j, 0:T].bitcast(F32),
                                            ALU.subtract).then_inc(hid_lo, 1)

                with dve.Fori(0, QUARTERS - 1) as q:
                    quarter(q, True)
                quarter(QUARTERS - 1, False)
                dve.wait_ge(down_out, DOWN_CREDIT + QUARTERS * KD * (l + 1))
                v.memset(GM[:, :, :], 0.0).then_inc(x_new, 1)
                dve.wait_ge(x_new, 3 + 2 * DEPTH1 + 2 * l)
            dve.wait_ge(root_ready, nn + 1)
            step(v.reciprocal(RS2[:, 0:T1], RT2[:, 0:T1]))
            for k in range(KD):
                v.scalar_tensor_tensor(H[:, k, 0:T1], X[:, k, 0:T1], col2("final_g_2", k), RS2[:, 0:T1],
                                       ALU.mult, ALU.mult).then_inc(h_ready, 1)


def constants():
    C = np.zeros((P, NCON), np.float32)

    def put(name, a):
        lo, hi = CON[name]
        C[:a.shape[0], lo:hi] = a.reshape(a.shape[0], -1)

    i = np.arange(P)
    put("ident", np.eye(P))
    put("flip", np.eye(P)[::-1])
    q = GRID - 1 - i % GRID
    start = np.clip(q - WCOLS // 2, 0, GRID - WCOLS)[:, None]
    k = np.arange(GRID)[None]
    put("window", np.where((k >= start) & (k < start + WCOLS), 0.0, -1e30))
    same = i[:, None] // GLA_C == i[None] // GLA_C
    put("mask_f", (same & (i[:, None] <= i[None])).astype(float))
    put("mask_b", (same & (i[:, None] > i[None])).astype(float))
    t = np.arange(SEQ)
    put("scan_f", np.tile((t % GLA_C != 0).astype(float), (P, 1)))
    put("scan_b", np.tile((t % GLA_C != GLA_C - 1).astype(float), (P, 1)))
    bands = (EMB - 1) // 2
    tl = np.linspace(0.0, 1.0, SEQ, dtype=np.float32)[:, None]
    ang = (np.linspace(1e-4, bands - 1, bands, dtype=np.float32)[None]
           * (2.0 * np.pi * np.arange(SEQ, dtype=np.float32)[:, None] / SEQ).astype(np.float32))
    put("zT", np.concatenate([tl, np.cos(ang), -np.sin(ang)], axis=1).T)
    th = (2 * t[None] + 1) * t[:, None] * np.pi / (2 * SEQ)

    def tiled(m):
        return m.reshape(2, P, -1).transpose(1, 0, 2)

    put("cos", tiled(np.cos(th)))
    put("sin", tiled(np.sin(th)))
    put("icos", tiled(np.cos(th).T / SEQ))
    put("isin", tiled(np.sin(th).T / SEQ))
    lo, hi = np.log(1e-2) / 1.5, np.log(1e-2) / 0.3
    deltas = np.linspace(lo, hi, HY, dtype=np.float32)
    put("decay", tiled(np.exp(-tl * np.abs(deltas)[None])))
    band = np.zeros((SEQ, 4, SEQ))
    for g, wn in enumerate(WINDOWS):
        half = wn // 2
        for tt in range(SEQ):
            a, b = max(tt - half, 0), min(tt + half, SEQ)
            band[a:b, g, tt] = 1.0 / (b - a)
            band[tt, g, tt] -= 1.0
    put("band", band.reshape(2, P, 4, SEQ).transpose(1, 0, 2, 3))
    return C


def kernel(**inputs):
    import concourse.bacc as bacc
    from concourse.bass_utils import run_bass_kernel_spmd as run

    def table(names, rows_of, tables, layer=None):
        out = np.zeros((tables, P, P), np.float32)
        flat = out.reshape(tables * P, P)
        for name in names:
            a = np.asarray(inputs[name])
            a = a[layer] if layer is not None else a
            if a.shape[-1] < P:
                flat[rows_of[name], :a.shape[-1]] = a
            else:
                a = a.reshape(-1, P)
                flat[rows_of[name]:rows_of[name] + len(a)] = a
        return out

    arrays = {
        "xT": np.ascontiguousarray(np.asarray(inputs["x"])[0].T),
        "ctxT": np.ascontiguousarray(np.asarray(inputs["ctx_2"])[0].T),
        "consts": constants(),
        "params1": np.concatenate([table(ROW1, ROW1, NT1, l) for l in range(DEPTH1)]),
        "params2": table(ROW2, ROW2, NT2),
    }
    nc = bacc.Bacc("TRN2", target_bir_lowering=False, num_devices=1)
    big = ("w_in", "w_br_hyena", "w_br_gla", "w_br_pool", "w_out", "ffn_w_up", "ffn_w_down", "hy_filt_w1",
           "hy_filt_w2", "hy_filt_w3", "gla_gate_w2", "pool_w", "mod_w_2", "mlp_w1_2", "mlp_w2_2", "na_wqkv_2",
           "na_wo_2", "na_rpb_2", "cv_w1_2", "cv_w2_2", "sc_win_2", "sc_wout_2")
    for name in big:
        arrays[name] = np.ascontiguousarray(inputs[name])
    aps = {n: nc.dram_tensor(n, a.shape, mybir.dt.from_np(a.dtype), kind="ExternalInput").ap()
           for n, a in arrays.items()}
    out = nc.dram_tensor("out_0", (D, SEQ), F32, kind="ExternalOutput").ap()
    build(nc, aps["xT"], aps["ctxT"], aps["consts"], aps["params1"], aps["params2"], aps, out)
    r = run(nc, [arrays], core_ids=[0])
    return np.ascontiguousarray(r.results[0]["out_0"].T)[None]
```

```python
from contextlib import ExitStack

import numpy as np

import concourse.bass as bass
from concourse import mybir

ALU = mybir.AluOpType
ACT = mybir.ActivationFunctionType
AX = mybir.AxisListType
F32 = mybir.dt.float32
F32R = mybir.dt.float32r

P = 128
D = 1024
KD = D // P
SEQ = 256
T1 = SEQ
T2 = 2 * SEQ
EPS = 1e-6
CREDIT = 4

DEPTH1 = 2
HY = 512
EMB = 33
ORDER = 64
HEADS1 = 4
RANK = 16
GLA_C = 64
WINDOWS = (2, 4, 8, 16)
D_FF = 2816
NFF = D_FF // P
D_IN = 3 * HY + 4 * 512 + 2 * RANK + 512 + 3 * D

DEPTH2 = 4
HEADS2 = 16
HD = D // HEADS2
GRID = 64
ROWS = SEQ // GRID
WCOLS = 16
RPB_R, RPB_C = 15, 31
TAPS = 31
FF2 = 4 * D

C_U, C_Q, C_K, C_V, C_G = 0, 1536, 2048, 2560, 3072
C_LR = 3584
C_POOL = C_LR + 2 * RANK
C_GATE = C_POOL + 512

CON = {}
_at = 0
for _n, _w in (("ident", P), ("flip", P), ("window", GRID),
               ("mask_f", P), ("mask_b", P), ("scan_f", SEQ), ("scan_b", SEQ), ("zT", SEQ),
               ("cos", 2 * SEQ), ("sin", 2 * SEQ), ("icos", 2 * SEQ), ("isin", 2 * SEQ),
               ("decay", 2 * HY), ("band", 8 * SEQ)):
    CON[_n] = (_at, _at + _w)
    _at += _w
NCON = _at
CON2 = CON["window"][1]

ROW1 = {}
_at = 0
for _n, _w in (("norm_mix_pre", 8), ("norm_mix_post", 8), ("norm_ffn_pre", 8), ("norm_ffn_post", 8),
               ("hy_conv_w", 36), ("hy_conv_b", 12), ("hy_bias", 4), ("gla_gate_b", 8), ("gla_norm", 1),
               ("pool_scale", 4), ("hy_filt_b1", 1), ("hy_filt_freq1", 1), ("hy_filt_b2", 1),
               ("hy_filt_freq2", 1), ("ffn_conv_w", 66), ("ffn_conv_b", 22)):
    ROW1[_n] = _at
    _at += _w
ROW2 = {}
_at = 0
for _n, _w in (("mod_b_2", 192), ("norm1_g_2", 32), ("norm2_g_2", 32), ("cv_b1_2", 16), ("cv_dw_2", 248),
               ("cv_dwb_2", 8), ("cv_ln_g_2", 8), ("cv_ln_b_2", 8), ("cv_b2_2", 8), ("sc_conv_2", 24),
               ("final_g_2", 8), ("c_2", 8), ("c_ctx_2", 8)):
    ROW2[_n] = _at
    _at += _w
NT1, NT2 = 2, 5

SL1 = {"u": (2, 3), "q": (5, 1), "k": (6, 1), "v": (7, 1), "g": (8, 1), "pool": (9, 1), "gates": (16, 6),
       "branch": (22, 3), "w_out": (25, 4), "up": (31, 11), "down": (42, 8)}
MOD1 = (0, 1, 10, 11, 12, 13, 14, 15, 29, 30, 50, 51)
PER1 = 52
MOD2 = 2 * 12
BEFORE2 = DEPTH1 * PER1

QUARTERS = FF2 // D
PROD_Q = 2 * KD
PROD_L = QUARTERS * PROD_Q
MIXER = (32, 24, 32, 32)
N_MIX = [sum(MIXER[:l]) + l * PROD_L for l in range(DEPTH2)]
N_MLP = [N_MIX[l] + MIXER[l] for l in range(DEPTH2)]
AHEAD = 3
SPLIT_CREDIT, HID_CREDIT, DOWN_CREDIT = 8, 2, 8
MODP = 12
ACT_LINKS, DVE_LINKS = 4, 89
MAGIC = 12582912.0
TWO_PI_HI, TWO_PI_MID, TWO_PI_LO = 6.28125, 0.0019350051879882812, 3.019916e-07


class Linear:

    def __init__(self, full, out, slab0, slabs, per, banks, split=None, out2=None):
        self.full, self.out, self.slab0, self.slabs, self.per, self.banks = full, out, slab0, slabs, per, banks
        self.events = slabs * per
        self.out2, self.first = out2, self.events if out2 is None else split

    def all_out(self, uses):
        return uses * self.first + self.first + CREDIT

    def wait_all_out(self, eng, uses):
        eng.wait_ge(self.out, self.all_out(uses))
        if self.out2 is not None:
            eng.wait_ge(self.out2, uses * (self.events - self.first) + self.events - self.first)

    def wait_bank(self, eng, uses, i4, e):
        if e < self.first + 4:
            eng.wait_ge(self.out, uses * self.first + i4 * self.per + e + 1)
        else:
            eng.wait_ge(self.out2, uses * (self.events - self.first) + e - self.first - 4 + 1)

    def read(self, e):
        return self.out if e < self.first else self.out2


class Links:

    def __init__(self, eng, sem):
        self.eng, self.sem, self.base, self.n = eng, sem, 0, 0

    def __call__(self, ins):
        self.mark(ins)
        self.wait()

    def mark(self, ins):
        ins.then_inc(self.sem, 1)
        self.n += 1

    def wait(self):
        self.eng.wait_ge(self.sem, self.base + self.n)


def build(nc, x, ctx_in, con, prm1, prm2, w, out):
    with ExitStack() as stack:
        place = {}

        def sb(name, shape):
            place[name] = (nc.sbuf_base + 31) // 32 * 32
            return stack.enter_context(nc.sbuf_tensor(name, shape, F32))

        def sem(name):
            return stack.enter_context(nc.semaphore(name))

        X = sb("X", [P, KD, T2])
        H = sb("H", [P, KD, T2])
        BIG = sb("BIG", [P, 16384])
        RING = sb("RING", [P, 4, 4096])
        CN = sb("CN", [P, NCON])
        SM = sb("SM", [P, 3200])
        PR1 = sb("PR1", [P, DEPTH1 * NT1 * P])
        PR2 = sb("PR2", [P, NT2 * P])
        PRC = sb("PRC", [P, NT1 * P])
        SCR = sb("SCR", [P, 512])
        ONES = sb("ONES", [P, P])
        MODS = sb("MODS", [P, DEPTH2 * 6 * KD, 2])
        GM = sb("GM", [P, KD, 2])
        epsc = sb("epsc", [P, 1])
        SC = sb("SC", [P, KD, 2])
        MROW1 = X[:, 0:2, T1:T2]
        MROW2 = SCR[:, :].rearrange("p (c t) -> p c t", c=2)
        PS = stack.enter_context(nc.psum_tensor("PS", [P, 8, 512], F32))

        def alias(name, host, at, shape):
            return nc.alloc_sbuf_tensor_at(name, shape, F32R, offset=place[host] + 4 * at)

        WRAW = RING[:, 0:2, :].rearrange("p a (b k n) -> p (a b) k n", b=2, k=KD)
        WH = alias("W_hi", "RING", 2 * 4096, [P, 4, KD, P])
        WL = alias("W_lo", "RING", 3 * 4096, [P, 4, KD, P])
        H_HI = alias("H_hi", "H", 0, [P, KD, T2])
        H_LO = alias("H_lo", "BIG", 12288, [P, KD, T2])
        HID_HI = alias("hidden_hi", "BIG", 0, [P, KD, T2])
        HID_LO = alias("hidden_lo", "BIG", 4096, [P, KD, T2])
        HNORM = BIG[:, 4096:8192].rearrange("p (c t) -> p c t", c=KD)
        RELU = BIG[:, 8192:9216].rearrange("p (c t) -> p c t", c=2)
        RELU2 = BIG[:, 9216:10240].rearrange("p (c t) -> p c t", c=2)

        def c(name):
            return CN[:, CON[name][0]:CON[name][1]]

        def v3(ap, n):
            return ap.rearrange("p (c t) -> p c t", c=n)

        ident, flip, window = c("ident"), c("flip"), c("window")
        zT = CN[0:EMB, CON["zT"][0]:CON["zT"][1]]
        COS, SIN, ICOS, ISIN = (v3(c(n), 2) for n in ("cos", "sin", "icos", "isin"))
        DECAY = v3(c("decay"), 2)
        BAND = c("band").rearrange("p (s g t) -> p s g t", s=2, g=4)

        FW1 = SM[0:EMB, 0:64]
        FW2 = SM[0:ORDER, 64:128]
        FW3 = SM[0:ORDER, 128:1152]
        GW2 = SM[0:2 * RANK, 1152:2176].rearrange("p (z d) -> p z d", z=2)
        PW = v3(SM[:, 2176:2688], 4)
        LRW = v3(SM[:, 2688:2944], KD)
        LR = SM[0:2 * RANK, 2944:3200]

        U = v3(BIG[:, 0:3072], 12)
        Q = v3(BIG[:, 3072:4096], 4)
        K = v3(BIG[:, 4096:5120], 4)
        G = v3(BIG[:, 5120:6144], 4)
        V = v3(BIG[:, 6144:7168], 2)
        UP = v3(BIG[:, 7168:8192], 2)
        YP = v3(BIG[:, 7168:8192], 4)
        W = BIG[:, 8192:16384]
        RAW = v3(W[:, 6144:7168], 4)
        HF, HB, FA, FB = (v3(W[:, i * 1024:(i + 1) * 1024], 2) for i in range(4))
        FARG = W[0:ORDER, 4096:4352]
        FK = W[0:ORDER, 4352:4608]
        H1 = W[0:ORDER, 4608:4864]
        KA = H[:, 0:4, T1:T2]
        KB = H[:, 4:8, T1:T2]
        ZV = v3(W[:, 0:1024], 4)
        ZT = v3(W[:, 1024:2048], 2)
        ZC = v3(W[:, 2048:3072], 4)
        ZS = v3(W[:, 3072:4096], 4)
        PP = v3(W[:, 4096:5120], 4)
        RR = v3(W[:, 5120:6144], 4)
        TMP = v3(W[:, 1024:2048], 4)
        DP = v3(W[:, 7168:8192], 4)
        X1, B1 = W[:, 0:1024], W[:, 1024:2048]
        E1, KE, QE = W[:, 2048:3072], W[:, 3072:4096], W[:, 4096:5120]
        SCO, KT = W[:, 5120:6144], W[:, 6144:7168]
        ST = [W[:, 1024:1536], W[:, 1536:2048], W[:, 7168:7680]]
        OG = BIG[:, 1024:2048]
        GT = v3(W[:, 0:6144], 24)
        MG = v3(W[:, 6144:8192], 8)
        Y1 = v3(BIG[:, 0:2048], KD)
        SQ1 = v3(BIG[:, 14336:16384], KD)
        FT = v3(BIG[:, 0:NFF * T1], NFF)
        FRAW = v3(BIG[:, 11264:12288], 4)
        Y2 = v3(BIG[:, 12288:14336], KD)

        RT2, RS2, MU = CN[:, CON2:CON2 + 512], CN[:, CON2 + 512:CON2 + 1024], CN[:, CON2 + 1024:CON2 + 1536]
        QT = v3(BIG[:, 0:4096], KD)
        KT2 = v3(BIG[:, 4096:8192], KD)
        VT = v3(BIG[:, 8192:12288], 4)
        SQ2 = v3(BIG[:, 8192:12288], KD)
        BI = [SM[:, 512 * j:512 * j + 512].rearrange("p (t r q) -> p t r q", t=2, r=ROWS) for j in range(2)]
        PB = [SM[:, 1024:1536], SM[:, 1536:2048], CN[:, CON2 + 1536:CON2 + 2048]]
        PT = [v3(SM[:, 2048 + 512 * j:2560 + 512 * j], 4) for j in range(2)]
        MX = SM[:, 3072:3200].rearrange("p (u c) -> p u c", c=2)
        UA = v3(BIG[:, 0:4096], KD)
        UPAD = BIG[:, 4096:4096 + KD * 2 * 286].rearrange("p (c h t) -> p c h t", c=KD, h=2)
        CV = v3(BIG[:, 8704:12800], KD)
        XC = v3(BIG[:, 4096:8192], KD)
        BG, CG, SY = (v3(BIG[:, 4096 * i:4096 * i + 4096], KD) for i in range(3))

        s_x, s_ctx, s_con, s_tab = sem("x_loaded"), sem("ctx_loaded"), sem("consts_loaded"), sem("tables_loaded")
        sq2_ready = sem("squares_by_pair")
        s_con2 = sem("spectral_consts_loaded")
        s_filt, s_small = sem("filter_weights_loaded"), sem("small_weights_loaded")
        s_slab = [sem(f"slab_loaded_{i}") for i in range(4)]
        slab_done = sem("slab_done")
        dve_step, act_step = sem("dve_step"), sem("act_step")
        ones_set, tab_full, tab_out = sem("ones_set"), sem("table_turned"), sem("table_in_place")
        x_new = sem("x_new")
        sq_ready, stat_full, root_ready, h_ready = sem("squares"), sem("sums"), sem("roots"), sem("h_chunks")
        prm_ready = sem("layer_params")

        def stage(name, slabs, per, banks, split=None):
            return Linear(sem(name + "_full"), sem(name + "_out"), slabs[0], slabs[1], per, banks,
                          split, None if split is None else sem(name + "_out_by_vector"))

        LO, HI = (0, 1, 2, 3), (4, 5, 6, 7)
        L1 = {"u": stage("u", SL1["u"], 4, LO), "q": stage("q", SL1["q"], 4, HI), "k": stage("k", SL1["k"], 4, LO),
              "v": stage("v", SL1["v"], 2, HI), "g": stage("g", SL1["g"], 4, LO),
              "pool": stage("pool", SL1["pool"], 2, HI), "gates": stage("gates", SL1["gates"], 4, HI),
              "branch": stage("branch", SL1["branch"], 8, LO), "w_out": stage("w_out", SL1["w_out"], 2, HI),
              "up": stage("up", SL1["up"], 4, LO, NFF), "down": stage("down", SL1["down"], 1, LO)}
        L2 = {"qkv": stage("qkv", (0, 6), 4, LO, 16),
              "wo": stage("wo", (0, 2), 4, LO), "cv1": stage("cv1", (0, 4), 4, LO),
              "cv2": stage("cv2", (0, 2), 4, LO), "sc1": stage("sc1", (0, 6), 4, LO, 16),
              "sc2": stage("sc2", (0, 2), 4, HI)}
        stages = list(L1.values()) + list(L2.values())

        filt_full, filt_out = sem("filter_psum"), sem("filter_sbuf")
        sin_arg, sin_out = sem("sine_arguments"), sem("sines")
        kern_full, kern_out = sem("kernel_spectrum_psum"), sem("kernel_spectrum")
        conv_u, conv_f = sem("u_convolved"), sem("ffn_convolved")
        zv_ready, zt_full, zt_out = sem("zv_ready"), sem("zv_turned_psum"), sem("zv_turned")
        zf_full, zf_out, prod_ready = sem("spectrum_psum"), sem("spectrum"), sem("spectra_product")
        hy_full, hy_out = sem("hyena_psum"), sem("hyena_out")
        pd_full, pd_out, pw_full, pw_out = sem("pool_diff_psum"), sem("pool_diff"), sem("pool_psum"), sem("pooled_out")
        lr_full, lr_out = sem("lowrank_psum"), sem("lowrank")
        gk_full, gk_out, ls_ready = sem("gate_psum"), sem("gate_logits"), sem("log_sigmoid_part")
        cum_ready, exp_ready, qk_ready = sem("log_decay_sums"), sem("decay_exps"), sem("decayed_qk")
        sco_full, sco_out = sem("gla_scores_psum"), sem("gla_scores")
        kt_full, kt_out = sem("gla_k_turned_psum"), sem("gla_k_turned")
        st_full, st_out = sem("gla_state_psum"), sem("gla_states")
        og_full, og_out = sem("gla_o_psum"), sem("gla_o")
        gsq, gst_full, groot, gla_done = sem("gla_squares"), sem("gla_sums"), sem("gla_roots"), sem("gla_done")
        gelu_out, ffn_hid = sem("gelu_out"), sem("ffn_hidden")
        mod_row, mod_turned, mod_out, silu_c = sem("mod_row"), sem("mod_turned"), sem("mod_vectors"), sem("silu_c")
        w_raw = [sem(f"raw_weights_{i}") for i in range(4)]
        w_hi, w_lo, w_used = sem("weights_hi"), sem("weights_lo"), sem("product_done")
        h_lo, hid_relu, hid_sq, hid_hi, hid_lo, down_out = (sem("h_lo"), sem("relu"), sem("relu_squared"), sem("hidden_hi_done"),
                                                  sem("hidden_lo_done"), sem("down_added"))
        bias_loaded = [sem("bias_loaded_0"), sem("bias_loaded_1")]
        bias_ready = sem("bias_masked")
        sc_full, max_ready, p_exp, p_norm = sem("scores"), sem("row_maxima"), sem("exps"), sem("probs")
        pt_full, pt_out, o_full, o_out = sem("probs_turned_psum"), sem("probs_turned"), sem("attn_psum"), sem("attn")
        o_hi = sem("attn_hi")
        cv_u, cv_dw, mu_full, mu_out = sem("conformer_gated"), sem("conformer_conv"), sem("mean_psum"), sem("means")
        xc_ready, cv_sq, cv_stat, cv_root = sem("centred"), sem("cv_squares"), sem("cv_sums"), sem("cv_roots")
        cv_norm, cv_act = sem("cv_normed"), sem("cv_activated")
        pad_set, sg_ready = sem("pads_zeroed"), sem("conformer_gates")
        sc_bg, mix_hi, mix_lo = sem("short_conv_gated"), sem("mixed_hi"), sem("mixed_lo")
        stored = sem("stored")
        h_shift = sem("h_modulated")

        def finished(eng, L, uses, before, i4, u, cc):
            if cc == L.per - 1:
                eng.wait_ge(slab_done, before + L.slab0 + i4 + u + 1 + CREDIT)
            else:
                eng.wait_ge(L.full, uses * (L.slabs * (L.per - 1)) + (i4 + u) * (L.per - 1) + cc + 1)

        blk = stack.enter_context(nc.Block())

        def slab(s, k, n):
            return RING[:, s % 4, 0:k * n].rearrange("p (k n) -> p k n", k=k)

        def tiles(a):
            return (0, 1, 2, 3) if a == 0 else (0, 1)

        def first_unit(a, h):
            return h * len(tiles(a))

        def unit0(a):
            return a * HEADS2 * 4

        def stat_bank(l, second):
            return 3 if (l % 3 == 2 if second else l > 0) else 7

        def bank(L, e):
            return PS[:, L.banks[e % 4]]

        @blk.sync
        def _(sp):
            cut = CON["cos"][0]
            sp.dma_start(v3(BIG[:, 0:512], 4), prm1.rearrange("t r f -> r t f")).then_inc(s_tab, 16)
            sp.dma_start(v3(BIG[:, 512:1152], 5), prm2.rearrange("t r f -> r t f")).then_inc(s_tab, 16)
            sp.dma_start(CN[:, 0:cut], con[:, 0:cut]).then_inc(s_con, 16)
            sp.dma_start(X[:, :, 0:T1], x.rearrange("(c p) t -> p c t", p=P)).then_inc(s_x, 16)
            sp.dma_start(CN[:, cut:NCON], con[:, cut:NCON]).then_inc(s_con2, 16)

            def load(s, dst, src, before4):
                sp.wait_ge(slab_done, before4 + s + 1)
                sp.dma_start(dst, src).then_inc(s_slab[s % 4], 16)

            def rows(a):
                return a.rearrange("l (k p) n -> l p k n", p=P)

            w_in, w_outs, up, down = rows(w["w_in"]), rows(w["w_out"]), rows(w["ffn_w_up"]), rows(w["ffn_w_down"])
            modw = rows(w["mod_w_2"])
            with sp.Fori(0, DEPTH1) as lay:
                base = lay * PER1

                def mod(j):
                    load(MOD1[j], slab(MOD1[j], KD, 512), modw[lay, :, :, 512 * j:512 * j + 512], base)

                mod(0)
                mod(1)
                for s, col in enumerate((C_U, C_U + 512, C_U + 1024, C_Q, C_K, C_V, C_G, C_POOL)):
                    load(s + 2, slab(s + 2, KD, 512), w_in[lay, :, :, col:col + 512], base)
                for j in range(2, 8):
                    mod(j)
                for j in range(6):
                    s = SL1["gates"][0] + j
                    load(s, slab(s, KD, 512), w_in[lay, :, :, C_GATE + 512 * j:C_GATE + 512 * j + 512], base)
                for j, n in enumerate(("w_br_hyena", "w_br_gla", "w_br_pool")):
                    s = SL1["branch"][0] + j
                    load(s, slab(s, 4, D), rows(w[n])[lay], base)
                for j in range(4):
                    s = SL1["w_out"][0] + j
                    load(s, slab(s, KD, 256), w_outs[lay, :, :, 256 * j:256 * j + 256], base)
                mod(8)
                mod(9)
                for j in range(11):
                    s = SL1["up"][0] + j
                    load(s, slab(s, KD, 512), up[lay, :, :, 512 * j:512 * j + 512], base)
                with sp.Fori(0, 2) as i:
                    for u in range(4):
                        sp.wait_ge(slab_done, base + SL1["down"][0] + i * 4 + u + 1)
                        s = SL1["down"][0] + u
                        sp.dma_start(slab(s, NFF, P), down[lay, :, :, bass.ds(i * 512 + u * P, P)]
                                     ).then_inc(s_slab[s % 4], 16)
                mod(10)
                mod(11)

            m1, m2 = rows(w["mlp_w1_2"]), rows(w["mlp_w2_2"])
            base = BEFORE2

            def block(n, src):
                sp.wait_ge(w_lo, n + 2)
                sp.dma_start(WRAW[:, n // 2 % 4], src).then_inc(w_raw[n // 2 % 4], 16)

            def columns(n, src):
                for j in range(src.shape[-1] // (2 * P)):
                    block(n + 2 * j, src[:, :, 2 * P * j:2 * P * j + 2 * P])

            sp.wait_ge(slab_done, base + 2)
            for l in range(DEPTH2):
                n = N_MIX[l]
                if l % 3 == 0:
                    columns(n, rows(w["na_wqkv_2"])[l // 3])
                    columns(n + 24, rows(w["na_wo_2"])[l // 3])
                elif l % 3 == 1:
                    columns(n, rows(w["cv_w1_2"])[0])
                    sp.wait_ge(w_lo, SPLIT_CREDIT + n + 16)
                    for m in range(2):
                        with sp.Fori(0, 3) as i:
                            for u in range(4):
                                if m == 0 and u == 2:
                                    sp.wait_ge(w_used, CREDIT + n + 16)
                                sp.wait_ge(slab_done, base + m * MODP + i * 4 + u + 1)
                                sp.dma_start(slab(u, KD, 512), modw[2 + m][:, :, bass.ds(i * 2048 + u * 512, 512)]
                                             ).then_inc(s_slab[u], 16)
                    sp.wait_ge(slab_done, base + MOD2 + 2)
                    columns(n + 16, rows(w["cv_w2_2"])[0])
                else:
                    columns(n, rows(w["sc_win_2"])[0])
                    columns(n + 24, rows(w["sc_wout_2"])[0])
                with sp.Fori(0, QUARTERS) as q:
                    for r in range(PROD_Q // 2):
                        sp.wait_ge(w_lo, q * PROD_Q + (N_MLP[l] + 2 * r + 2))
                        if r < KD // 2:
                            src = m1[l][:, :, bass.ds(q * D + 2 * P * r, 2 * P)]
                        else:
                            src = m2[l][:, bass.ds(q * KD, KD), 2 * P * (r - KD // 2):2 * P * (r - KD // 2 + 1)]
                        sp.dma_start(WRAW[:, r % 4], src).then_inc(w_raw[r % 4], 16)
            sp.wait_ge(h_ready, 8 * (2 * DEPTH1 + 2 * DEPTH2 + 1))
            sp.dma_start(out.rearrange("(c p) t -> p c t", p=P), H[:, :, 0:T1]).then_inc(stored, 16)
            sp.wait_ge(stored, 16)

        @blk.gpsimd
        def _(gp):
            for st in stages:
                gp.sem_inc(st.out, CREDIT)
            for s in (slab_done, conv_u, conv_f):
                gp.sem_inc(s, CREDIT)
            gp.sem_inc(mod_out, 1)
            for s, n in ((w_lo, SPLIT_CREDIT), (w_used, CREDIT), (hid_relu, CREDIT), (hid_lo, HID_CREDIT),
                         (down_out, DOWN_CREDIT)):
                gp.sem_inc(s, n)
            nc.gpsimd.memset(GW2, 0.0).then_inc(ones_set, 1)
            nc.gpsimd.memset(ONES[:, :], 1.0).then_inc(ones_set, 1)
            nc.gpsimd.memset(epsc[:, :], EPS).then_inc(ones_set, 1)
            nc.gpsimd.memset(MROW1, 0.0).then_inc(ones_set, 1)
            gp.wait_ge(ones_set, 4)
            gp.sem_inc(gla_done, 1)
            with gp.Fori(0, DEPTH1) as lay:
                gp.wait_ge(gla_done, lay + 1)
                for i, (dst, src) in enumerate(((FW1, w["hy_filt_w1"][lay]), (FW2, w["hy_filt_w2"][lay]), (FW3, w["hy_filt_w3"][lay]),
                                 (GW2[0:RANK, 0, :], w["gla_gate_w2"][lay, 0]),
                                 (GW2[RANK:2 * RANK, 1, :], w["gla_gate_w2"][lay, 1]),
                                 (PW, w["pool_w"].rearrange("l g c d -> l c g d")[lay]),
                                 (LRW, w["w_in"].rearrange("l (k p) n -> l p k n", p=P)[lay, :, :, C_LR:C_LR + 2 * RANK]))):
                    gp.dma_start(dst, src).then_inc(s_filt if i < 3 else s_small, 16)
            gp.wait_ge(x_new, 1 + 2 * DEPTH1)
            gp.wait_ge(mod_out, 2 * MODP + 1)
            gp.dma_start(X[:, :, T1:T2], ctx_in.rearrange("(c p) t -> p c t", p=P)).then_inc(s_ctx, 16)
            rpb = w["na_rpb_2"]
            for a in range(2):
                if a == 1:
                    gp.wait_ge(x_new, 1 + 2 * DEPTH1 + 6)
                for h in range(HEADS2):
                    n = a * HEADS2 + h
                    if h >= 2:
                        gp.wait_ge(sc_full, unit0(a) + first_unit(a, h - 1))
                    elif a == 1:
                        gp.wait_ge(sc_full, unit0(1))
                    for t in range(2):
                        for r in range(2):
                            off = (a * HEADS2 + h) * RPB_R * RPB_C + (6 - 2 * t) * RPB_C - 48 + RPB_C * r
                            src = bass.AP(rpb.tensor, off, [[1, GRID], [RPB_C, ROWS], [1, GRID]])
                            gp.dma_start(BI[h % 2][GRID * r:GRID * r + GRID, t], src).then_inc(bias_loaded[h % 2], 16)
                    gp.wait_ge(bias_loaded[h % 2], 64 * (n // 2 + 1))
                    for t in range(2):
                        mk = nc.gpsimd.tensor_tensor(BI[h % 2][:, t], BI[h % 2][:, t],
                                                     window.rearrange("p (o q) -> p o q", o=1)
                                                     .to_broadcast([P, ROWS, GRID]), ALU.add)
                    mk.then_inc(bias_ready, 1)

        @blk.tensor
        def _(pe):
            def chain(dst, pairs):
                n = len(pairs)
                for i, (a, b) in enumerate(pairs):
                    mm = pe.matmul(dst, a, b, start=i == 0, stop=i == n - 1)
                return mm

            def product(L, uses, before, i4, u, cc, dst, pairs):
                s = L.slab0 + u
                if cc == 0:
                    pe.wait_ge(s_slab[s % 4], before * 4 + i4 * 4 + 16 * (s // 4 + 1))
                L.wait_bank(pe, uses, i4, u * L.per + cc)
                mm = chain(dst, pairs)
                if cc == L.per - 1:
                    mm.then_inc(slab_done, 1)
                else:
                    mm.then_inc(L.full, 1)

            def linear(L, uses, before, rhs, k, n, T, i4=0, us=None, first=None):
                for u in (range(L.slabs) if us is None else us):
                    ws = slab(L.slab0 + u, k, n)
                    for cc in range(L.per):
                        product(L, uses, before, i4, u, cc, bank(L, u * L.per + cc)[:, 0:T],
                                [(ws[:, kk, P * cc:P * cc + P], rhs(kk)) for kk in range(k)])

            def first_products(dsts, ns, x_hi, x_lo, T, hi_wait, lo_wait):
                for k in range(KD):
                    hi_wait(k)
                    for dst, n in zip(dsts, ns):
                        pe.matmul(dst, WH[:, n % 4, k, :], x_hi[:, k, 0:T], start=k == 0, stop=False)
                        pe.matmul(dst, WL[:, n % 4, k, :], x_hi[:, k, 0:T], start=False, stop=False)
                for i, (dst, n) in enumerate(zip(dsts, ns)):
                    for k in range(KD):
                        if i == 0:
                            lo_wait(k)
                        mm = pe.matmul(dst, WH[:, n % 4, k, :], x_lo[:, k, 0:T], start=False, stop=k == KD - 1)
                    mm.then_inc(w_used, 1)

            def split_start(L, uses, n, T, x_hi, x_lo, hi_wait, lo_wait):
                pe.wait_ge(w_lo, n + AHEAD + SPLIT_CREDIT)
                L.wait_bank(pe, uses, 0, AHEAD - 1)
                first_products([bank(L, e)[:, 0:T] for e in range(AHEAD)], range(n, n + AHEAD), x_hi, x_lo, T,
                               hi_wait, lo_wait)

            def split_product(L, uses, n, e, T, x_hi, x_lo):
                pe.wait_ge(w_lo, n + 1 + SPLIT_CREDIT)
                L.wait_bank(pe, uses, 0, e)
                for k in range(KD):
                    for i, (wt, xt) in enumerate(((WH, x_hi), (WH, x_lo), (WL, x_hi))):
                        mm = pe.matmul(bank(L, e)[:, 0:T], wt[:, n % 4, k, :], xt[:, k, 0:T],
                                       start=k == 0 and i == 0, stop=k == KD - 1 and i == 2)
                mm.then_inc(w_used, 1)

            def norm_sums(n, sq, T):
                for half in range(2):
                    pe.wait_ge(sq_ready, n * 2 + half + 1)
                    for kk in range(4 * half, 4 * half + 4):
                        mm = pe.matmul(PS[:, 7, 0:T], ONES[:, :], sq[:, kk, 0:T], start=kk == 0, stop=kk == 7)
                mm.then_inc(stat_full, 1)

            def norm_sums2(n, T, b):
                for i in range(4):
                    pe.wait_ge(sq2_ready, (n - 4 * DEPTH1) * 4 + i + 1)
                    for kk in (2 * i, 2 * i + 1):
                        mm = pe.matmul(PS[:, b, 0:T], ONES[:, :], SQ2[:, kk, 0:T], start=kk == 0, stop=kk == 7)
                mm.then_inc(stat_full, 1)

            def mod_piece(pos, before, p, row, i4=0):
                pe.wait_ge(s_slab[pos % 4], before * 4 + i4 * 4 + 16 * (pos // 4 + 1))
                pe.wait_ge(mod_out, p + 1)
                ws = slab(pos, KD, 512)
                chain(PS[0:2, 3, :], [(SC[:, kk, :], ws[:, kk, :]) for kk in range(KD)]).then_inc(slab_done, 1)
                pe.wait_ge(mod_row, p + 1)
                for j in range(4):
                    tr = pe.transpose(PS[:, 3, P * j:P * j + P], row[:, j // 2, P * (j % 2):P * (j % 2) + P], ident)
                tr.then_inc(mod_turned, 1)

            pe.wait_ge(s_tab, 32)
            pe.wait_ge(s_con, 16)
            pe.wait_ge(ones_set, 4)
            for t in range(2 * NT1 + NT2):
                tr = pe.transpose(PS[:, t // 4, P * (t % 4):P * (t % 4) + P], BIG[:, P * t:P * t + P], ident)
            tr.then_inc(tab_full, 1)
            pe.wait_ge(tab_out, 1)

            with pe.Fori(0, DEPTH1) as lay:
                before = lay * PER1
                pe.wait_ge(s_filt, lay * 48 + 48)
                pe.wait_ge(prm_ready, lay + 1)
                pe.matmul(PS[:, 0, 0:SEQ], SM[0:EMB, 0:P], zT, start=True, stop=True).then_inc(filt_full, 1)
                pe.wait_ge(sin_out, lay * 2 + 1)
                pe.matmul(PS[:, 1, 0:SEQ], SM[0:ORDER, 64:64 + P], H1, start=True, stop=True).then_inc(filt_full, 1)
                pe.wait_ge(sin_out, lay * 2 + 2)
                for half in range(2):
                    for tt in range(2):
                        pe.matmul(PS[:, 2 * half + tt], H1[:, P * tt:P * tt + P], FW3[:, 512 * half:512 * half + 512],
                                  start=True, stop=True).then_inc(filt_full, 1)
                pe.wait_ge(filt_out, lay + 1)
                pe.wait_ge(s_con2, 16)
                for j, (m, src) in enumerate(((COS, FA), (SIN, FB))):
                    for f in range(2):
                        chain(PS[:, 4 + 2 * j + f], [(m[:, ss, P * f:P * f + P], src[:, ss, :]) for ss in range(2)]
                              ).then_inc(kern_full, 1)
                mod1 = lambda *js: [mod_piece(MOD1[j], before, lay * MODP + j, MROW1) for j in js]
                pe.wait_ge(silu_c, 1)
                mod1(0, 1)
                pe.wait_ge(kern_out, lay * 4 + 4)

                norm_sums(lay * 4, SQ1, T1)
                pe.wait_ge(h_ready, lay * 16 + 8)
                rhs = lambda kk: H[:, kk, 0:T1]
                pe.wait_ge(mod_out, lay * MODP + 3)
                pe.wait_ge(s_small, lay * 64 + 64)
                linear(L1["u"], lay, before, rhs, KD, 512, T1)
                linear(L1["q"], lay, before, rhs, KD, 512, T1)
                L1["u"].wait_all_out(pe, lay)
                linear(L1["k"], lay, before, rhs, KD, 512, T1)
                L1["q"].wait_all_out(pe, lay)
                for tt in range(2):
                    product(L1["v"], lay, before, 0, 0, tt, bank(L1["v"], tt),
                            [(H[:, kk, P * tt:P * tt + P], slab(L1["v"].slab0, KD, 512)[:, kk, :]) for kk in range(KD)])
                L1["k"].wait_all_out(pe, lay)
                linear(L1["g"], lay, before, rhs, KD, 512, T1)
                chain(PS[0:2 * RANK, 6, 0:T1], [(LRW[:, kk, :], rhs(kk)) for kk in range(KD)]).then_inc(lr_full, 1)
                L1["v"].wait_all_out(pe, lay)
                for tt in range(2):
                    product(L1["pool"], lay, before, 0, 0, tt, bank(L1["pool"], tt),
                            [(H[:, kk, P * tt:P * tt + P], slab(L1["pool"].slab0, KD, 512)[:, kk, :]) for kk in range(KD)])

                L1["pool"].wait_all_out(pe, lay)
                L1["g"].wait_all_out(pe, lay)
                for g in range(4):
                    chain(PS[:, g, 0:T1], [(UP[:, ss, P * g:P * g + P], BAND[:, ss, g, :]) for ss in range(2)]
                          ).then_inc(pd_full, 1)
                for g in range(4):
                    pe.wait_ge(pd_out, lay * 4 + g + 1)
                    pe.matmul(PS[:, 4 + g, 0:T1], PW[:, g, :], DP[:, g, :], start=True, stop=True).then_inc(pw_full, 1)

                pe.wait_ge(zv_ready, lay + 1)
                for ss in range(2):
                    for j in range(4):
                        tr = pe.transpose(PS[:, ss, P * j:P * j + P], ZV[:, j, P * ss:P * ss + P], ident)
                    tr.then_inc(zt_full, 1)
                pe.wait_ge(zt_out, lay * 2 + 2)
                pe.wait_ge(pw_out, lay * 4 + 4)
                for j, m in enumerate((COS, SIN)):
                    for f in range(2):
                        chain(PS[:, 4 + 2 * j + f], [(m[:, ss, P * f:P * f + P], ZT[:, ss, :]) for ss in range(2)]
                              ).then_inc(zf_full, 1)
                pe.wait_ge(prod_ready, lay + 1)
                P2 = W[:, 4096:5120].rearrange("p (f n) -> p f n", f=2)
                R2 = W[:, 5120:6144].rearrange("p (f n) -> p f n", f=2)
                for j in range(4):
                    chain(PS[:, j, 0:T1], [(P2[:, f, P * j:P * j + P], ICOS[:, f, :]) for f in range(2)]
                          + [(R2[:, f, P * j:P * j + P], ISIN[:, f, :]) for f in range(2)]).then_inc(hy_full, 1)

                pe.wait_ge(lr_out, lay + 1)
                for z in range(2):
                    zz = lay * 2 + z
                    pe.wait_ge(zf_out, lay * 4 + 4) if z == 0 else pe.wait_ge(sco_out, lay * 4 + 2)
                    for j in range(4):
                        mm = pe.matmul(PS[:, 4 + j // 2, T1 * (j % 2):T1 * (j % 2) + T1],
                                       GW2[:, z, P * j:P * j + P], LR, start=True, stop=True)
                        if j % 2:
                            mm.then_inc(gk_full, 1)
                    if z == 0:
                        pe.wait_ge(hy_out, lay * 4 + 4)
                    mod1(*((2, 3) if z == 0 else (5, 6)))
                    pe.wait_ge(qk_ready, zz + 1)
                    for b in range(2):
                        for j in range(4):
                            h, tt = 2 * b + j // 2, j % 2
                            o = T1 * h + P * tt
                            mm = pe.matmul(PS[:, 4 + b, P * j:P * j + P], KE[:, o:o + P], QE[:, o:o + P],
                                           start=True, stop=True)
                        mm.then_inc(sco_full, 1)
                    if z == 1:
                        pe.wait_ge(og_out, lay * 4 + 2)
                    for b in range(2):
                        for j in range(4):
                            o = 512 * b + P * j
                            tr = pe.transpose(PS[:, 6 + b, P * j:P * j + P], X1[:, o:o + P], ident)
                        tr.then_inc(kt_full, 1)
                    if z == 0:
                        mod1(4)
                    pe.wait_ge(kt_out, zz * 2 + 2)
                    for i, n in enumerate((0, 1, 2) if z == 0 else (3, 2, 1)):
                        r = GLA_C * (n % 2)
                        for h in range(HEADS1):
                            o = T1 * h + P * (n // 2)
                            mm = pe.matmul(PS[:, i, P * h:P * h + P], KT[r:r + GLA_C, o:o + P],
                                           V[r:r + GLA_C, n // 2, P * h:P * h + P], start=True, stop=True)
                        mm.then_inc(st_full, 1)
                    pe.wait_ge(sco_out, zz * 2 + 2)
                    pe.wait_ge(st_out, zz + 1)
                    for b in range(2):
                        for h in (2 * b, 2 * b + 1):
                            for n in range(4):
                                o = T1 * h + GLA_C * n
                                dst = PS[:, 6 + b, T1 * (h % 2) + GLA_C * n:T1 * (h % 2) + GLA_C * n + GLA_C]
                                pairs = [(V[:, n // 2, P * h:P * h + P], SCO[:, o:o + GLA_C])]
                                i = n - 1 if z == 0 else 2 - n
                                if i >= 0:
                                    pairs.append((ST[i][:, P * h:P * h + P], QE[:, o:o + GLA_C]))
                                mm = chain(dst, pairs)
                        mm.then_inc(og_full, 1)
                mod1(7)
                pe.wait_ge(gsq, lay + 1)
                for b in range(2):
                    for h in (2 * b, 2 * b + 1):
                        mm = pe.matmul(PS[:, 4 + b, T1 * (h % 2):T1 * (h % 2) + T1], ONES[:, :],
                                       W[:, T1 * h:T1 * h + T1], start=True, stop=True)
                    mm.then_inc(gst_full, 1)

                pe.wait_ge(gla_done, lay + 2)
                pe.wait_ge(mod_out, lay * MODP + 9)
                linear(L1["gates"], lay, before, rhs, KD, 512, T1)
                L1["gates"].wait_all_out(pe, lay)
                for j, ys in enumerate((U, Q, YP)):
                    linear(L1["branch"], lay, before, lambda kk, ys=ys: ys[:, kk, :], 4, D, T1, us=(j,))
                L1["branch"].wait_all_out(pe, lay)
                linear(L1["w_out"], lay, before, lambda kk: MG[:, kk, :], KD, 256, T1)
                L1["w_out"].wait_all_out(pe, lay)
                mod1(8)
                norm_sums(lay * 4 + 1, SQ1, T1)
                mod1(9)

                norm_sums(lay * 4 + 2, SQ1, T1)
                pe.wait_ge(h_ready, lay * 16 + 16)
                pe.wait_ge(mod_out, lay * MODP + 11)
                linear(L1["up"], lay, before, rhs, KD, 512, T1)
                with pe.Fori(0, 2) as i:
                    L1["up"].wait_all_out(pe, lay)
                    linear(L1["down"], lay, before, lambda kk: FT[:, kk, :], NFF, P, T1, i4=i * 4, us=range(4))
                L1["down"].wait_all_out(pe, lay)
                mod1(10)
                norm_sums(lay * 4 + 3, SQ1, T1)
                mod1(11)
                pe.wait_ge(mod_out, lay * MODP + 13)

            nn = 4 * DEPTH1
            for l in range(DEPTH2):
                n0 = N_MIX[l]
                T = T2 if l < DEPTH2 - 1 else T1
                norm_sums2(nn, T2, stat_bank(l, 0))
                nn += 1
                h_waits = (lambda k: pe.wait_ge(h_shift, KD * 2 * l + k + 1),
                           lambda k: pe.wait_ge(h_lo, KD * 2 * l + k + 1))
                if l % 3 == 0:
                    a = l // 3
                    split_start(L2["qkv"], a, n0, T, H_HI, H_LO, *h_waits)
                    for e in range(AHEAD, 16):
                        split_product(L2["qkv"], a, n0 + e, e, T if e < 8 else T2, H_HI, H_LO)
                    for pair in range(4):
                        n = n0 + 16 + 2 * pair
                        pe.wait_ge(w_lo, n + 2 + SPLIT_CREDIT)
                        sl = n % 4
                        for tt in range(4):
                            e = 16 + 2 * pair + tt // 2
                            if tt % 2 == 0:
                                L2["qkv"].wait_bank(pe, a, 0, e)
                            mm = chain(bank(L2["qkv"], e)[:, SEQ * (tt % 2):SEQ * (tt % 2) + SEQ],
                                       [(xt[:, k, P * tt:P * tt + P], wt[:, sl:sl + 2, k, :]) for k in range(KD)
                                        for wt, xt in ((WH, H_HI), (WL, H_HI), (WH, H_LO))])
                        mm.then_inc(w_used, 2)
                    L2["qkv"].wait_all_out(pe, a)

                    units = [(h, t) for h in range(HEADS2) for t in tiles(a)]
                    def scores(n):
                        h, t = units[n]
                        g = unit0(a) + n
                        r = HD * (h % 2)
                        dst = PS[:, n % 3]
                        if n >= 3:
                            pe.wait_ge(p_exp, g - 2)
                        q = QT[r:r + HD, h // 2, P * t:P * t + P]
                        if t < 2:
                            if t == 0:
                                pe.wait_ge(bias_ready, a * HEADS2 + h + 1)
                            pe.matmul(dst[:, 0:SEQ], flip, BI[h % 2][:, t].rearrange("p r q -> p (r q)"),
                                      start=True, stop=False)
                            pe.matmul(dst[:, 0:SEQ], q, KT2[r:r + HD, h // 2, 0:SEQ], start=False, stop=True)
                            pe.matmul(dst[:, SEQ:T2], q, KT2[r:r + HD, h // 2, SEQ:T2],
                                      start=True, stop=True).then_inc(sc_full, 1)
                        else:
                            pe.matmul(dst[:, SEQ:T2], q, KT2[r:r + HD, h // 2, SEQ:T2],
                                      start=True, stop=True).then_inc(sc_full, 1)

                    def turn(n):
                        h, t = units[n]
                        g = unit0(a) + n
                        pe.wait_ge(p_norm, g + 1)
                        if n >= 2:
                            pe.wait_ge(pt_out, g - 1)
                        for j in (range(4) if t < 2 else (2, 3)):
                            tr = pe.transpose(PS[:, 3 + n % 2, P * j:P * j + P], PB[n % 3][:, P * j:P * j + P], ident)
                        tr.then_inc(pt_full, 1)

                    def values(n):
                        h, t = units[n]
                        g = unit0(a) + n
                        r = HD * (h % 2)
                        pe.wait_ge(pt_out, g + 1)
                        if t == 0 and h % 2 == 0 and h >= 4:
                            pe.wait_ge(o_out, a * 8 + h // 2 - 1)
                        mm = chain(PS[r:r + HD, 5 + (h // 2) % 2, P * t:P * t + P],
                                   [(VT[:, j, HD * h:HD * h + HD], PT[n % 2][:, j, :])
                                    for j in (range(4) if t < 2 else (2, 3))])
                        if h % 2 and t == tiles(a)[-1]:
                            mm.then_inc(o_full, 1)

                    N = len(units)
                    for n in range(N + 3):
                        if n < N:
                            scores(n)
                        if 2 <= n <= N + 1:
                            turn(n - 2)
                        if n >= 3:
                            values(n - 3)
                    pe.wait_ge(o_out, a * 8 + 8)
                    for e in range(8):
                        split_product(L2["wo"], a, n0 + 24 + e, e, T, H_HI, H_LO)
                elif l % 3 == 1:
                    before = BEFORE2
                    split_start(L2["cv1"], 0, n0, T2, H_HI, H_LO, *h_waits)
                    for e in range(AHEAD, 16):
                        split_product(L2["cv1"], 0, n0 + e, e, T2, H_HI, H_LO)
                    pe.wait_ge(L2["cv1"].out, L2["cv1"].all_out(0))
                    for n in range(2):
                        with pe.Fori(0, 3) as i:
                            for u in range(4):
                                mod_piece(n * MODP + u, before, i * 4 + ((2 + n) * MODP + u), MROW2, i4=i * 4)
                    pe.wait_ge(mod_out, 4 * MODP + 1)
                    pe.wait_ge(cv_dw, 1)
                    chain(PS[:, 7, :], [(ONES[:, :], CV[:, kk, :]) for kk in range(KD)]).then_inc(mu_full, 1)
                    pe.wait_ge(cv_sq, 1)
                    chain(PS[:, 7, :], [(ONES[:, :], UA[:, kk, :]) for kk in range(KD)]).then_inc(cv_stat, 1)
                    split_start(L2["cv2"], 0, n0 + 16, T2, H_HI, H_LO, lambda k: pe.wait_ge(mix_hi, k + 1),
                                lambda k: pe.wait_ge(mix_lo, k + 1))
                    for e in range(AHEAD, 8):
                        split_product(L2["cv2"], 0, n0 + 16 + e, e, T2, H_HI, H_LO)
                else:
                    split_start(L2["sc1"], 0, n0, T2, H_HI, H_LO, *h_waits)
                    for e in range(AHEAD, 24):
                        split_product(L2["sc1"], 0, n0 + e, e, T2, H_HI, H_LO)
                    split_start(L2["sc2"], 0, n0 + 24, T2, HID_HI, HID_LO, lambda k: pe.wait_ge(mix_hi, KD + k + 1),
                                lambda k: pe.wait_ge(mix_lo, KD + k + 1))
                    for e in range(AHEAD, 8):
                        split_product(L2["sc2"], 0, n0 + 24 + e, e, T2, HID_HI, HID_LO)

                norm_sums2(nn, T, stat_bank(l, 1))
                nn += 1

                def feed_forward(q, ahead, products):
                    hid, n = (l * QUARTERS + ahead) * KD, N_MLP[l] + ahead * PROD_Q
                    for j in products:
                        m = j % KD
                        b, x_hi, x_lo = (LO[m % 4], H_HI, H_LO) if j < KD else (HI[m % 4], HID_HI, HID_LO)
                        pe.wait_ge(w_lo, q * PROD_Q + (n + j + 1 + SPLIT_CREDIT))
                        if j < KD:
                            pe.wait_ge(hid_relu, q * KD + (hid + m + 1))
                        else:
                            pe.wait_ge(down_out, q * KD + (hid + m + 1 + DOWN_CREDIT - 4))
                        for k in range(KD):
                            if j == KD:
                                pe.wait_ge(hid_lo, q * KD + (hid + k + 1 + HID_CREDIT))
                            for i, (wt, xt) in enumerate(((WH, x_hi), (WH, x_lo), (WL, x_hi))):
                                mm = pe.matmul(PS[:, b, 0:T], wt[:, j % 4, k, :], xt[:, k, 0:T],
                                               start=k == 0 and i == 0, stop=k == KD - 1 and i == 2)
                        mm.then_inc(w_used, 1)

                pe.wait_ge(w_lo, N_MLP[l] + AHEAD + SPLIT_CREDIT)
                pe.wait_ge(hid_relu, l * QUARTERS * KD + AHEAD)
                first_products([PS[:, LO[j], 0:T] for j in range(AHEAD)], range(N_MLP[l], N_MLP[l] + AHEAD),
                               H_HI, H_LO, T, lambda k: pe.wait_ge(h_shift, KD * (2 * l + 1) + k + 1),
                               lambda k: pe.wait_ge(h_lo, KD * (2 * l + 1) + k + 1))
                feed_forward(0, 0, range(AHEAD, PROD_Q))
                with pe.Fori(0, QUARTERS - 1) as q:
                    feed_forward(q, 1, range(PROD_Q))
            norm_sums2(nn, T1, stat_bank(DEPTH2, 0))


        def col1(name, j=0):
            return PRC[:, ROW1[name] + j:ROW1[name] + j + 1]

        def col2(name, j=0):
            return PR2[:, ROW2[name] + j:ROW2[name] + j + 1]

        @blk.scalar
        def _(act):
            A = nc.scalar.activation
            step = Links(act, act_step)

            def squares(dst, src, T):
                for half in range(2):
                    ks = slice(4 * half, 4 * half + 4)
                    A(dst[:, ks, 0:T], src[:, ks, 0:T], ACT.Square).then_inc(sq_ready, 1)

            def squares2(T, done=None, count=0):
                for i in range(4):
                    if done is not None:
                        act.wait_ge(done, count + 2 * i + 2)
                    A(SQ2[:, 2 * i:2 * i + 2, 0:T], X[:, 2 * i:2 * i + 2, 0:T], ACT.Square).then_inc(sq2_ready, 1)

            def root(n, T, dst, b=7):
                act.wait_ge(stat_full, n + 1)
                A(dst[:, 0:T], PS[:, b, 0:T], ACT.Sqrt, scale=1.0 / D, bias=epsc[:, :]).then_inc(root_ready, 1)

            def take(L, uses, before, events, put, i4=0):
                for e in events:
                    finished(act, L, uses, before, i4, e // L.per, e % L.per)
                    put(e, bank(L, e)).then_inc(L.read(e), 1)

            act.wait_ge(ones_set, 4)
            act.wait_ge(tab_out, 1)
            for j, name in enumerate(("c_2", "c_ctx_2")):
                r = ROW2[name]
                last = A(SC[:, :, j], PR2[:, r:r + KD], ACT.Silu)
            last.then_inc(silu_c, 1)

            def mod_piece(pos, before, p, row, i4=0):
                act.wait_ge(slab_done, before + i4 + pos + 1 + CREDIT)
                A(row[0:2], PS[0:2, 3, :].rearrange("p (c t) -> p c t", c=2), ACT.Copy).then_inc(mod_row, 1)

            with act.Fori(0, DEPTH1) as lay:
                before = lay * PER1
                mod1 = lambda *js: [mod_piece(MOD1[j], before, lay * MODP + j, MROW1) for j in js]
                step.base, step.n = lay * ACT_LINKS, 0
                for j in range(2):
                    act.wait_ge(sin_arg, lay * 2 + j + 1)
                    A(H1, FARG, ACT.Sin).then_inc(sin_out, 1)
                for j, dst in enumerate((KA, KB)):
                    for f in range(2):
                        act.wait_ge(kern_full, lay * 4 + 2 * j + f + 1)
                        A(dst[:, 2 * f:2 * f + 2, :], v3(PS[:, 4 + 2 * j + f], 2), ACT.Copy).then_inc(kern_out, 1)
                act.wait_ge(x_new, lay * 2 + 1)
                squares(SQ1, X, T1)
                mod1(0, 1)
                root(lay * 4, T1, SCR)

                def conv_in(raw, dst, wname, bname, n, freed, count):
                    def put(e, ps):
                        act.wait_ge(freed, lay * count + e + 1)
                        A(raw[:, e % 4, :], ps[:, 0:T1], ACT.Identity)
                        return A(dst[:, e, :], ps[:, 0:T1], ACT.Identity, scale=col1(wname, n + e), bias=col1(bname, e))
                    return put

                take(L1["u"], lay, before, range(12), conv_in(RAW, U, "hy_conv_w", "hy_conv_b", 12, conv_u, 12))
                take(L1["q"], lay, before, range(4),
                     lambda e, ps: A(Q[:, e, :], ps[:, 0:T1], ACT.Copy, scale=float(P) ** -0.5))
                take(L1["k"], lay, before, range(4), lambda e, ps: A(K[:, e, :], ps[:, 0:T1], ACT.Copy))
                take(L1["g"], lay, before, range(4), lambda e, ps: A(G[:, e, :], ps[:, 0:T1], ACT.Silu))
                act.wait_ge(lr_full, lay + 1)
                A(LR, PS[0:2 * RANK, 6, 0:T1], ACT.Copy).then_inc(lr_out, 1)
                for g in range(4):
                    act.wait_ge(pd_full, lay * 4 + g + 1)
                    A(DP[:, g, :], PS[:, g, 0:T1], ACT.Copy).then_inc(pd_out, 1)
                for j in range(4):
                    act.wait_ge(zf_full, lay * 4 + j + 1)
                    A(W[:, 2048 + 512 * j:2560 + 512 * j], PS[:, 4 + j], ACT.Copy).then_inc(zf_out, 1)
                for z in range(2):
                    zz = lay * 2 + z
                    act.wait_ge(gk_out, zz + 1)
                    step(A(B1, X1, ACT.Abs))
                    step(A(B1, B1, ACT.Exp, scale=-1.0))
                    A(B1, B1, ACT.Ln, bias=1.0).then_inc(ls_ready, 1)
                    mod1(2 if z == 0 else 5)
                    act.wait_ge(cum_ready, zz + 1)
                    A(E1, B1, ACT.Exp)
                    A(KE, B1, ACT.Exp, scale=-1.0).then_inc(exp_ready, 1)
                    mod1(3 if z == 0 else 6)
                    for b in range(2):
                        act.wait_ge(kt_full, zz * 2 + b + 1)
                        A(KT[:, 512 * b:512 * b + 512], PS[:, 6 + b], ACT.Copy).then_inc(kt_out, 1)
                    if z == 0:
                        mod1(4)
                act.wait_ge(og_out, lay * 4 + 4)
                A(W[:, 0:1024], OG, ACT.Square).then_inc(gsq, 1)
                mod1(7)
                for b in range(2):
                    act.wait_ge(gst_full, lay * 2 + b + 1)
                    A(W[:, 1024 + 512 * b:1536 + 512 * b], PS[:, 4 + b], ACT.Sqrt, scale=1.0 / P,
                      bias=epsc[:, :]).then_inc(groot, 1)
                take(L1["gates"], lay, before, range(24), lambda e, ps: A(GT[:, e, :], ps[:, 0:T1], ACT.Sigmoid))
                take(L1["w_out"], lay, before, range(8), lambda e, ps: A(Y1[:, e, :], ps[:, 0:T1], ACT.Copy))
                L1["w_out"].wait_all_out(act, lay)
                squares(SQ1, Y1, T1)
                mod1(8)
                root(lay * 4 + 1, T1, SCR)
                mod1(9)
                act.wait_ge(x_new, lay * 2 + 2)
                squares(SQ1, X, T1)
                root(lay * 4 + 2, T1, SCR)
                take(L1["up"], lay, before, range(NFF), conv_in(FRAW, FT, "ffn_conv_w", "ffn_conv_b", NFF, conv_f, NFF))
                for m in range(NFF):
                    act.wait_ge(conv_f, lay * NFF + CREDIT + m + 1)
                    A(FT[:, m, :], FT[:, m, :], ACT.Gelu).then_inc(gelu_out, 1)
                with act.Fori(0, 2) as i:
                    take(L1["down"], lay, before, range(4),
                         lambda e, ps: A(Y2[:, bass.ds(i * 4 + e, 1), :], ps[:, 0:T1].rearrange("p (o t) -> p o t", o=1),
                                         ACT.Copy), i4=i * 4)
                L1["down"].wait_all_out(act, lay)
                squares(SQ1, Y2, T1)
                mod1(10)
                root(lay * 4 + 3, T1, SCR)
                mod1(11)
                assert step.n == ACT_LINKS, step.n
            step.base, step.n = 0, ACT_LINKS * DEPTH1

            nn = 4 * DEPTH1
            norms = 0

            def split_hi(l, q, j):
                r = j // 2
                act.wait_ge(w_raw[r % 4], q * 32 + (16 * ((N_MLP[l] + j) // 8 + 1)))
                act.wait_ge(w_used, q * PROD_Q + (N_MLP[l] + j + 1))
                A(WH[:, j % 4], WRAW[:, r % 4, :, P * (j % 2):P * (j % 2) + P], ACT.Copy).then_inc(w_hi, 1)

            def split_hi_of(*products):
                for n in products:
                    act.wait_ge(w_raw[n // 2 % 4], 16 * (n // 8 + 1))
                    act.wait_ge(w_used, n + 1)
                    A(WH[:, n % 4], WRAW[:, n // 2 % 4, :, P * (n % 2):P * (n % 2) + P], ACT.Copy).then_inc(w_hi, 1)

            def take_split(L, uses, n, events, put, last=None):
                for e in events:
                    if last is None or n + e + AHEAD < last:
                        split_hi_of(n + e + AHEAD)
                    act.wait_ge(w_used, n + e + 1 + CREDIT)
                    put(e, bank(L, e)).then_inc(L.out, 1)

            def shift_hi(l, j, T):
                for k in range(KD):
                    act.wait_ge(h_ready, 8 * (2 * DEPTH1 + norms) + k + 1)
                    for s in range(T // T1):
                        ts = slice(T1 * s, T1 * s + T1)
                        last = A(H_HI[:, k, ts], HNORM[:, k, ts], ACT.Identity,
                                 bias=MODS[:, 48 * l + KD * j + k, s:s + 1])
                    last.then_inc(h_shift, 1)

            act.wait_ge(s_ctx, 16)
            act.wait_ge(slab_done, BEFORE2 + 3)
            split_hi_of(*range(AHEAD))
            for l in range(DEPTH2):
                n0 = N_MIX[l]
                T = T2 if l < DEPTH2 - 1 else T1
                if l == 0:
                    act.wait_ge(x_new, 1 + 2 * DEPTH1)
                    squares2(T2)
                else:
                    squares2(T2, down_out, DOWN_CREDIT + QUARTERS * KD * l - KD)
                root(nn, T2, RT2, stat_bank(l, 0))
                nn += 1
                act.wait_ge(mod_out, MODP * (l + 1 if l < 2 else 4) + 1)
                shift_hi(l, 0, T2)
                norms += 1
                if l % 3 == 0:
                    a = l // 3
                    L = L2["qkv"]
                    take_split(L, a, n0, range(8),
                               lambda e, ps: A(QT[:, e, 0:T], ps[:, 0:T], ACT.Copy, scale=float(HD) ** -0.5))
                    take_split(L, a, n0, range(8, 16), lambda e, ps: A(KT2[:, e - 8, :], ps, ACT.Copy))
                    split_hi_of(*range(n0 + 16 + AHEAD, n0 + 24 + AHEAD))
                    units = [(h, t) for h in range(HEADS2) for t in tiles(a)]
                    per_pair = 2 * len(tiles(a))
                    for n in range(len(units) + 4):
                        if n < len(units):
                            g = unit0(a) + n
                            lo = 0 if units[n][1] < 2 else SEQ
                            act.wait_ge(max_ready, g + 1)
                            if n >= 3:
                                act.wait_ge(pt_full, g - 2)
                            A(PB[n % 3][:, lo:T2], PS[:, n % 3, lo:T2], ACT.Exp, bias=MX[:, n, 0:1],
                              accum_out=MX[:, n, 1:2]).then_inc(p_exp, 1)
                        if 2 <= n <= len(units) + 1:
                            g = unit0(a) + n - 2
                            lo = 0 if units[n - 2][1] < 2 else 2
                            act.wait_ge(pt_full, g + 1)
                            A(PT[n % 2][:, lo:4, :], v3(PS[:, 3 + n % 2], 4)[:, lo:4, :],
                              ACT.Copy).then_inc(pt_out, 1)
                        if n >= 4 and (n - 3) % per_pair == 0:
                            k = (n - 3) // per_pair - 1
                            act.wait_ge(o_full, a * 8 + k + 1)
                            A(H_HI[:, k, 0:T], PS[:, 5 + k % 2, 0:T], ACT.Copy).then_inc(o_hi, 1)
                    split_hi_of(*range(n0 + 24 + AHEAD, n0 + 32 + AHEAD))
                elif l % 3 == 1:
                    before = BEFORE2
                    L = L2["cv1"]
                    take_split(L, 0, n0, range(8),
                               lambda e, ps: A(UA[:, e, :], ps, ACT.Identity, bias=col2("cv_b1_2", e)))
                    take_split(L, 0, n0, range(8, 16),
                               lambda e, ps: A(CV[:, e - 8, :], ps, ACT.Sigmoid, bias=col2("cv_b1_2", e)), last=n0 + 16)
                    for n in range(2):
                        with act.Fori(0, 3) as i:
                            for u in range(4):
                                mod_piece(n * MODP + u, before, None, MROW2, i4=i * 4)
                    act.wait_ge(slab_done, before + MOD2 + 3)
                    split_hi_of(*range(n0 + 16, n0 + 16 + AHEAD))
                    act.wait_ge(mu_full, 1)
                    A(MU, PS[:, 7, :], ACT.Copy, scale=1.0 / D).then_inc(mu_out, 1)
                    act.wait_ge(xc_ready, 1)
                    A(UA[:, :, :], XC[:, :, :], ACT.Square).then_inc(cv_sq, 1)
                    act.wait_ge(cv_stat, 1)
                    A(RT2, PS[:, 7, :], ACT.Sqrt, scale=1.0 / D, bias=epsc[:, :]).then_inc(cv_root, 1)
                    for k in range(KD):
                        act.wait_ge(cv_norm, k + 1)
                        A(UA[:, k, :], XC[:, k, :], ACT.Silu, bias=col2("cv_ln_b_2", k)).then_inc(cv_act, 1)
                        act.wait_ge(cv_act, k + 1)
                        A(H_HI[:, k, :], UA[:, k, :], ACT.Copy).then_inc(mix_hi, 1)
                    split_hi_of(*range(n0 + 16 + AHEAD, n0 + 24 + AHEAD))
                else:
                    L = L2["sc1"]
                    take_split(L, 0, n0, range(8), lambda e, ps: A(BG[:, e, :], ps, ACT.Copy))
                    take_split(L, 0, n0, range(8, 16), lambda e, ps: A(CG[:, e - 8, :], ps, ACT.Copy))
                    for m in range(KD):
                        split_hi_of(n0 + 16 + m + AHEAD)
                        act.wait_ge(sc_bg, m + 1)
                        A(HID_HI[:, m, :], SY[:, m, :], ACT.Copy).then_inc(mix_hi, 1)
                    split_hi_of(*range(n0 + 24 + AHEAD, n0 + 32 + AHEAD))
                L = L2[("wo", "cv2", "sc2")[l % 3]]
                squares2(T, L.out, CREDIT + KD * (l // 3))
                root(nn, T, RT2, stat_bank(l, 1))
                nn += 1
                shift_hi(l, 3, T)
                norms += 1

                def quarter(q, more):
                    hid = l * QUARTERS * KD
                    for j in range(PROD_Q):
                        if j < KD:
                            act.wait_ge(w_used, q * PROD_Q + (N_MLP[l] + j + 1 + CREDIT))
                            act.wait_ge(hid_lo, q * KD + (hid + j + 1))
                            A(RELU[:, j % 2, 0:T], PS[:, LO[j % 4], 0:T], ACT.Relu).then_inc(hid_relu, 1)
                        if more or j + AHEAD < PROD_Q:
                            split_hi(l, q, j + AHEAD)
                        if j < KD:
                            act.wait_ge(hid_relu, q * KD + (hid + j + 1 + CREDIT))
                            A(HID_HI[:, j, 0:T], RELU[:, j % 2, 0:T], ACT.Square).then_inc(hid_hi, 1)

                if l < DEPTH2 - 1:
                    with act.Fori(0, QUARTERS) as q:
                        quarter(q, True)
                else:
                    with act.Fori(0, QUARTERS - 1) as q:
                        quarter(q, True)
                    quarter(QUARTERS - 1, False)
            squares2(T1, down_out, DOWN_CREDIT + QUARTERS * KD * DEPTH2 - KD)
            root(nn, T1, RT2, stat_bank(DEPTH2, 0))

        @blk.vector
        def _(dve):
            v = nc.vector
            step = Links(dve, dve_step)

            def take(L, uses, before, events, put, i4=0):
                for e in events:
                    finished(dve, L, uses, before, i4, e // L.per, e % L.per)
                    put(e, bank(L, e)).then_inc(L.read(e), 1)

            def conv3(dst, raw, w0, w2, done):
                n = dst.shape[-1]
                step(v.scalar_tensor_tensor(dst[..., 1:n], raw[..., 0:n - 1], w0, dst[..., 1:n], ALU.mult, ALU.add))
                last = v.scalar_tensor_tensor(dst[..., 0:n - 1], raw[..., 1:n], w2, dst[..., 0:n - 1],
                                              ALU.mult, ALU.add)
                if done is None:
                    step(last)
                else:
                    last.then_inc(done, 1)

            def rms_into_h(n, gain):
                dve.wait_ge(root_ready, n + 1)
                step(v.reciprocal(SCR[:, T1:T2], SCR[:, 0:T1]))
                for k in range(KD):
                    v.scalar_tensor_tensor(H[:, k, 0:T1], X[:, k, 0:T1], col1(gain, k), SCR[:, T1:T2],
                                           ALU.mult, ALU.mult).then_inc(h_ready, 1)

            def add_normed(n, gain, Y):
                dve.wait_ge(root_ready, n + 1)
                step(v.reciprocal(SCR[:, T1:T2], SCR[:, 0:T1]))
                for k in range(KD):
                    last = v.scalar_tensor_tensor(Y[:, k, :], Y[:, k, :], col1(gain, k), SCR[:, T1:T2],
                                                  ALU.mult, ALU.mult)
                step(last)
                v.tensor_tensor(X[:, :, 0:T1], X[:, :, 0:T1], Y, ALU.add).then_inc(x_new, 1)

            def mod_piece(p, c0):
                dve.wait_ge(mod_turned, p + 1)
                v.tensor_tensor(MODS[:, bass.ds(c0, 4), :], v3(PS[:, 3], 4)[:, :, 0:2],
                                PR2[:, bass.ds(c0 + ROW2["mod_b_2"], 4)]
                                .rearrange("p (k o) -> p k o", o=1).to_broadcast([P, 4, 2]), ALU.add).then_inc(mod_out, 1)

            dve.wait_ge(tab_full, 1)
            v.tensor_copy(PR1[:, :], PS[:, 0])
            v.tensor_copy(PR2[:, 0:512], PS[:, 1])
            v.tensor_copy(PR2[:, 512:640], PS[:, 2, 0:P]).then_inc(tab_out, 1)
            dve.wait_ge(tab_out, 1)
            dve.wait_ge(s_x, 16)
            dve.wait_ge(s_con, 16)
            v.memset(GM[:, :, :], 0.0).then_inc(x_new, 1)
            with dve.Fori(0, DEPTH1) as lay:
                before = lay * PER1
                step.base, step.n = lay * DVE_LINKS, 0
                v.tensor_copy(PRC[:, :], PR1[:, bass.ds(lay * (NT1 * P), NT1 * P)]).then_inc(prm_ready, 1)
                dve.wait_ge(prm_ready, lay + 1)
                for j, (b, f) in enumerate((("hy_filt_b1", "hy_filt_freq1"), ("hy_filt_b2", "hy_filt_freq2"))):
                    dve.wait_ge(filt_full, lay * 6 + j + 1)
                    step(v.tensor_scalar(FARG, PS[0:ORDER, j, 0:SEQ], col1(b)[0:ORDER], col1(f)[0:ORDER], ALU.add, ALU.mult))
                    step(v.tensor_scalar(FK, FARG, 1.0 / (2.0 * np.pi), MAGIC, ALU.mult, ALU.add))
                    step(v.tensor_scalar(FK, FK, -MAGIC, None, ALU.add))
                    for part in (TWO_PI_HI, TWO_PI_MID, TWO_PI_LO):
                        step(v.scalar_tensor_tensor(FARG, FK, -part, FARG, ALU.mult, ALU.add))
                    v.tensor_scalar(FARG, FARG, 3.1415925, -3.1415925, ALU.min, ALU.max).then_inc(sin_arg, 1)
                dve.wait_ge(filt_full, lay * 6 + 6)
                dve.wait_ge(s_con2, 16)
                for tt in range(2):
                    v.tensor_tensor(HF[:, tt, :], PS[:, tt], DECAY[:, tt, :], ALU.mult)
                    last = v.tensor_tensor(HB[:, tt, :], PS[:, 2 + tt], DECAY[:, tt, :], ALU.mult)
                step(last)
                step(v.memset(HB[0:1, 0, :], 0.0))
                v.tensor_tensor(FA, HF, HB, ALU.add)
                v.tensor_tensor(FB, HF, HB, ALU.subtract).then_inc(filt_out, 1)

                mod1 = lambda *js: [mod_piece(lay * MODP + j, lay * 48 + 4 * j) for j in js]
                mod1(0, 1)
                rms_into_h(lay * 4, "norm_mix_pre")
                for e in range(12):
                    dve.wait_ge(L1["u"].out, lay * 12 + CREDIT + e + 1)
                    conv3(U[:, e, :], RAW[:, e % 4, :], col1("hy_conv_w", e), col1("hy_conv_w", 24 + e), conv_u)
                dve.wait_ge(conv_u, lay * 12 + CREDIT + 12)
                v.tensor_tensor(ZV, U[:, 4:8, :], U[:, 8:12, :], ALU.mult).then_inc(zv_ready, 1)
                take(L1["v"], lay, before, range(2), lambda e, ps: v.tensor_copy(V[:, e, :], ps))
                take(L1["pool"], lay, before, range(2), lambda e, ps: v.tensor_copy(UP[:, e, :], ps))
                for g in range(4):
                    dve.wait_ge(pw_full, lay * 4 + g + 1)
                    v.tensor_scalar(YP[:, g, :], PS[:, 4 + g, 0:T1], col1("pool_scale", g), None,
                                    ALU.mult).then_inc(pw_out, 1)
                for ss in range(2):
                    dve.wait_ge(zt_full, lay * 2 + ss + 1)
                    v.tensor_copy(ZT[:, ss, :], PS[:, ss]).then_inc(zt_out, 1)
                dve.wait_ge(kern_out, lay * 4 + 4)
                dve.wait_ge(zf_out, lay * 4 + 4)
                v.tensor_tensor(PP, ZC, KA, ALU.mult)
                step(v.tensor_tensor(TMP, ZS, KB, ALU.mult))
                v.tensor_tensor(RR, ZC, KB, ALU.mult)
                step(v.tensor_tensor(PP, PP, TMP, ALU.subtract))
                step(v.tensor_tensor(TMP, ZS, KA, ALU.mult))
                v.tensor_tensor(RR, RR, TMP, ALU.add).then_inc(prod_ready, 1)
                dve.wait_ge(prod_ready, lay + 1)
                for j in range(4):
                    dve.wait_ge(hy_full, lay * 4 + j + 1)
                    step(v.scalar_tensor_tensor(TMP[:, j, :], ZV[:, j, :], col1("hy_bias", j), PS[:, j, 0:T1],
                                                ALU.mult, ALU.add))
                    v.tensor_tensor(U[:, j, :], U[:, j, :], TMP[:, j, :], ALU.mult).then_inc(hy_out, 1)
                for z in range(2):
                    zz = lay * 2 + z
                    for j in range(4):
                        if j % 2 == 0:
                            dve.wait_ge(gk_full, zz * 2 + j // 2 + 1)
                        o = T1 * (j % 2)
                        last = v.tensor_scalar(X1[:, T1 * j:T1 * j + T1], PS[:, 4 + j // 2, o:o + T1],
                                               col1("gla_gate_b", 4 * z + j), None, ALU.add)
                    last.then_inc(gk_out, 1)
                    dve.wait_ge(ls_ready, zz + 1)
                    step(v.scalar_tensor_tensor(X1, X1, 0.0, B1, ALU.min, ALU.subtract))
                    step(v.tensor_scalar(X1, X1, 1.0 / 16.0, -1.0, ALU.mult, ALU.max))
                    for j in range(4):
                        la, cum = X1[:, T1 * j:T1 * j + T1], B1[:, T1 * j:T1 * j + T1]
                        if z == 0:
                            last = v.tensor_tensor_scan(out=cum, data0=c("scan_f"), data1=la, initial=0.0,
                                                        op0=ALU.mult, op1=ALU.add)
                        else:
                            last = v.tensor_tensor_scan(out=cum[:, ::-1], data0=c("scan_b")[:, ::-1], data1=la[:, ::-1],
                                                        initial=0.0, op0=ALU.mult, op1=ALU.add)
                    last.then_inc(cum_ready, 1)
                    mod1(2 if z == 0 else 5)
                    dve.wait_ge(exp_ready, zz + 1)
                    v.tensor_tensor(QE, BIG[:, 3072:4096], E1, ALU.mult)
                    step(v.tensor_tensor(KE, BIG[:, 4096:5120], KE, ALU.mult))
                    edge = GLA_C - 1 if z == 0 else 0
                    chunks = lambda ap: ap.rearrange("p (n t) -> p n t", t=GLA_C)
                    v.tensor_tensor(chunks(X1), chunks(KE), chunks(E1)[:, :, edge:edge + 1].to_broadcast([P, 16, GLA_C]),
                                    ALU.mult).then_inc(qk_ready, 1)
                    mod1(3 if z == 0 else 6)
                    mask = c("mask_f" if z == 0 else "mask_b").rearrange("p (o t) -> p o t", o=1)
                    for b in range(2):
                        dve.wait_ge(sco_full, zz * 2 + b + 1)
                        v.tensor_tensor(v3(SCO[:, 512 * b:512 * b + 512], 4), v3(PS[:, 4 + b], 4),
                                        mask.to_broadcast([P, 4, P]), ALU.mult).then_inc(sco_out, 1)
                    if z == 0:
                        mod1(4)
                    for i in range(3):
                        dve.wait_ge(st_full, zz * 3 + i + 1)
                        if i == 0:
                            step(v.tensor_copy(ST[0], PS[:, 0]))
                            continue
                        n = i if z == 0 else 3 - i
                        for h in range(HEADS1):
                            hs = slice(P * h, P * h + P)
                            o = T1 * h + GLA_C * n + edge
                            last = v.scalar_tensor_tensor(ST[i][:, hs], ST[i - 1][:, hs], E1[:, o:o + 1],
                                                          PS[:, i, hs], ALU.mult, ALU.add)
                        if i == 1:
                            step(last)
                        else:
                            last.then_inc(st_out, 1)
                    for b in range(2):
                        dve.wait_ge(og_full, zz * 2 + b + 1)
                        og = OG[:, 512 * b:512 * b + 512]
                        if z == 0:
                            v.tensor_copy(og, PS[:, 6 + b]).then_inc(og_out, 1)
                        else:
                            v.tensor_tensor(og, og, PS[:, 6 + b], ALU.add).then_inc(og_out, 1)
                mod1(7)
                dve.wait_ge(groot, lay * 2 + 2)
                step(v.reciprocal(B1, B1))
                yg = BIG[:, 3072:4096]
                step(v.scalar_tensor_tensor(yg, OG, col1("gla_norm"), B1, ALU.mult, ALU.mult))
                v.tensor_tensor(yg, yg, BIG[:, 5120:6144], ALU.mult).then_inc(gla_done, 1)

                L1["gates"].wait_all_out(dve, lay)

                def merge(e, ps):
                    if e < 8:
                        return v.tensor_tensor(MG[:, e, :], GT[:, e, :], ps[:, 0:T1], ALU.mult)
                    step(v.tensor_tensor(GT[:, e, :], GT[:, e, :], ps[:, 0:T1], ALU.mult))
                    return v.tensor_tensor(MG[:, e % 8, :], MG[:, e % 8, :], GT[:, e, :], ALU.add)

                take(L1["branch"], lay, before, range(24), merge)
                mod1(8)
                add_normed(lay * 4 + 1, "norm_mix_post", Y1)
                mod1(9)
                dve.wait_ge(x_new, lay * 2 + 2)
                rms_into_h(lay * 4 + 2, "norm_ffn_pre")
                for m in range(NFF):
                    dve.wait_ge(L1["up"].out, lay * NFF + CREDIT + m + 1)
                    conv3(FT[:, m, :], FRAW[:, m % 4, :], col1("ffn_conv_w", m), col1("ffn_conv_w", 2 * NFF + m), conv_f)

                def times_gelu(e, ps):
                    dve.wait_ge(gelu_out, lay * NFF + e - NFF + 1)
                    return v.tensor_tensor(FT[:, e - NFF, :], FT[:, e - NFF, :], ps[:, 0:T1], ALU.mult)

                take(L1["up"], lay, before, range(NFF, 2 * NFF), times_gelu)
                mod1(10)
                add_normed(lay * 4 + 3, "norm_ffn_post", Y2)
                mod1(11)
                dve.wait_ge(x_new, lay * 2 + 3)
                assert step.n == DVE_LINKS, step.n
            step.base, step.n = 0, DVE_LINKS * DEPTH1

            nn = 4 * DEPTH1

            def gain_rstd(n, l, gain, j, T):
                grow = PR2[:, ROW2[gain] + KD * l:ROW2[gain] + KD * l + KD].rearrange("p (k o) -> p k o", o=1)
                step(v.scalar_tensor_tensor(GM[:, :, :], MODS[:, 48 * l + KD * (j + 1):48 * l + KD * (j + 2), :], 1.0,
                                            grow.to_broadcast([P, KD, 2]), ALU.add, ALU.mult))
                dve.wait_ge(root_ready, n + 1)
                step(v.reciprocal(RS2[:, 0:T], RT2[:, 0:T]))

            def split_lo(l, q, j):
                r = j // 2
                dve.wait_ge(w_hi, q * PROD_Q + (N_MLP[l] + j + 1))
                v.tensor_tensor(WL[:, j % 4], WRAW[:, r % 4, :, P * (j % 2):P * (j % 2) + P],
                                WH[:, j % 4].bitcast(F32), ALU.subtract).then_inc(w_lo, 1)

            def split_lo_of(*products):
                for n in products:
                    dve.wait_ge(w_hi, n + 1)
                    v.tensor_tensor(WL[:, n % 4], WRAW[:, n // 2 % 4, :, P * (n % 2):P * (n % 2) + P],
                                    WH[:, n % 4].bitcast(F32), ALU.subtract).then_inc(w_lo, 1)

            def take_split(L, uses, n, events, put):
                for e in events:
                    split_lo_of(n + e + AHEAD)
                    dve.wait_ge(w_used, n + e + 1 + CREDIT)
                    put(e, bank(L, e)).then_inc(L.read(e), 1)

            def scaled_and_lo(n, l, gain, j, T):
                gain_rstd(n, l, gain, j, T)
                for k in range(KD):
                    for s in range(T // T1):
                        ts = slice(T1 * s, T1 * s + T1)
                        last = v.scalar_tensor_tensor(HNORM[:, k, ts], X[:, k, ts], GM[:, k, s:s + 1], RS2[:, ts],
                                                      ALU.mult, ALU.mult)
                    last.then_inc(h_ready, 1)
                for k in range(KD):
                    dve.wait_ge(h_shift, (2 * l + j // 3) * KD + k + 1)
                    for s in range(T // T1):
                        ts = slice(T1 * s, T1 * s + T1)
                        last = v.scalar_tensor_tensor(H_LO[:, k, ts], HNORM[:, k, ts],
                                                      MODS[:, 48 * l + KD * j + k, s:s + 1],
                                                      H_HI[:, k, ts].bitcast(F32), ALU.add, ALU.subtract)
                    last.then_inc(h_lo, 1)

            def add_gated(j, k, T, src):
                for s in range(T // T1):
                    ts = slice(T1 * s, T1 * s + T1)
                    last = v.scalar_tensor_tensor(X[:, k, ts], src[:, ts], MODS[:, 48 * l + KD * j + k, s:s + 1], X[:, k, ts],
                                                  ALU.mult, ALU.add)
                return last

            for l in range(DEPTH2):
                n0 = N_MIX[l]
                T = T2 if l < DEPTH2 - 1 else T1
                if l == 0:
                    dve.wait_ge(slab_done, BEFORE2 + 4)
                    split_lo_of(*range(AHEAD))
                dve.wait_ge(mod_out, MODP * (l + 1 if l < 2 else 4) + 1)
                if l == 0:
                    dve.wait_ge(s_ctx, 16)
                scaled_and_lo(nn, l, "norm1_g_2", 0, T2)
                nn += 1
                if l % 3 == 0:
                    a = l // 3
                    split_lo_of(*range(n0 + AHEAD, n0 + 16 + AHEAD))
                    for e in range(16, 24):
                        split_lo_of(n0 + e + AHEAD)
                        dve.wait_ge(w_used, n0 + (e // 2 * 2 + 2) + CREDIT)
                        t0, c0 = 2 * (e % 2), SEQ * ((e - 16) // 2)
                        v.tensor_copy(VT[:, t0:t0 + 2, c0:c0 + SEQ], v3(bank(L2["qkv"], e), 2)).then_inc(L2["qkv"].out2, 1)
                    units = [(h, t) for h in range(HEADS2) for t in tiles(a)]
                    N = len(units)
                    per_pair = 2 * len(tiles(a))
                    for n in range(N + 4):
                        if n < N:
                            g = unit0(a) + n
                            lo = 0 if units[n][1] < 2 else SEQ
                            dve.wait_ge(sc_full, g + 1)
                            v.tensor_reduce(MX[:, n, 0:1], PS[:, n % 3, lo:T2], AX.X, ALU.max,
                                            negate=True).then_inc(max_ready, 1)
                        if 1 <= n <= N:
                            g = unit0(a) + n - 1
                            lo = 0 if units[n - 1][1] < 2 else SEQ
                            pb = PB[(n - 1) % 3][:, lo:T2]
                            dve.wait_ge(p_exp, g + 1)
                            step(v.reciprocal(MX[:, n - 1, 1:2], MX[:, n - 1, 1:2]))
                            v.tensor_scalar(pb, pb, MX[:, n - 1, 1:2], None, ALU.mult).then_inc(p_norm, 1)
                        if n >= 4 and (n - 3) % per_pair == 0:
                            k = (n - 3) // per_pair - 1
                            dve.wait_ge(o_full, a * 8 + k + 1)
                            dve.wait_ge(o_hi, a * 8 + k + 1)
                            v.tensor_tensor(H_LO[:, k, 0:T], PS[:, 5 + k % 2, 0:T], H_HI[:, k, 0:T].bitcast(F32),
                                            ALU.subtract).then_inc(o_out, 1)
                    take_split(L2["wo"], a, n0 + 24, range(8), lambda e, ps: add_gated(2, e, T, ps))
                elif l % 3 == 1:
                    before = BEFORE2
                    dve.wait_ge(h_lo, KD * (2 * l + 1))
                    v.memset(UPAD[:, :, :, 0:15], 0.0)
                    v.memset(UPAD[:, :, :, 15 + SEQ:286], 0.0)
                    split_lo_of(*range(n0 + AHEAD, n0 + 8 + AHEAD))
                    for k in range(KD):
                        if 8 + k + AHEAD < 16:
                            split_lo_of(n0 + 8 + k + AHEAD)
                        dve.wait_ge(L2["cv1"].out, CREDIT + 8 + k + 1)
                        last = v.tensor_tensor(UPAD[:, k, :, 15:15 + SEQ], v3(UA[:, k, :], 2), v3(CV[:, k, :], 2), ALU.mult)
                    step(last)
                    for k in range(KD):
                        cvk = v3(CV[:, k, :], 2)
                        for tap in range(TAPS):
                            win = UPAD[:, k, :, tap:tap + SEQ]
                            wcol = col2("cv_dw_2", KD * tap + k)
                            if tap == 0:
                                step(v.tensor_scalar(cvk, win, wcol, col2("cv_dwb_2", k), ALU.mult, ALU.add))
                            elif tap < TAPS - 1 or k < KD - 1:
                                step(v.scalar_tensor_tensor(cvk, win, wcol, cvk, ALU.mult, ALU.add))
                            else:
                                v.scalar_tensor_tensor(cvk, win, wcol, cvk, ALU.mult, ALU.add).then_inc(cv_dw, 1)
                            if tap % 10 == 5:
                                m = 3 * k + tap // 10
                                mod_piece(2 * MODP + m, 96 + 4 * m)
                    dve.wait_ge(slab_done, before + MOD2 + 4)
                    split_lo_of(*range(n0 + 16, n0 + 16 + AHEAD))
                    dve.wait_ge(mu_out, 1)
                    v.tensor_tensor(XC, CV, MU.rearrange("p (o t) -> p o t", o=1).to_broadcast([P, KD, T2]),
                                    ALU.subtract).then_inc(xc_ready, 1)
                    dve.wait_ge(cv_root, 1)
                    step(v.reciprocal(RS2, RT2))
                    for k in range(KD):
                        v.scalar_tensor_tensor(XC[:, k, :], XC[:, k, :], col2("cv_ln_g_2", k), RS2, ALU.mult,
                                               ALU.mult).then_inc(cv_norm, 1)

                    for k in range(KD):
                        dve.wait_ge(mix_hi, k + 1)
                        v.tensor_tensor(H_LO[:, k, :], UA[:, k, :], H_HI[:, k, :].bitcast(F32),
                                        ALU.subtract).then_inc(mix_lo, 1)

                    def add_conf(e, ps):
                        t = SM[:, 512 * (e % 4):512 * (e % 4) + 512]
                        step(v.tensor_scalar(t, ps, col2("cv_b2_2", e), None, ALU.add))
                        return add_gated(2, e, T2, t)

                    take_split(L2["cv2"], 0, n0 + 16, range(8), add_conf)
                else:
                    def mixed_lo(m):
                        dve.wait_ge(mix_hi, KD + m + 1)
                        v.tensor_tensor(HID_LO[:, m, :], SY[:, m, :], HID_HI[:, m, :].bitcast(F32),
                                        ALU.subtract).then_inc(mix_lo, 1)

                    split_lo_of(*range(n0 + AHEAD, n0 + 16 + AHEAD))
                    dve.wait_ge(L2["sc1"].out, CREDIT + 16)
                    for m in range(KD):
                        take_split(L2["sc1"], 0, n0, (16 + m,),
                                   lambda e, ps: v.tensor_tensor(CG[:, m, :], CG[:, m, :], ps, ALU.mult))
                        dve.wait_ge(L2["sc1"].out2, m + 1)
                        s, y = v3(CG[:, m, :], 2), v3(SY[:, m, :], 2)
                        step(v.tensor_scalar(y, s, col2("sc_conv_2", KD + m), None, ALU.mult))
                        conv3(y, s, col2("sc_conv_2", m), col2("sc_conv_2", 2 * KD + m), None)
                        v.tensor_tensor(SY[:, m, :], BG[:, m, :], SY[:, m, :], ALU.mult).then_inc(sc_bg, 1)
                        if m:
                            mixed_lo(m - 1)
                    mixed_lo(KD - 1)
                    take_split(L2["sc2"], 0, n0 + 24, range(8), lambda e, ps: add_gated(2, e, T2, ps))
                v.memset(GM[:, :, :], 0.0).then_inc(x_new, 1)
                dve.wait_ge(x_new, 2 + 2 * DEPTH1 + 2 * l)
                scaled_and_lo(nn, l, "norm2_g_2", 3, T)
                nn += 1

                def quarter(q, more):
                    hid = l * QUARTERS * KD
                    for j in range(PROD_Q):
                        if j < KD:
                            r1, r2 = RELU[:, j % 2, 0:T], RELU2[:, j % 2, 0:T]
                            dve.wait_ge(hid_relu, q * KD + (hid + j + 1 + CREDIT))
                            dve.wait_ge(hid_lo, q * KD + (hid + j + 1))
                            v.tensor_tensor(r2, r1, r1, ALU.mult).then_inc(hid_sq, 1)
                        else:
                            dve.wait_ge(w_used, q * PROD_Q + (N_MLP[l] + j + 1 + CREDIT))
                            dve.wait_ge(down_out, q * KD + (hid + j - KD + 1))
                            add_gated(5, j - KD, T, PS[:, HI[j % 4]]).then_inc(down_out, 1)
                        if more or j + AHEAD < PROD_Q:
                            split_lo(l, q, j + AHEAD)
                        if j < KD:
                            dve.wait_ge(hid_sq, q * KD + (hid + j + 1))
                            dve.wait_ge(hid_hi, q * KD + (hid + j + 1))
                            v.tensor_tensor(HID_LO[:, j, 0:T], r2, HID_HI[:, j, 0:T].bitcast(F32),
                                            ALU.subtract).then_inc(hid_lo, 1)

                if l < DEPTH2 - 1:
                    with dve.Fori(0, QUARTERS) as q:
                        quarter(q, True)
                else:
                    with dve.Fori(0, QUARTERS - 1) as q:
                        quarter(q, True)
                    quarter(QUARTERS - 1, False)
                dve.wait_ge(down_out, DOWN_CREDIT + QUARTERS * KD * (l + 1))
                v.memset(GM[:, :, :], 0.0).then_inc(x_new, 1)
                dve.wait_ge(x_new, 3 + 2 * DEPTH1 + 2 * l)
            dve.wait_ge(root_ready, nn + 1)
            step(v.reciprocal(RS2[:, 0:T1], RT2[:, 0:T1]))
            for k in range(KD):
                v.scalar_tensor_tensor(H[:, k, 0:T1], X[:, k, 0:T1], col2("final_g_2", k), RS2[:, 0:T1],
                                       ALU.mult, ALU.mult).then_inc(h_ready, 1)


def constants():
    C = np.zeros((P, NCON), np.float32)

    def put(name, a):
        lo, hi = CON[name]
        C[:a.shape[0], lo:hi] = a.reshape(a.shape[0], -1)

    i = np.arange(P)
    put("ident", np.eye(P))
    put("flip", np.eye(P)[::-1])
    q = GRID - 1 - i % GRID
    start = np.clip(q - WCOLS // 2, 0, GRID - WCOLS)[:, None]
    k = np.arange(GRID)[None]
    put("window", np.where((k >= start) & (k < start + WCOLS), 0.0, -1e30))
    same = i[:, None] // GLA_C == i[None] // GLA_C
    put("mask_f", (same & (i[:, None] <= i[None])).astype(float))
    put("mask_b", (same & (i[:, None] > i[None])).astype(float))
    t = np.arange(SEQ)
    put("scan_f", np.tile((t % GLA_C != 0).astype(float), (P, 1)))
    put("scan_b", np.tile((t % GLA_C != GLA_C - 1).astype(float), (P, 1)))
    bands = (EMB - 1) // 2
    tl = np.linspace(0.0, 1.0, SEQ, dtype=np.float32)[:, None]
    ang = (np.linspace(1e-4, bands - 1, bands, dtype=np.float32)[None]
           * (2.0 * np.pi * np.arange(SEQ, dtype=np.float32)[:, None] / SEQ).astype(np.float32))
    put("zT", np.concatenate([tl, np.cos(ang), -np.sin(ang)], axis=1).T)
    th = (2 * t[None] + 1) * t[:, None] * np.pi / (2 * SEQ)

    def tiled(m):
        return m.reshape(2, P, -1).transpose(1, 0, 2)

    put("cos", tiled(np.cos(th)))
    put("sin", tiled(np.sin(th)))
    put("icos", tiled(np.cos(th).T / SEQ))
    put("isin", tiled(np.sin(th).T / SEQ))
    lo, hi = np.log(1e-2) / 1.5, np.log(1e-2) / 0.3
    deltas = np.linspace(lo, hi, HY, dtype=np.float32)
    put("decay", tiled(np.exp(-tl * np.abs(deltas)[None])))
    band = np.zeros((SEQ, 4, SEQ))
    for g, wn in enumerate(WINDOWS):
        half = wn // 2
        for tt in range(SEQ):
            a, b = max(tt - half, 0), min(tt + half, SEQ)
            band[a:b, g, tt] = 1.0 / (b - a)
            band[tt, g, tt] -= 1.0
    put("band", band.reshape(2, P, 4, SEQ).transpose(1, 0, 2, 3))
    return C


def kernel(**inputs):
    import concourse.bacc as bacc
    from concourse.bass_utils import run_bass_kernel_spmd as run

    def table(names, rows_of, tables, layer=None):
        out = np.zeros((tables, P, P), np.float32)
        flat = out.reshape(tables * P, P)
        for name in names:
            a = np.asarray(inputs[name])
            a = a[layer] if layer is not None else a
            if a.shape[-1] < P:
                flat[rows_of[name], :a.shape[-1]] = a
            else:
                a = a.reshape(-1, P)
                flat[rows_of[name]:rows_of[name] + len(a)] = a
        return out

    arrays = {
        "xT": np.ascontiguousarray(np.asarray(inputs["x"])[0].T),
        "ctxT": np.ascontiguousarray(np.asarray(inputs["ctx_2"])[0].T),
        "consts": constants(),
        "params1": np.concatenate([table(ROW1, ROW1, NT1, l) for l in range(DEPTH1)]),
        "params2": table(ROW2, ROW2, NT2),
    }
    nc = bacc.Bacc("TRN2", target_bir_lowering=False, num_devices=1)
    big = ("w_in", "w_br_hyena", "w_br_gla", "w_br_pool", "w_out", "ffn_w_up", "ffn_w_down", "hy_filt_w1",
           "hy_filt_w2", "hy_filt_w3", "gla_gate_w2", "pool_w", "mod_w_2", "mlp_w1_2", "mlp_w2_2", "na_wqkv_2",
           "na_wo_2", "na_rpb_2", "cv_w1_2", "cv_w2_2", "sc_win_2", "sc_wout_2")
    for name in big:
        arrays[name] = np.ascontiguousarray(inputs[name])
    aps = {n: nc.dram_tensor(n, a.shape, mybir.dt.from_np(a.dtype), kind="ExternalInput").ap()
           for n, a in arrays.items()}
    out = nc.dram_tensor("out_0", (D, SEQ), F32, kind="ExternalOutput").ap()
    build(nc, aps["xT"], aps["ctxT"], aps["consts"], aps["params1"], aps["params2"], aps, out)
    r = run(nc, [arrays], core_ids=[0])
    return np.ascontiguousarray(r.results[0]["out_0"].T)[None]
```
